# Optimizing a Trainium2 kernel written in Bass

```python
import jax, jax.numpy as jnp
from jax import lax
import numpy as np

D_MODEL = 1024
BATCH = 1
SEQ = 512
DEPTH = 1
DEC_BATCH = 1
DEC_SEQ = 64
PAST_LEN = 1024

CHUNK = 64
N_META = 16
POOL_W = D_MODEL // 2
POOL_WINDOWS = (2, 4, 8, 16)
N_POOL_GROUPS = len(POOL_WINDOWS)
POOL_GC = POOL_W // N_POOL_GROUPS
POOL_STATE = max(POOL_WINDOWS) - 1
SB_HEADS = 8
SB_HEAD_DIM = 64
ATTN_W = SB_HEADS * SB_HEAD_DIM
QBLOCK = 128
D_FF = 4 * D_MODEL
IN_W = POOL_W + 3 * ATTN_W + 2 * D_MODEL
LN_EPS = 1e-5
ALPHA = (2.0 * DEPTH) ** 0.25
BETA_INIT = (8.0 * DEPTH) ** -0.25
SB_SCALE = SB_HEAD_DIM ** -0.5

kernel_name = "hybrid_pool_stickbreak_streaming_step"

def _layer_norm(x, g, b):
    xf = x.astype(jnp.float32)
    mu = jnp.mean(xf, axis=-1, keepdims=True)
    var = jnp.mean(jnp.square(xf - mu), axis=-1, keepdims=True)
    return ((xf - mu) * lax.rsqrt(var + LN_EPS) * g + b).astype(x.dtype)

def _multiscale_pool(u, u_past, n_past):
    B, T, C = u.shape
    full = jnp.concatenate([u_past, u], axis=1)
    csum = jnp.concatenate([jnp.zeros((B, 1, C), jnp.float32),
                            jnp.cumsum(full.astype(jnp.float32), axis=1)], axis=1)
    hi = csum[:, POOL_STATE + 1:]
    pos = jnp.arange(T)
    outs = []
    for g, w in enumerate(POOL_WINDOWS):
        sl = slice(g * POOL_GC, (g + 1) * POOL_GC)
        lo = csum[:, POOL_STATE + 1 - w: POOL_STATE + 1 - w + T, sl]
        cnt = jnp.minimum(w, n_past + pos + 1).astype(jnp.float32)[None, :, None]
        outs.append((hi[..., sl] - lo) / cnt)
    mean = jnp.concatenate(outs, axis=-1)
    pooled = (mean - u.astype(jnp.float32)).astype(u.dtype)
    return pooled, full[:, -POOL_STATE:]

def _sb_block(q_blk, q_idx, keys, vals):
    z = jnp.einsum('bqhd,bkhd->bhqk', q_blk, keys).astype(jnp.float32) * SB_SCALE
    visible = jnp.arange(keys.shape[1])[None, :] < q_idx[:, None]
    log_keep = jnp.where(visible, jax.nn.log_sigmoid(-z), 0.0)
    tail = lax.cumsum(log_keep, axis=3, reverse=True) - log_keep
    weight = jnp.where(visible, jnp.exp(jax.nn.log_sigmoid(z) + tail), 0.0)
    return jnp.einsum('bhqk,bkhd->bqhd', weight.astype(vals.dtype), vals)

def _stick_breaking_attention(q, keys, vals, n_hist):
    B, T, H, Dh = q.shape
    nblk = -(-T // QBLOCK)
    t_pad = nblk * QBLOCK
    q_pad = jnp.pad(q, ((0, 0), (0, t_pad - T), (0, 0), (0, 0)))
    q_blocks = q_pad.reshape(B, nblk, QBLOCK, H, Dh).transpose(1, 0, 2, 3, 4)
    idx_blocks = (n_hist + jnp.arange(t_pad)).reshape(nblk, QBLOCK)
    out = lax.map(lambda a: _sb_block(a[0], a[1], keys, vals), (q_blocks, idx_blocks))
    return out.transpose(1, 0, 2, 3, 4).reshape(B, t_pad, H, Dh)[:, :T]

def _layer(h, k_hist, v_hist, u_past, n_past, w_in, b_in, w_pool_grp, pool_scale, w_br_pool, w_br_attn,
           w_out, b_out, ln1_g, ln1_b, w_mlp1, b_mlp1, w_mlp2, b_mlp2, ln2_g, ln2_b):
    B, T, _ = h.shape
    z = h @ w_in + b_in
    u, q, k, v, ga, gb = jnp.split(
        z, [POOL_W, POOL_W + ATTN_W, POOL_W + 2 * ATTN_W, POOL_W + 3 * ATTN_W,
            POOL_W + 3 * ATTN_W + D_MODEL], axis=-1)
    pooled, u_state = _multiscale_pool(u, u_past, n_past)
    pooled = pooled.reshape(B, T, N_POOL_GROUPS, POOL_GC)
    pool_out = jnp.einsum('btgc,gcd->btgd', pooled, w_pool_grp).reshape(B, T, POOL_W) * pool_scale
    q = q.reshape(B, T, SB_HEADS, SB_HEAD_DIM)
    k = k.reshape(B, T, SB_HEADS, SB_HEAD_DIM)
    v = v.reshape(B, T, SB_HEADS, SB_HEAD_DIM)
    keys = jnp.concatenate([k_hist, k], axis=1)
    vals = jnp.concatenate([v_hist, v], axis=1)
    attn = _stick_breaking_attention(q, keys, vals, k_hist.shape[1]).reshape(B, T, ATTN_W)
    mix = jax.nn.sigmoid(ga) * (pool_out @ w_br_pool) + jax.nn.sigmoid(gb) * (attn @ w_br_attn)
    h = _layer_norm(ALPHA * h + (mix @ w_out + b_out), ln1_g, ln1_b)
    f = jnp.square(jax.nn.relu(h @ w_mlp1 + b_mlp1)) @ w_mlp2 + b_mlp2
    h = _layer_norm(ALPHA * h + f, ln2_g, ln2_b)
    return h, k, v, u_state

def setup_inputs(seed: int = 0) -> dict:
    key = jax.random.key(seed)
    ks = jax.random.split(key, 24)

    def nrm(k, shape, scale):
        return jax.random.normal(k, shape, jnp.float32) * scale

    return {
        "x_prompt": nrm(ks[0], (BATCH, SEQ, D_MODEL), 1.0),
        "x_sample": nrm(ks[1], (DEC_BATCH, DEC_SEQ, D_MODEL), 1.0),
        "cache_k": nrm(ks[2], (DEPTH, DEC_BATCH, PAST_LEN, SB_HEADS, SB_HEAD_DIM), 1.0),
        "cache_v": nrm(ks[3], (DEPTH, DEC_BATCH, PAST_LEN, SB_HEADS, SB_HEAD_DIM), 1.0),
        "state_pool": nrm(ks[4], (DEPTH, DEC_BATCH, POOL_STATE, POOL_W), 1.0),
        "meta": nrm(ks[5], (N_META, D_MODEL), 1.0),
        "ln_in_g": 1.0 + nrm(ks[6], (D_MODEL,), 0.05),
        "ln_in_b": nrm(ks[7], (D_MODEL,), 0.02),
        "w_in": nrm(ks[8], (DEPTH, D_MODEL, IN_W), D_MODEL ** -0.5),
        "b_in": nrm(ks[9], (DEPTH, IN_W), 0.02),
        "w_pool_grp": nrm(ks[10], (DEPTH, N_POOL_GROUPS, POOL_GC, POOL_GC), POOL_GC ** -0.5),
        "pool_scale": 1.0 + nrm(ks[11], (DEPTH, POOL_W), 0.1),
        "w_br_pool": nrm(ks[12], (DEPTH, POOL_W, D_MODEL), POOL_W ** -0.5 * BETA_INIT),
        "w_br_attn": nrm(ks[13], (DEPTH, ATTN_W, D_MODEL), ATTN_W ** -0.5 * BETA_INIT),
        "w_out": nrm(ks[14], (DEPTH, D_MODEL, D_MODEL), D_MODEL ** -0.5 * BETA_INIT),
        "b_out": nrm(ks[15], (DEPTH, D_MODEL), 0.02),
        "ln1_g": 1.0 + nrm(ks[16], (DEPTH, D_MODEL), 0.05),
        "ln1_b": nrm(ks[17], (DEPTH, D_MODEL), 0.02),
        "w_mlp1": nrm(ks[18], (DEPTH, D_MODEL, D_FF), D_MODEL ** -0.5 * BETA_INIT),
        "b_mlp1": nrm(ks[19], (DEPTH, D_FF), 0.02),
        "w_mlp2": nrm(ks[20], (DEPTH, D_FF, D_MODEL), D_FF ** -0.5 * BETA_INIT),
        "b_mlp2": nrm(ks[21], (DEPTH, D_MODEL), 0.02),
        "ln2_g": 1.0 + nrm(ks[22], (DEPTH, D_MODEL), 0.05),
        "ln2_b": nrm(ks[23], (DEPTH, D_MODEL), 0.02),
    }

def reference(x_prompt, x_sample, cache_k, cache_v, state_pool, meta, ln_in_g, ln_in_b, w_in, b_in,
              w_pool_grp, pool_scale, w_br_pool, w_br_attn, w_out, b_out, ln1_g, ln1_b,
              w_mlp1, b_mlp1, w_mlp2, b_mlp2, ln2_g, ln2_b):
    B = x_prompt.shape[0]
    meta_rows = jnp.broadcast_to(meta.astype(x_prompt.dtype)[None], (B, N_META, D_MODEL))
    hp = _layer_norm(jnp.concatenate([meta_rows, x_prompt], axis=1), ln_in_g, ln_in_b)
    hs = _layer_norm(x_sample, ln_in_g, ln_in_b)
    kp_l, vp_l, up_l, ks_l, vs_l, us_l = [], [], [], [], [], []
    for l in range(DEPTH):
        wl = (w_in[l], b_in[l], w_pool_grp[l], pool_scale[l], w_br_pool[l], w_br_attn[l], w_out[l], b_out[l],
              ln1_g[l], ln1_b[l], w_mlp1[l], b_mlp1[l], w_mlp2[l], b_mlp2[l], ln2_g[l], ln2_b[l])
        zero_hist = jnp.zeros((B, 0, SB_HEADS, SB_HEAD_DIM), hp.dtype)
        zero_pool = jnp.zeros((B, POOL_STATE, POOL_W), hp.dtype)
        hp, kp, vp, up = _layer(hp, zero_hist, zero_hist, zero_pool, 0, *wl)
        hs, ks_, vs_, us = _layer(hs, cache_k[l], cache_v[l], state_pool[l], POOL_STATE, *wl)
        kp_l.append(kp); vp_l.append(vp); up_l.append(up)
        ks_l.append(ks_); vs_l.append(vs_); us_l.append(us)
    y_prompt = hp[:, N_META:]
    return (y_prompt, hs, jnp.stack(kp_l), jnp.stack(vp_l), jnp.stack(up_l),
            jnp.stack(ks_l), jnp.stack(vs_l), jnp.stack(us_l))


_drawn_inputs = setup_inputs


def setup_inputs(seed=0):
    import zlib

    import numpy as np

    out = dict(_drawn_inputs(seed))
    spreads = {}
    factors = {'cache_k': 8.0,
     'cache_v': 3.957,
     'state_pool': 4.142,
     'ln_in_b': 2.737,
     'pool_scale': 3.919,
     'b_out': 3.435,
     'ln1_b': 2.84,
     'b_mlp1': 6.828,
     'b_mlp2': 3.356,
     'ln2_b': 2.912}
    for name, (base, spread) in spreads.items():
        noise = np.random.default_rng([zlib.crc32(name.encode()), seed]).standard_normal(out[name].shape)
        drawn = base * np.exp(spread * noise) if base else spread * noise
        out[name] = __import__('jax').numpy.asarray(drawn.astype(out[name].dtype))
    for name, factor in factors.items():
        out[name] = (out[name] * factor).astype(out[name].dtype)
    return out
```

```python
from contextlib import ExitStack

import concourse.bass as bass
from concourse import mybir

F32 = mybir.dt.float32
F32R = mybir.dt.float32r
BF16 = mybir.dt.bfloat16
ALU = mybir.AluOpType
ACT = mybir.ActivationFunctionType

P = 128
D_MODEL, META, SEQ, DEC, PAST = 1024, 16, 512, 64, 1024
HEADS, HD = 8, 64
ATTN_W, POOL_W, D_FF = HEADS * HD, 512, 4096
POOL_WINDOWS = (2, 4, 8, 16)
STATE = max(POOL_WINDOWS) - 1
T = META + SEQ + DEC
TA = SEQ + DEC
HT, HA = T // 2, TA // 2
KC = D_MODEL // P
PAIRS = HEADS // 2
ALPHA = 2.0 ** 0.25
SB_SCALE = HD ** -0.5
LN_EPS = 1e-5
NEG = -1.0e30
BANK = 512

UNIT = KC * P
U_K, U_V, U_Q, U_U, U_GATE, U_BR, U_OUT = 0, 4, 8, 12, 16, 32, 40
U_MLP1, U_MLP2 = (48, 80), (64, 96)
UNITS = 112
RAW, SPLIT = 4, 2
N_K, N_Q, N_U, N_GATE, N_BR, N_OUT = 0, 4, 8, 12, 28, 36
N_MLP1, N_MLP2 = (44, 68), (60, 84)
FH = D_FF // P // 2

V_BIN, V_PSCALE, V_BOUT = 0, 32, 36
V_LNIN_G, V_LNIN_B, V_LN1_G, V_LN1_B, V_LN2_G, V_LN2_B = 44, 52, 60, 68, 76, 84
V_B1, V_B2, V_COUNT = 92, 124, 132
C_U, C_Q, C_K, C_GATE = 0, 4, 8, 16

QS = [max(0, P * b - META) for b in range(5)]
QW = [SEQ - q for q in QS]
OFF = [sum(QW[:b]) for b in range(5)]
ZP = sum(QW)
ZS = 3 * BANK
TAIL = T - P
SAMPLE_BLOCKS = [(8, 7, 6), (5, 4, 3), (2, 1, 0)]
ITEMS = 3 + HEADS
UP = META + SEQ
UT = UP + STATE + DEC


def bank_pieces(dst, n):
    at = 0
    while at < n:
        w = min(n - at, BANK - (dst + at) % BANK)
        yield dst + at, at, w
        at += w


def encoder_step(nc, x, wstream, vecs_d, bv_d, kc_d, vc_d, state_d, wpool_d, y_out, k_out, v_out, s_out):
    with ExitStack() as ctx:
        base = 16512

        def sb(name, shape, dt, at):
            return nc.alloc_sbuf_tensor_at(name, [P] + shape, dt, offset=base + 4 * at)

        def sem(name):
            return ctx.enter_context(nc.semaphore(name))

        raw = sb("raw", [RAW, UNIT], F32, 0)
        whi = sb("whi", [SPLIT, UNIT], F32R, 4096)
        wlo = sb("wlo", [SPLIT, UNIT], F32R, 6144)
        h_hi = sb("h_hi", [KC, T], F32R, 8192)
        h_lo = sb("h_lo", [KC, T], F32R, 12928)
        bv = sb("bv", [ATTN_W], F32, 17664)
        tri = sb("tri", [P], F32, 18176)
        neg1 = sb("neg1", [P], F32, 18304)
        tri_r = sb("tri_r", [P], F32R, 18432)
        neg1_r = sb("neg1_r", [P], F32R, 18560)
        ident = sb("ident", [P], BF16, 18688)
        mask_diag = sb("mask_diag", [P], BF16, 18752)
        mask_tail = sb("mask_tail", [META], BF16, 18816)
        mask_new = sb("mask_new", [HEADS, DEC], BF16, 18824)
        vecs = sb("vecs", [V_COUNT], F32, 19080)
        bq8 = sb("bq8", [4], F32, 19216)
        b1_now = sb("b1_now", [4], F32, 19224)
        wpool = sb("wpool", [4, P], F32, 19232)
        A0 = 19744
        kcache = sb("kcache", [PAIRS, PAST], F32, A0)
        vcache = sb("vcache", [8, ATTN_W], F32, A0 + 4096)
        gates = sb("gates", [2, KC, TA], F32, A0)
        k_t = sb("k_t", [PAIRS, T], F32, A0 + 9216)
        q_t = sb("q_t", [HEADS, TA], F32, A0 + 11584)
        v_t = sb("v_t", [5, ATTN_W], F32, A0 + 16192)
        attn_hi = sb("attn_hi", [PAIRS, TA], F32R, A0 + 18752)
        attn_lo = sb("attn_lo", [PAIRS, TA], F32R, A0 + 21056)
        u_t = sb("u_t", [4, UT], F32, A0 + 23360)
        sa = sb("sa", [ZS], F32, A0 + 25848)
        sp_hi = sb("sp_hi", [ZS], F32R, A0 + 27384)
        sp_lo = sb("sp_lo", [ZS], F32R, A0 + 28920)
        later = sb("later", [2, BANK], F32, A0 + 30456)
        win = sb("win", [2, 608], F32, A0 + 31480)
        ust = sb("ust", [4, 2 * STATE], F32, A0 + 32704)
        pool_hi = sb("pool_hi", [4, TA], F32R, A0 + 9216)
        pool_lo = sb("pool_lo", [4, TA], F32R, A0 + 11520)
        mix_hi = sb("mix_hi", [KC, TA], F32R, A0 + 13824)
        mix_lo = sb("mix_lo", [KC, TA], F32R, A0 + 23360)
        br_a = sb("br_a", [2, HA], F32, A0 + 29000)
        br_b = sb("br_b", [2, HA], F32, A0 + 29576)
        f_hi = sb("f_hi", [FH, TA], F32R, A0 + 4608)
        f_lo = sb("f_lo", [FH, TA], F32R, A0 + 13824)
        relu_t = sb("relu_t", [2, HA], F32, A0 + 29000)
        relu_sq = sb("relu_sq", [2, HA], F32, A0 + 29576)

        z = ctx.enter_context(nc.psum_tensor("z", [P, 3, BANK], F32))
        xo = ctx.enter_context(nc.psum_tensor("xo", [P, 2, BANK], F32))
        lin = ctx.enter_context(nc.psum_tensor("lin", [P, 2, BANK], F32))
        small = ctx.enter_context(nc.psum_tensor("small", [P, BANK], F32))
        zf = z[:, :, :].rearrange("p b n -> p (b n)")

        vecs_in, bv_in, wpool_in = sem("vecs_in"), sem("bv_in"), sem("wpool_in")
        kc_in, vc_in, state_in = sem("kc_in"), sem("vc_in"), sem("state_in")
        x_in = [sem(f"x_in{k}") for k in range(KC)]
        unit_in = [sem(f"unit_in{s}") for s in range(RAW)]
        hi_split, lo_split = sem("hi_split"), sem("lo_split")
        half_done, unit_done = sem("half_done"), sem("unit_done")
        bank_free = [sem("bank_free0"), sem("bank_free1")]
        made, consts = sem("made"), sem("consts")
        q_zero, bq8_done = sem("q_zero"), sem("bq8_done")
        v_ready, k_stored, v_stored, s_stored, y_stored = (
            sem("v_ready"), sem("k_stored"), sem("v_stored"), sem("s_stored"), sem("y_stored"))
        qk_done, abs_done, expn_done, ln_done, sp_done = (
            sem("qk_done"), sem("abs_done"), sem("expn_done"), sem("ln_done"), sem("sp_done"))
        sphi_done, splo_done, later_done, tri_done, w_done, pv_done = (
            sem("sphi_done"), sem("splo_done"), sem("later_done"), sem("tri_done"), sem("w_done"), sem("pv_done"))
        attn_hi_done, attn_lo_done = sem("attn_hi_done"), sem("attn_lo_done")
        win_done, ust_done, pooled = sem("win_done"), sem("ust_done"), sem("pooled")
        pool_mm, pool_scaled, pool_hi_done, pool_lo_done = (
            sem("pool_mm"), sem("pool_scaled"), sem("pool_hi_done"), sem("pool_lo_done"))
        sig_done, br_gated, br_summed, mix_hi_done, mix_lo_done = (
            sem("sig_done"), sem("br_gated"), sem("br_summed"), sem("mix_hi_done"), sem("mix_lo_done"))
        b1_loaded = sem("b1_loaded")
        relu_done, f_hi_done, f_sq_done, f_lo_done = (
            sem("relu_done"), sem("f_hi_done"), sem("f_sq_done"), sem("f_lo_done"))

        class Norm:

            def __init__(self, name, width, r_at, tmp_at, g, b, col):
                self.w, self.hw, self.g, self.b, self.col = width, width // 2, g, b, col
                self.r = sb(name + "_r", [KC, width], F32, A0 + r_at)
                t = [sb(f"{name}_{s}", [n, width], F32, A0 + tmp_at + o * width)
                     for s, n, o in (("shift", 1, 0), ("sum", 1, 1), ("sumsq", 1, 2), ("mean", 1, 3),
                                     ("rstd", 1, 4), ("d", 2, 5), ("sq", 2, 7))]
                self.shift, self.sum, self.sumsq, self.mean, self.rstd, self.d, self.sq = t
                self.s = {s: sem(f"{name}_{s}") for s in (
                    "row", "part", "shift_mm", "shift", "d", "sq", "sum", "sumsq", "sums_mm", "step",
                    "var", "std", "rstd", "centred", "scaled", "hi", "affine", "lo", "mm")}

        ln_in = Norm("ln_in", T, 18752, 23488, V_LNIN_G, V_LNIN_B, 0)
        ln1 = Norm("ln1", TA, 0, 4608, V_LN1_G, V_LN1_B, META)
        ln2 = Norm("ln2", TA, 0, 23040, V_LN2_G, V_LN2_B, META)
        block = ctx.enter_context(nc.Block())

        def vec(col):
            return vecs[:, bass.ds(col, 1)]

        def both(t, w):
            return t.rearrange("p (b n) -> p b n", b=2)

        @block.sync
        def _(sp):
            def load_unit(q4, j, first=False):
                if not first:
                    sp.wait_ge(lo_split, (q4 - 1) * RAW + j + 1)
                sp.dma_start(raw[:, j, :], wstream[q4 * RAW + j]).then_inc(unit_in[j], 16)

            for k in range(KC):
                sp.dma_start(ln_in.r[:, k, :], x[k]).then_inc(x_in[k], 16)
            for j in range(RAW):
                load_unit(0, j, first=True)
            sp.dma_start(bv[:, :], bv_d).then_inc(bv_in, 16)
            sp.dma_start(kcache[:, :, :], kc_d).then_inc(kc_in, 16)
            load_unit(1, 0)
            load_unit(1, 1)
            sp.dma_start(vcache[:, :, :], vc_d).then_inc(vc_in, 16)
            load_unit(1, 2)
            load_unit(1, 3)
            with sp.Fori(2, UNITS // RAW) as q4:
                for j in range(RAW):
                    load_unit(q4, j)
            for k in range(KC):
                sp.wait_ge(ln2.s["hi"], k + 1)
                sp.dma_start(y_out[:, k, :], ln2.r[:, k, :]).then_inc(y_stored, 16)
            sp.wait_ge(y_stored, 16 * KC)
            sp.wait_ge(k_stored, 16)
            sp.wait_ge(v_stored, 32)
            sp.wait_ge(s_stored, 16)

        @block.tensor
        def _(pe):
            def split_ready(q4, j):
                pe.wait_ge(lo_split, 4 * q4 + j + 1)

            def product(out, j, k, hi, lo, first, last):
                w_h, w_l = whi[:, j % SPLIT, bass.ts(k, P)], wlo[:, j % SPLIT, bass.ts(k, P)]
                pe.matmul(out, w_h, hi, start=first, stop=False)
                pe.matmul(out, w_h, lo, start=False, stop=False)
                return pe.matmul(out, w_l, hi, start=False, stop=last)

            def linear(q4, j, n, hi, lo, col, hw, chunk0=0, chunk_ready=None, part=(True, True)):
                split_ready(q4, j)
                opens, closes = part

                def free(h):
                    if opens and not (isinstance(n, int) and n == 0):
                        pe.wait_ge(bank_free[h], n)

                def mm(h, k):
                    c = slice(col + h * hw, col + (h + 1) * hw)
                    return product(lin[:, h, 0:hw], j, k, hi[:, chunk0 + k, c], lo[:, chunk0 + k, c],
                                   opens and k == 0, closes and k == KC - 1)

                if chunk_ready is None:
                    for h in range(2):
                        free(h)
                        for k in range(KC):
                            last = mm(h, k)
                        if h == 0 and closes:
                            last.then_inc(half_done, 1)
                    last.then_inc(unit_done, 1)
                else:
                    free(0)
                    free(1)
                    for k in range(KC):
                        chunk_ready(k)
                        for h in range(2):
                            last = mm(h, k)
                            if h == 0 and k == KC - 1 and closes:
                                last.then_inc(half_done, 1)
                    last.then_inc(unit_done, 1)

            def sum_halves(dst, src, ln):
                for h in range(2):
                    last = pe.matmul(dst[:, h, 0:ln.hw], neg1[:, :], src[:, h * ln.hw:(h + 1) * ln.hw],
                                     start=True, stop=True)
                return last

            def norm_shift(ln):
                sum_halves(z, ln.r[:, 0, :], ln).then_inc(ln.s["shift_mm"], 1)

            def norm_sums(ln):
                pe.wait_ge(ln.s["sum"], KC)
                sum_halves(xo, ln.sum[:, 0, :], ln)
                pe.wait_ge(ln.s["sumsq"], KC)
                pe.wait_ge(ln.s["shift"], 1)
                sum_halves(z, ln.sumsq[:, 0, :], ln).then_inc(ln.s["sums_mm"], 1)

            pe.wait_ge(made, 4)
            pe.wait_ge(x_in[0], 16)
            norm_shift(ln_in)
            for k in range(KC):
                pe.wait_ge(ln_in.s["d"], k + 1)
                for h in range(2):
                    last = pe.matmul(xo[:, h, 0:HT], neg1[:, :], ln_in.d[:, k % 2, h * HT:(h + 1) * HT],
                                     start=(k == 0), stop=(k == KC - 1))
                last.then_inc(ln_in.s["mm"], 1)
            pe.wait_ge(ln_in.s["sumsq"], KC)
            sum_halves(z, ln_in.sumsq[:, 0, :], ln_in).then_inc(ln_in.s["sums_mm"], 1)

            for m in range(4):
                linear(0, m, N_K + m, h_hi, h_lo, 0, HT,
                       chunk_ready=(lambda k: pe.wait_ge(ln_in.s["lo"], k + 1)) if m == 0 else None)

            for j in range(4):
                split_ready(1, j)
                for c in range(2):
                    k = 2 * j + c
                    m_h = whi[:, j % SPLIT, bass.ts(c, ATTN_W)]
                    m_l = wlo[:, j % SPLIT, bass.ts(c, ATTN_W)]
                    for t in range(5):
                        t0 = min(t * P, TAIL)
                        out = z[:, t, :] if t < 3 else xo[:, t - 3, :]
                        hi, lo = h_hi[:, k, t0:t0 + P], h_lo[:, k, t0:t0 + P]
                        pe.matmul(out, hi, m_h, start=(k == 0), stop=False)
                        pe.matmul(out, hi, m_l, start=False, stop=False)
                        last = pe.matmul(out, lo, m_h, start=False, stop=(k == KC - 1))
                last.then_inc(unit_done, 1)

            for m in range(4):
                linear(2, m, N_Q + m, h_hi, h_lo, META, HA)

            def scores(i):
                if i == 0:
                    pe.wait_ge(v_ready, 5)
                    pe.wait_ge(bank_free[0], N_Q + 4)
                    pe.wait_ge(bank_free[1], N_Q + 4)
                    pe.wait_ge(kc_in, 16)
                    pe.wait_ge(made, 8)
                    pe.wait_ge(consts, 1)
                else:
                    pe.wait_ge(w_done, 2 * i)
                if i < 3:
                    for pos, b in enumerate(SAMPLE_BLOCKS[i]):
                        for p in range(PAIRS):
                            keys = k_t[:, p, TAIL:T] if b == 8 else kcache[:, p, bass.ts(b, P)]
                            last = pe.matmul(z[:, pos, bass.ts(p, P)], keys, q_t[:, 2 * p:2 * p + 2, SEQ:TA],
                                             start=(p == 0), stop=(b != 8), skip_group_check=True)
                        if b == 8:
                            last = pe.matmul(z[:, pos, :], ident[:, :],
                                             mask_new[:, :, :].rearrange("p h q -> p (h q)"),
                                             start=False, stop=True, skip_group_check=True)
                    last.then_inc(qk_done, 1)
                    return
                h = i - 3
                for b in range(5):
                    k0 = min(b * P, TAIL)
                    for dst, at, w in bank_pieces(OFF[b], QW[b]):
                        pe.matmul(zf[:, dst:dst + w], k_t[:, h // 2, k0:k0 + P],
                                  q_t[:, h, QS[b] + at:QS[b] + at + w],
                                  start=(dst % BANK == 0), stop=True, skip_group_check=True)
                for b in range(5):
                    mask = mask_diag[:, META:P] if b == 0 else mask_diag[:, :] if b < 4 else mask_tail[:, :]
                    for dst, at, w in bank_pieces(OFF[b], mask.shape[-1]):
                        last = pe.matmul(zf[:, dst:dst + w], ident[:, :], mask[:, at:at + w],
                                         start=False, stop=True, skip_group_check=True)
                last.then_inc(qk_done, 1)

            def subtract(dst, stationary, src, n):
                for d, at, w in bank_pieces(dst, n):
                    for part in (sp_hi, sp_lo):
                        last = pe.matmul(zf[:, d:d + w], stationary[:, :], part[:, src + at:src + at + w],
                                         start=False, stop=True, skip_group_check=True)
                return last

            def suffix_sums(i):
                pe.wait_ge(splo_done, 2 * i + 2)
                if i < 3:
                    if i:
                        pe.wait_ge(later_done, (2, 5)[i - 1])
                    for pos in range(3):
                        last = subtract(pos * BANK, tri_r, pos * BANK, BANK)
                        for before in range(pos):
                            last = subtract(pos * BANK, neg1_r, before * BANK, BANK)
                        if i:
                            last = pe.matmul(z[:, pos, :], neg1[:, :], later[:, i - 1, :],
                                             start=False, stop=True, skip_group_check=True)
                else:
                    for b in range(5):
                        last = subtract(OFF[b], tri_r, OFF[b], QW[b])
                        for c in range(b + 1, 5):
                            last = subtract(OFF[b] + QS[c] - QS[b], neg1_r, OFF[c], QW[c])
                last.then_inc(tri_done, 1)

            def weighted_values(i):
                pe.wait_ge(w_done, 2 * i + 1)
                if i < 3:
                    if i == 0:
                        pe.wait_ge(vc_in, 16)
                    for pos, b in enumerate(SAMPLE_BLOCKS[i]):
                        if pos == 1:
                            pe.wait_ge(w_done, 2 * i + 2)
                        for p in range(PAIRS):
                            vals = v_t[:, 4, bass.ts(p, P)] if b == 8 else vcache[:, b, bass.ts(p, P)]
                            last = pe.matmul(small[:, bass.ts(p, P)], vals,
                                             sa[:, pos * BANK + p * P:pos * BANK + (p + 1) * P],
                                             start=(b == 8 and p == 0), stop=(b == 0), skip_group_check=True)
                else:
                    h = i - 3
                    if h >= 2:
                        pe.wait_ge(attn_lo_done, 2 + h - 1)
                    for b in range(5):
                        if b == 1:
                            pe.wait_ge(w_done, 2 * i + 2)
                        last = pe.matmul(xo[:, h % 2, QS[b]:SEQ], v_t[:, b, bass.ts(h // 2, P)],
                                         sa[:, OFF[b]:OFF[b] + QW[b]],
                                         start=(b == 0), stop=(b == 4), skip_group_check=True)
                last.then_inc(pv_done, 1)

            def pool_group(s):
                pe.wait_ge(pooled, 1)
                pe.wait_ge(wpool_in, 16)
                pe.wait_ge(attn_lo_done, 2)
                if s:
                    pe.wait_ge(pool_scaled, s)
                if s < 4:
                    pe.matmul(small[:, :], wpool[:, s, :], u_t[:, s, META:UP], start=True, stop=True)\
                        .then_inc(pool_mm, 1)
                else:
                    for g in range(4):
                        last = pe.matmul(small[:, bass.ts(g, DEC)], wpool[:, g, :], u_t[:, g, UP + STATE:UT],
                                         start=(g == 0), stop=True, skip_group_check=True)
                    last.then_inc(pool_mm, 1)

            for i in range(ITEMS):
                units = [U_U + 2 * i, U_U + 2 * i + 1] if i < 2 else []
                if i >= 3:
                    units = [U_GATE + 2 * (i - 3), U_GATE + 2 * (i - 3) + 1]
                scores(i)
                for step in range(2):
                    if units:
                        u = units[step]
                        if u < U_GATE:
                            linear(u // 4, u % 4, N_U + u - U_U, h_hi, h_lo, 0, HT)
                        else:
                            linear(u // 4, u % 4, N_GATE + u - U_GATE, h_hi, h_lo, META, HA)
                    if step == 0:
                        suffix_sums(i)
                weighted_values(i)
                if i - 3 >= 3:
                    pool_group(i - 6)

            def branches(q4, j, n):
                split_ready(q4, j)
                for h in range(2):
                    pe.wait_ge(bank_free[h], n)
                    c = slice(h * HA, (h + 1) * HA)
                    for k in range(4):
                        product(lin[:, h, 0:HA], j, k, pool_hi[:, k, c], pool_lo[:, k, c], k == 0, k == 3)
                    for k in range(4):
                        last = product(xo[:, h, 0:HA], j, 4 + k, attn_hi[:, k, c], attn_lo[:, k, c],
                                       k == 0, k == 3)
                    if h == 0:
                        last.then_inc(half_done, 1)
                last.then_inc(unit_done, 1)

            pe.wait_ge(pool_lo_done, 2)
            pe.wait_ge(attn_lo_done, 2 + HEADS)
            with pe.Fori(0, 2) as it:
                for j in range(4):
                    branches(U_BR // 4 + it, j, N_BR + 4 * it + j)

            for m in range(8):
                linear(U_OUT // 4 + m // 4, m % 4, N_OUT + m, mix_hi, mix_lo, 0, HA,
                       chunk_ready=(lambda k: pe.wait_ge(mix_lo_done, 2 * k + 2)) if m == 0 else None)
                if m == 1:
                    pe.wait_ge(ln1.s["row"], 1)
                    norm_shift(ln1)
            norm_sums(ln1)

            for s in range(2):
                if s == 0:
                    linear(U_MLP1[0] // 4, 0, N_MLP1[0], h_hi, h_lo, META, HA,
                           chunk_ready=lambda k: pe.wait_ge(ln1.s["lo"], k + 1))
                    for j in range(1, 4):
                        linear(U_MLP1[0] // 4, j, N_MLP1[0] + j, h_hi, h_lo, META, HA)
                with pe.Fori(1 - s, FH // 4) as it:
                    for j in range(4):
                        linear(U_MLP1[s] // 4 + it, j, N_MLP1[s] + 4 * it + j, h_hi, h_lo, META, HA)

                def mlp2(it):
                    for j in range(4):
                        pe.wait_ge(f_lo_done, 2 * FH * s + FH * (j % 2 + 1))
                        linear(U_MLP2[s] // 4 + it, j, N_MLP2[s] + 2 * it + j // 2, f_hi, f_lo, 0, HA,
                               chunk0=KC * (j % 2), part=(j % 2 == 0, j % 2 == 1))
                if s == 0:
                    with pe.Fori(0, 4) as it:
                        mlp2(it)
                else:
                    mlp2(0)
                    pe.wait_ge(ln2.s["row"], 1)
                    norm_shift(ln2)
                    with pe.Fori(1, 4) as it:
                        mlp2(it)
            norm_sums(ln2)

        @block.scalar
        def _(act):
            def apart():
                act.wait_ge(consts, 1)

            def split(q4, j):
                act.wait_ge(unit_in[j], 16 * (q4 + 1))
                if not (isinstance(q4, int) and 4 * q4 + j < SPLIT):
                    act.wait_ge(unit_done, 4 * q4 + j - 1)
                nc.scalar.activation(whi[:, j % SPLIT, :], raw[:, j, :], ACT.Copy).then_inc(hi_split, 1)

            def split_next(q4, j):
                split(q4 + (j + 1) // 4, (j + 1) % 4)

            def square_chunk(ln, k, par):
                act.wait_ge(ln.s["d"], k + 1)
                if not isinstance(k, int):
                    act.wait_ge(ln.s["sumsq"], k)
                elif k >= 2:
                    act.wait_ge(ln.s["sumsq"], k - 1)
                nc.scalar.activation(ln.sq[:, par, :], ln.d[:, par, :], ACT.Square).then_inc(ln.s["sq"], 1)

            def root(ln):
                act.wait_ge(ln.s["var"], 1)
                nc.scalar.activation(ln.rstd[:, 0, :], ln.sumsq[:, 0, :], ACT.Sqrt).then_inc(ln.s["std"], 1)

            def affine(ln, k):
                act.wait_ge(ln.s["scaled"], k + 1)
                out = ln.r[:, k, :] if ln is ln2 else h_hi[:, k, ln.col:T]
                nc.scalar.activation(out, ln.r[:, k, :], ACT.Identity, bias=vec(ln.b + k),
                                     scale=vec(ln.g + k)).then_inc(ln.s["hi"], 1)

            act.dma_start(vecs[:, :], vecs_d).then_inc(vecs_in, 16)
            act.dma_start(wpool[:, :, :], wpool_d).then_inc(wpool_in, 16)

            act.wait_ge(made, 4)
            nc.scalar.activation(tri_r[:, :], tri[:, :], ACT.Copy)
            nc.scalar.activation(neg1_r[:, :], neg1[:, :], ACT.Copy).then_inc(consts, 1)
            for k in range(KC):
                square_chunk(ln_in, k, k % 2)
            split(0, 0)
            root(ln_in)
            act.wait_ge(vecs_in, 16)
            for k in range(KC):
                affine(ln_in, k)

            for m in range(4):
                split_next(0, m)
                act.wait_ge(half_done, N_K + m + 1)
                nc.scalar.activation(k_t[:, m, 0:HT], lin[:, 0, 0:HT], ACT.Identity,
                                     bias=vec(V_BIN + C_K + m)).then_inc(bank_free[0], 1)
            for j in range(4):
                split_next(1, j)
            act.wait_ge(bq8_done, 1)
            act.wait_ge(q_zero, 1)
            for m in range(4):
                split_next(2, m)
                act.wait_ge(half_done, N_Q + m + 1)
                for e in range(2):
                    rows = slice(64 * e, 64 * e + 64)
                    last = nc.scalar.activation(q_t[rows, 2 * m + e, 0:HA], lin[rows, 0, 0:HA], ACT.Identity,
                                                bias=bq8[rows, m:m + 1], scale=SB_SCALE)
                last.then_inc(bank_free[0], 1)

            def softplus_tail(i):
                act.wait_ge(qk_done, i + 1)
                n = (ZS if i < 3 else ZP) // 2
                pieces = [slice(c * n, (c + 1) * n) for c in range(2)]
                for c in range(2):
                    nc.scalar.activation(sa[:, pieces[c]], zf[:, pieces[c]], ACT.Abs).then_inc(abs_done, 1)
                for c in range(2):
                    act.wait_ge(abs_done, 2 * i + c + 1)
                    nc.scalar.activation(sa[:, pieces[c]], sa[:, pieces[c]], ACT.Exp, scale=-1.0)\
                        .then_inc(expn_done, 1)
                for c in range(2):
                    act.wait_ge(expn_done, 2 * i + c + 1)
                    nc.scalar.activation(sa[:, pieces[c]], sa[:, pieces[c]], ACT.Ln, bias=1.0)\
                        .then_inc(ln_done, 1)

            def softplus_hi(i):
                n = (ZS if i < 3 else ZP) // 2
                for c in range(2):
                    act.wait_ge(sp_done, 2 * i + c + 1)
                    nc.scalar.activation(sp_hi[:, c * n:(c + 1) * n], sa[:, c * n:(c + 1) * n], ACT.Copy)\
                        .then_inc(sphi_done, 1)

            def weights(i):
                act.wait_ge(tri_done, i + 1)
                n = ZS if i < 3 else ZP
                for a, b in ((0, BANK), (BANK, n)):
                    nc.scalar.activation(sa[:, a:b], zf[:, a:b], ACT.Exp).then_inc(w_done, 1)

            def head_out_hi(i):
                if i < 2:
                    return
                act.wait_ge(pv_done, i + 1)
                if i == 2:
                    for e in range(2):
                        rows = slice(64 * e, 64 * e + 64)
                        src = small[rows, :].rearrange("p (c n) -> p c n", c=PAIRS)[:, :, 64 * e:64 * e + 64]
                        nc.scalar.activation(attn_hi[rows, :, SEQ:TA], src, ACT.Copy).then_inc(attn_hi_done, 1)
                else:
                    h = i - 3
                    rows = slice(64 * (h % 2), 64 * (h % 2) + 64)
                    nc.scalar.activation(attn_hi[rows, h // 2, 0:SEQ], xo[rows, h % 2, :], ACT.Copy)\
                        .then_inc(attn_hi_done, 1)

            def unit_between(u):
                if u < U_GATE:
                    m = u - U_U
                    act.wait_ge(half_done, N_U + m + 1)
                    nc.scalar.activation(u_t[:, m, 0:HT], lin[:, 0, 0:HT], ACT.Identity,
                                         bias=vec(V_BIN + C_U + m)).then_inc(bank_free[0], 1)
                else:
                    m = u - U_GATE
                    act.wait_ge(half_done, N_GATE + m + 1)
                    nc.scalar.activation(gates[:, m // KC, m % KC, 0:HA], lin[:, 0, 0:HA], ACT.Identity,
                                         bias=vec(V_BIN + C_GATE + m)).then_inc(bank_free[0], 1)

            for i in range(ITEMS):
                units = [U_U + 2 * i, U_U + 2 * i + 1] if i < 2 else []
                if i >= 3:
                    units = [U_GATE + 2 * (i - 3), U_GATE + 2 * (i - 3) + 1]
                softplus_tail(i)
                if units:
                    split_next(units[0] // 4, units[0] % 4)
                softplus_hi(i)
                if units:
                    unit_between(units[0])
                    split_next(units[1] // 4, units[1] % 4)
                weights(i)
                if units:
                    unit_between(units[1])
                head_out_hi(i)
            act.wait_ge(pool_scaled, 5)
            act.wait_ge(k_stored, 16)
            nc.scalar.activation(pool_hi[:, :, 0:SEQ], u_t[:, :, META:UP], ACT.Copy).then_inc(pool_hi_done, 1)
            nc.scalar.activation(pool_hi[:, :, SEQ:TA], u_t[:, :, UP + STATE:UT], ACT.Copy)\
                .then_inc(pool_hi_done, 1)
            act.wait_ge(v_stored, 32)

            with act.Fori(0, 2) as it:
                for j in range(4):
                    m = 4 * it + j
                    split_next(U_BR // 4 + it, j)
                    for g in range(2):
                        nc.scalar.activation(gates[:, g, bass.ds(m, 1), :], gates[:, g, bass.ds(m, 1), :],
                                             ACT.Sigmoid).then_inc(sig_done, 1)
                    for h in range(2):
                        act.wait_ge(br_summed, 2 * m + h + 1)
                        apart()
                        nc.scalar.activation(mix_hi[:, bass.ds(m, 1), h * HA:(h + 1) * HA], br_a[:, h:h + 1, :],
                                             ACT.Copy).then_inc(mix_hi_done, 1)

            for m in range(8):
                split_next(U_OUT // 4 + m // 4, m % 4)
                act.wait_ge(half_done, N_OUT + m + 1)
                nc.scalar.activation(ln1.r[:, m, 0:HA], lin[:, 0, 0:HA], ACT.Identity,
                                     bias=vec(V_BOUT + m)).then_inc(bank_free[0], 1)
                act.wait_ge(unit_done, U_OUT + m + 1)
                nc.scalar.activation(ln1.r[:, m, HA:TA], lin[:, 1, 0:HA], ACT.Identity,
                                     bias=vec(V_BOUT + m)).then_inc(bank_free[1], 1)
                if m >= 2:
                    square_chunk(ln1, m - 2, m % 2)
            square_chunk(ln1, 6, 0)
            square_chunk(ln1, 7, 1)
            root(ln1)
            for k in range(KC):
                affine(ln1, k)

            def hidden(s, it):
                nc.scalar.activation(b1_now[:, :], vecs[:, bass.ds(V_B1 + FH * s + 4 * it, 4)], ACT.Copy)\
                    .then_inc(b1_loaded, 1)
                for j in range(4):
                    c = 4 * it + j
                    split_next(U_MLP1[s] // 4 + it, j)
                    if j == 0:
                        act.wait_ge(b1_loaded, FH // 4 * s + it + 1)
                    for h in range(2):
                        if h == 0:
                            if not (s == 0 and isinstance(c, int) and c == 0):
                                act.wait_ge(f_lo_done, 2 * (FH * s + c))
                            act.wait_ge(half_done, N_MLP1[s] + c + 1)
                        else:
                            act.wait_ge(unit_done, U_MLP1[s] + c + 1)
                        nc.scalar.activation(relu_t[:, h, :], lin[:, h, 0:HA], ACT.Relu,
                                             bias=b1_now[:, j:j + 1]).then_inc(bank_free[h], 1)
                        act.wait_ge(bank_free[h], N_MLP1[s] + c + 1)
                        apart()
                        nc.scalar.activation(f_hi[:, bass.ds(c, 1), h * HA:(h + 1) * HA], relu_t[:, h:h + 1, :],
                                             ACT.Square).then_inc(f_hi_done, 1)

            for s in range(2):
                if s == 0:
                    hidden(0, 0)
                with act.Fori(1 - s, FH // 4) as it:
                    hidden(s, it)
                if s == 0:
                    with act.Fori(0, 4) as it:
                        for j in range(4):
                            m = 2 * it + j // 2
                            split_next(U_MLP2[0] // 4 + it, j)
                            if j % 2:
                                act.wait_ge(half_done, N_MLP2[0] + m + 1)
                                apart()
                                nc.scalar.activation(ln2.r[:, bass.ds(m, 1), 0:HA], lin[:, 0:1, 0:HA],
                                                     ACT.Identity, bias=vec(V_B2 + m)).then_inc(bank_free[0], 1)
                                act.wait_ge(unit_done, U_MLP2[0] + 4 * it + j + 1)
                                apart()
                                nc.scalar.activation(ln2.r[:, bass.ds(m, 1), HA:TA], lin[:, 1:2, 0:HA],
                                                     ACT.Identity, bias=vec(V_B2 + m)).then_inc(bank_free[1], 1)
                else:
                    split_next(U_MLP2[1] // 4, 0)
                    split_next(U_MLP2[1] // 4, 1)
                    split_next(U_MLP2[1] // 4, 2)
                    split_next(U_MLP2[1] // 4, 3)
                    square_chunk(ln2, 0, 0)
                    with act.Fori(1, 3) as it:
                        for j in range(4):
                            split_next(U_MLP2[1] // 4 + it, j)
                            if j % 2 == 0:
                                square_chunk(ln2, 2 * it - 1 + j // 2, (1 + j // 2) % 2)
                    for j in range(3):
                        split_next(U_MLP2[1] // 4 + 3, j)
                        if j % 2 == 0:
                            square_chunk(ln2, 5 + j // 2, (1 + j // 2) % 2)
                    square_chunk(ln2, 7, 1)
            root(ln2)
            for k in range(KC):
                affine(ln2, k)

        @block.vector
        def _(dve):
            tt = nc.vector.tensor_tensor

            def split(q4, j):
                dve.wait_ge(hi_split, 4 * q4 + j + 1)
                tt(wlo[:, j % SPLIT, :], raw[:, j, :], whi[:, j % SPLIT, :].bitcast(F32), ALU.subtract)\
                    .then_inc(lo_split, 1)

            def split_next(q4, j):
                split(q4 + (j + 1) // 4, (j + 1) % 4)

            def norm_shift(ln):
                dve.wait_ge(ln.s["shift_mm"], 1)
                nc.vector.tensor_scalar(both(ln.shift[:, 0, :], ln.w), z[:, 0:2, 0:ln.hw], -1.0 / P, None,
                                        ALU.mult).then_inc(ln.s["shift"], 1)
                dve.wait_ge(ln.s["shift"], 1)

            def shifted(ln, k, par):
                if not isinstance(k, int):
                    dve.wait_ge(ln.s["sq"], k)
                    dve.wait_ge(ln.s["sum"], k)
                elif k >= 2:
                    dve.wait_ge(ln.s["sq"], k - 1)
                    dve.wait_ge(ln.s["mm"] if ln is ln_in else ln.s["sum"], k - 1)
                tt(ln.d[:, par:par + 1, :], ln.r[:, bass.ds(k, 1), :], ln.shift[:, 0:1, :], ALU.subtract)\
                    .then_inc(ln.s["d"], 1)

            def normalise(ln):
                s, n = ln.s, ln.w
                dve.wait_ge(s["sums_mm"], 1)
                ts = nc.vector.tensor_scalar
                ts(both(ln.sum[:, 0, :], n), xo[:, :, 0:ln.hw], -1.0 / D_MODEL, None, ALU.mult)\
                    .then_inc(s["step"], 1)
                dve.wait_ge(s["step"], 1)
                tt(ln.sq[:, 0, :], ln.sum[:, 0, :], ln.sum[:, 0, :], ALU.mult).then_inc(s["step"], 1)
                tt(ln.mean[:, 0, :], ln.sum[:, 0, :], ln.shift[:, 0, :], ALU.add).then_inc(s["step"], 1)
                dve.wait_ge(s["step"], 2)
                nc.vector.scalar_tensor_tensor(out=both(ln.sq[:, 1, :], n), in0=z[:, 0:2, 0:ln.hw],
                                               scalar=-1.0 / D_MODEL, in1=both(ln.sq[:, 0, :], n),
                                               op0=ALU.mult, op1=ALU.subtract).then_inc(s["step"], 1)
                dve.wait_ge(s["step"], 4)
                ts(ln.sumsq[:, 0, :], ln.sq[:, 1, :], 0.0, LN_EPS, ALU.max, ALU.add).then_inc(s["var"], 1)
                for k in range(KC):
                    tt(ln.r[:, k, :], ln.r[:, k, :], ln.mean[:, 0, :], ALU.subtract).then_inc(s["centred"], 1)
                dve.wait_ge(s["std"], 1)
                nc.vector.reciprocal(ln.rstd[:, 0, :], ln.rstd[:, 0, :]).then_inc(s["rstd"], 1)
                dve.wait_ge(s["rstd"], 1)
                dve.wait_ge(s["centred"], KC)
                for k in range(KC):
                    tt(ln.r[:, k, :], ln.r[:, k, :], ln.rstd[:, 0, :], ALU.mult).then_inc(s["scaled"], 1)
                    if ln is not ln2 and k:
                        norm_lo(ln, k - 1)
                if ln is not ln2:
                    norm_lo(ln, KC - 1)

            def norm_lo(ln, k):
                dve.wait_ge(ln.s["affine"], k + 1)
                dve.wait_ge(ln.s["hi"], k + 1)
                tt(h_lo[:, k, ln.col:T], ln.d[:, k % 2, :], h_hi[:, k, ln.col:T].bitcast(F32), ALU.subtract)\
                    .then_inc(ln.s["lo"], 1)

            dve.wait_ge(x_in[0], 16)
            norm_shift(ln_in)

            def add_squares(k):
                dve.wait_ge(ln_in.s["sq"], k + 1)
                if k == 0:
                    nc.vector.tensor_copy(ln_in.sumsq[:, 0, :], ln_in.sq[:, 0, :]).then_inc(ln_in.s["sumsq"], 1)
                else:
                    dve.wait_ge(ln_in.s["sumsq"], k)
                    tt(ln_in.sumsq[:, 0, :], ln_in.sumsq[:, 0, :], ln_in.sq[:, k % 2, :], ALU.add)\
                        .then_inc(ln_in.s["sumsq"], 1)

            for k in range(KC):
                dve.wait_ge(x_in[k], 16)
                shifted(ln_in, k, k % 2)
                if k:
                    add_squares(k - 1)
            add_squares(KC - 1)
            split(0, 0)
            normalise(ln_in)
            dve.wait_ge(vecs_in, 16)
            nc.vector.tensor_scalar(bq8[:, :], vecs[:, V_BIN + C_Q:V_BIN + C_Q + 4], SB_SCALE, None, ALU.mult)\
                .then_inc(bq8_done, 1)

            def add_bias(out, src, col, freed=None):
                op = nc.vector.tensor_scalar(out, src, vec(col), None, ALU.add)
                if freed is not None:
                    op.then_inc(freed, 1)

            for m in range(4):
                split_next(0, m)
                dve.wait_ge(unit_done, U_K + m + 1)
                add_bias(k_t[:, m, HT:T], lin[:, 1, 0:HT], V_BIN + C_K + m, bank_free[1])
            for j in range(4):
                split_next(1, j)
            dve.wait_ge(unit_done, U_V + 4)
            dve.wait_ge(bv_in, 16)
            for t in range(5):
                tt(v_t[:, t, :], z[:, t, :] if t < 3 else xo[:, t - 3, :], bv[:, :], ALU.add)\
                    .then_inc(v_ready, 1)
            dve.wait_ge(q_zero, 1)
            for m in range(4):
                split_next(2, m)
                dve.wait_ge(unit_done, U_Q + m + 1)
                for e in range(2):
                    rows = slice(64 * e, 64 * e + 64)
                    last = nc.vector.tensor_scalar(q_t[rows, 2 * m + e, HA:TA], lin[rows, 1, 0:HA],
                                                   vecs[rows, V_BIN + C_Q + m:V_BIN + C_Q + m + 1], SB_SCALE,
                                                   ALU.add, ALU.mult)
                last.then_inc(bank_free[1], 1)

            def softplus(i):
                n = (ZS if i < 3 else ZP) // 2
                for c in range(2):
                    cols = slice(c * n, (c + 1) * n)
                    dve.wait_ge(ln_done, 2 * i + c + 1)
                    nc.vector.scalar_tensor_tensor(out=sa[:, cols], in0=zf[:, cols], scalar=0.0, in1=sa[:, cols],
                                                   op0=ALU.max, op1=ALU.add).then_inc(sp_done, 1)

            def add_later(i):
                if i > 1:
                    return
                dve.wait_ge(sp_done, 2 * i + 2)
                terms = [sa[:, pos * BANK:(pos + 1) * BANK] for pos in range(3)]
                if i == 1:
                    terms.insert(0, later[:, 0, :])
                acc, done = later[:, i, :], 2 * i
                tt(acc, terms[0], terms[1], ALU.add).then_inc(later_done, 1)
                for t in terms[2:]:
                    done += 1
                    dve.wait_ge(later_done, done)
                    tt(acc, acc, t, ALU.add).then_inc(later_done, 1)

            def softplus_lo(i):
                n = (ZS if i < 3 else ZP) // 2
                for c in range(2):
                    cols = slice(c * n, (c + 1) * n)
                    dve.wait_ge(sphi_done, 2 * i + c + 1)
                    tt(sp_lo[:, cols], sa[:, cols], sp_hi[:, cols].bitcast(F32), ALU.subtract)\
                        .then_inc(splo_done, 1)

            def head_out_lo(i):
                if i == 2:
                    for e in range(2):
                        rows = slice(64 * e, 64 * e + 64)
                        dve.wait_ge(attn_hi_done, e + 1)
                        src = small[rows, :].rearrange("p (c n) -> p c n", c=PAIRS)[:, :, 64 * e:64 * e + 64]
                        tt(attn_lo[rows, :, SEQ:TA], src, attn_hi[rows, :, SEQ:TA].bitcast(F32), ALU.subtract)\
                            .then_inc(attn_lo_done, 1)
                elif i > 2:
                    h = i - 3
                    rows = slice(64 * (h % 2), 64 * (h % 2) + 64)
                    dve.wait_ge(attn_hi_done, 2 + h + 1)
                    tt(attn_lo[rows, h // 2, 0:SEQ], xo[rows, h % 2, :], attn_hi[rows, h // 2, 0:SEQ].bitcast(F32),
                       ALU.subtract).then_inc(attn_lo_done, 1)

            def unit_between(u):
                dve.wait_ge(unit_done, u + 1)
                if u < U_GATE:
                    m = u - U_U
                    add_bias(u_t[:, m, HT:UP], lin[:, 1, 0:UP - HT], V_BIN + C_U + m)
                    add_bias(u_t[:, m, UP + STATE:UT], lin[:, 1, UP - HT:HT], V_BIN + C_U + m, bank_free[1])
                else:
                    m = u - U_GATE
                    add_bias(gates[:, m // KC, m % KC, HA:TA], lin[:, 1, 0:HA], V_BIN + C_GATE + m, bank_free[1])

            def pool_scale(s):
                dve.wait_ge(pool_mm, s + 1)
                if s < 4:
                    nc.vector.tensor_scalar(u_t[:, s, META:UP], small[:, :], vec(V_PSCALE + s), None, ALU.mult)\
                        .then_inc(pool_scaled, 1)
                else:
                    for g in range(4):
                        last = nc.vector.tensor_scalar(u_t[:, g, UP + STATE:UT], small[:, bass.ts(g, DEC)],
                                                       vec(V_PSCALE + g), None, ALU.mult)
                    last.then_inc(pool_scaled, 1)

            for i in range(ITEMS):
                units = [U_U + 2 * i, U_U + 2 * i + 1] if i < 2 else []
                if i >= 3:
                    units = [U_GATE + 2 * (i - 3), U_GATE + 2 * (i - 3) + 1]
                if units:
                    split_next(units[0] // 4, units[0] % 4)
                softplus(i)
                add_later(i)
                softplus_lo(i)
                if units:
                    unit_between(units[0])
                    split_next(units[1] // 4, units[1] % 4)
                    unit_between(units[1])
                head_out_lo(i)
                if i - 3 >= 3:
                    pool_scale(i - 6)
            dve.wait_ge(pool_hi_done, 1)
            tt(pool_lo[:, :, 0:SEQ], u_t[:, :, META:UP], pool_hi[:, :, 0:SEQ].bitcast(F32), ALU.subtract)\
                .then_inc(pool_lo_done, 1)
            dve.wait_ge(pool_hi_done, 2)
            tt(pool_lo[:, :, SEQ:TA], u_t[:, :, UP + STATE:UT], pool_hi[:, :, SEQ:TA].bitcast(F32), ALU.subtract)\
                .then_inc(pool_lo_done, 1)

            with dve.Fori(0, 2) as it:
                for j in range(4):
                    m = 4 * it + j
                    split_next(U_BR // 4 + it, j)
                    for h in range(2):
                        cols = slice(h * HA, (h + 1) * HA)
                        dve.wait_ge(half_done, N_BR + m + 1) if h == 0 else dve.wait_ge(unit_done, U_BR + m + 1)
                        dve.wait_ge(sig_done, 2 * m + 2)
                        tt(br_a[:, h:h + 1, :], lin[:, h:h + 1, 0:HA], gates[:, 0, bass.ds(m, 1), cols], ALU.mult)
                        tt(br_b[:, h:h + 1, :], xo[:, h:h + 1, 0:HA], gates[:, 1, bass.ds(m, 1), cols], ALU.mult)\
                            .then_inc(bank_free[h], 1)
                        dve.wait_ge(bank_free[h], N_BR + m + 1)
                        tt(br_a[:, h:h + 1, :], br_a[:, h:h + 1, :], br_b[:, h:h + 1, :], ALU.add)\
                            .then_inc(br_summed, 1)
                    for h in range(2):
                        cols = slice(h * HA, (h + 1) * HA)
                        dve.wait_ge(mix_hi_done, 2 * m + h + 1)
                        tt(mix_lo[:, bass.ds(m, 1), cols], br_a[:, h:h + 1, :],
                           mix_hi[:, bass.ds(m, 1), cols].bitcast(F32), ALU.subtract).then_inc(mix_lo_done, 1)
                    dve.wait_ge(mix_lo_done, 2 * m + 2)

            stt = nc.vector.scalar_tensor_tensor

            def add_residual(ln, m):
                for part, done in ((h_hi, ln.s["part"]), (h_lo, ln.s["row"])):
                    stt(out=ln.r[:, bass.ds(m, 1), :], in0=part[:, bass.ds(m, 1), META:T].bitcast(F32),
                        scalar=ALPHA, in1=ln.r[:, bass.ds(m, 1), :], op0=ALU.mult, op1=ALU.add).then_inc(done, 1)
                    dve.wait_ge(done, m + 1)

            for m in range(8):
                split_next(U_OUT // 4 + m // 4, m % 4)
                dve.wait_ge(bank_free[0], N_OUT + m + 1)
                dve.wait_ge(bank_free[1], N_OUT + m + 1)
                add_residual(ln1, m)
                if m == 2:
                    norm_shift(ln1)
                if m >= 2:
                    shifted(ln1, m - 2, m % 2)
            shifted(ln1, 6, 0)
            shifted(ln1, 7, 1)
            normalise(ln1)

            def hidden(s, it):
                for j in range(4):
                    c = 4 * it + j
                    split_next(U_MLP1[s] // 4 + it, j)
                    for h in range(2):
                        dve.wait_ge(bank_free[h], N_MLP1[s] + c + 1)
                        tt(relu_sq[:, h, :], relu_t[:, h, :], relu_t[:, h, :], ALU.mult).then_inc(f_sq_done, 1)
                        dve.wait_ge(f_sq_done, 2 * (FH * s + c) + h + 1)
                        dve.wait_ge(f_hi_done, 2 * (FH * s + c) + h + 1)
                        cols = slice(h * HA, (h + 1) * HA)
                        tt(f_lo[:, bass.ds(c, 1), cols], relu_sq[:, h:h + 1, :],
                           f_hi[:, bass.ds(c, 1), cols].bitcast(F32), ALU.subtract).then_inc(f_lo_done, 1)

            for s in range(2):
                if s == 0:
                    hidden(0, 0)
                with dve.Fori(1 - s, FH // 4) as it:
                    hidden(s, it)
                if s == 0:
                    with dve.Fori(0, 4) as it:
                        for j in range(4):
                            m = 2 * it + j // 2
                            split_next(U_MLP2[0] // 4 + it, j)
                            if j % 2:
                                dve.wait_ge(bank_free[0], N_MLP2[0] + m + 1)
                                dve.wait_ge(bank_free[1], N_MLP2[0] + m + 1)
                                stt(out=ln2.r[:, bass.ds(m, 1), :], in0=h_hi[:, bass.ds(m, 1), META:T].bitcast(F32),
                                    scalar=ALPHA, in1=ln2.r[:, bass.ds(m, 1), :], op0=ALU.mult, op1=ALU.add)\
                                    .then_inc(ln2.s["part"], 1)
                                dve.wait_ge(ln2.s["part"], 2 * m + 1)
                                stt(out=ln2.r[:, bass.ds(m, 1), :], in0=h_lo[:, bass.ds(m, 1), META:T].bitcast(F32),
                                    scalar=ALPHA, in1=ln2.r[:, bass.ds(m, 1), :], op0=ALU.mult, op1=ALU.add)\
                                    .then_inc(ln2.s["part"], 1)
                else:
                    dve.wait_ge(ln2.s["part"], 2 * KC)
                    U4 = U_MLP2[1] // 4

                    def pair(it, first=False, final=False):
                        for j in range(4):
                            m = 2 * it + j // 2
                            if not (final and j == 3):
                                split_next(U4 + it, j)
                            if j % 2:
                                for h in range(2):
                                    if h == 0:
                                        dve.wait_ge(half_done, N_MLP2[1] + m + 1)
                                    else:
                                        dve.wait_ge(unit_done, U_MLP2[1] + 4 * it + j + 1)
                                    cols = slice(h * HA, (h + 1) * HA)
                                    op = tt(ln2.r[:, bass.ds(m, 1), cols], lin[:, h:h + 1, 0:HA],
                                            ln2.r[:, bass.ds(m, 1), cols], ALU.add)
                                    op.then_inc(bank_free[h], 1)
                                if first and j == 1:
                                    dve.wait_ge(bank_free[1], N_MLP2[1] + 1)
                                    nc.vector.tensor_copy(ln2.d[:, 1, 0:1], ln2.r[:, 0, TA - 1:TA])\
                                        .then_inc(ln2.s["row"], 1)
                            elif first and j == 2:
                                pass
                            elif not first:
                                dve.wait_ge(bank_free[1], N_MLP2[1] + m)
                                shifted(ln2, m - 1, (j // 2 + 1) % 2)

                    pair(0, first=True)
                    norm_shift(ln2)
                    shifted(ln2, 0, 0)
                    with dve.Fori(1, 3) as it:
                        pair(it)
                    pair(3, final=True)
                    dve.wait_ge(bank_free[1], N_MLP2[1] + 8)
                    shifted(ln2, 7, 1)
            normalise(ln2)

        @block.gpsimd
        def _(pool):
            nc.gpsimd.memset(tri[:, :], -1.0).then_inc(made, 1)
            nc.gpsimd.memset(neg1[:, :], -1.0).then_inc(made, 1)
            nc.gpsimd.memset(ident[:, :], 0.0).then_inc(made, 1)
            pool.wait_ge(made, 3)
            nc.gpsimd.affine_select(out=tri[:, :], in_=tri[:, :], compare_op=ALU.is_ge, fill=0.0, base=0,
                                    pattern=[[-1, P]], channel_multiplier=1).then_inc(made, 1)
            nc.gpsimd.affine_select(out=ident[:, :], in_=ident[:, :], compare_op=ALU.not_equal, fill=1.0, base=0,
                                    pattern=[[-1, P]], channel_multiplier=1).then_inc(made, 1)
            nc.gpsimd.memset(mask_diag[:, :], 0.0)
            nc.gpsimd.memset(mask_tail[:, :], 0.0)
            nc.gpsimd.memset(mask_new[:, :, :], 0.0).then_inc(win_done, 1)
            pool.wait_ge(win_done, 1)
            nc.gpsimd.affine_select(out=mask_diag[:, :], in_=mask_diag[:, :], compare_op=ALU.is_ge, fill=NEG,
                                    base=-1, pattern=[[1, P]], channel_multiplier=-1).then_inc(made, 1)
            lead = UP - META - TAIL
            nc.gpsimd.affine_select(out=mask_tail[:, :], in_=mask_tail[:, :], compare_op=ALU.is_ge, fill=NEG,
                                    base=-lead, pattern=[[0, META]], channel_multiplier=1)
            nc.gpsimd.affine_select(out=mask_new[:, :, :], in_=mask_new[:, :, :], compare_op=ALU.is_ge, fill=NEG,
                                    base=-(P - DEC), pattern=[[0, HEADS], [0, DEC]], channel_multiplier=1)\
                .then_inc(win_done, 1)
            pool.wait_ge(win_done, 2)
            nc.gpsimd.affine_select(out=mask_tail[:, :], in_=mask_tail[:, :], compare_op=ALU.is_ge, fill=NEG,
                                    base=lead - 1, pattern=[[1, META]], channel_multiplier=-1).then_inc(made, 1)
            nc.gpsimd.affine_select(out=mask_new[:, :, :], in_=mask_new[:, :, :], compare_op=ALU.is_ge, fill=NEG,
                                    base=P - DEC - 1, pattern=[[0, HEADS], [1, DEC]], channel_multiplier=-1)\
                .then_inc(made, 1)
            nc.gpsimd.memset(q_t[:, :, :], 0.0).then_inc(q_zero, 1)

            def affine_chunks(ln):
                for k in range(KC):
                    pool.wait_ge(ln.s["scaled"], k + 1)
                    if k >= 2:
                        pool.wait_ge(ln.s["lo"], k - 1)
                    nc.gpsimd.tensor_scalar(ln.d[:, k % 2, :], ln.r[:, k, :], vec(ln.g + k), vec(ln.b + k),
                                            ALU.mult, ALU.add).then_inc(ln.s["affine"], 1)

            pool.wait_ge(vecs_in, 16)
            affine_chunks(ln_in)
            pool.dma_start(u_t[:, :, UP:UP + STATE], state_d).then_inc(state_in, 16)
            for h in range(2):
                pool.wait_ge(bank_free[h], N_K + 4)
            pool.dma_start(k_out, k_t[:, :, :]).then_inc(k_stored, 16)
            pool.wait_ge(v_ready, 5)
            pool.dma_start(v_out[0:4 * P, :].rearrange("(t p) d -> p t d", p=P), v_t[:, 0:4, :])\
                .then_inc(v_stored, 16)
            pool.dma_start(v_out[4 * P:T, :], v_t[4 * P - TAIL:P, 4, :]).then_inc(v_stored, 16)

            pool.wait_ge(state_in, 16)
            for h in range(2):
                pool.wait_ge(bank_free[h], N_U + 4)
            nc.gpsimd.tensor_copy(ust[:, :, 0:STATE], u_t[:, :, UP - STATE:UP])
            nc.gpsimd.tensor_copy(ust[:, :, STATE:2 * STATE], u_t[:, :, UT - STATE:UT]).then_inc(ust_done, 1)
            done = 2
            for g, w in enumerate(POOL_WINDOWS):
                src, reach = u_t[:, g, :], 1
                while reach < w:
                    dst = win[:, (reach.bit_length() - 1) % 2, 0:UT]
                    nc.gpsimd.tensor_tensor(dst[:, 2 * reach - 1:UT], src[:, 2 * reach - 1:UT],
                                            src[:, reach - 1:UT - reach], ALU.add).then_inc(win_done, 1)
                    done += 1
                    pool.wait_ge(win_done, done)
                    src, reach = dst, 2 * reach
                nc.gpsimd.tensor_scalar(src[:, META:UT], src[:, META:UT], 1.0 / w, 0.0, ALU.mult, ALU.add)\
                    .then_inc(win_done, 1)
                done += 1
                pool.wait_ge(win_done, done)
                if g == 0:
                    pool.wait_ge(ust_done, 1)
                last = nc.gpsimd.tensor_tensor(u_t[:, g, META:UT], src[:, META:UT], u_t[:, g, META:UT],
                                               ALU.subtract)
                if g < 3:
                    last.then_inc(win_done, 1)
                    done += 1
                    pool.wait_ge(win_done, done)
            last.then_inc(pooled, 1)
            pool.dma_start(s_out, ust[:, :, :]).then_inc(s_stored, 16)

            def add_chunk(ln, k, par):
                first = isinstance(k, int) and k == 0
                for t, acc, src in (("d", ln.sum, ln.d), ("sq", ln.sumsq, ln.sq)):
                    done = ln.s["sum"] if t == "d" else ln.s["sumsq"]
                    pool.wait_ge(ln.s[t], k + 1)
                    if first:
                        nc.gpsimd.tensor_copy(acc[:, 0, :], src[:, par, :]).then_inc(done, 1)
                    else:
                        pool.wait_ge(done, k)
                        nc.gpsimd.tensor_tensor(acc[:, 0, :], acc[:, 0, :], src[:, par, :], ALU.add)\
                            .then_inc(done, 1)

            for m in range(8):
                add_chunk(ln1, m, m % 2)
            affine_chunks(ln1)
            for m in range(8):
                add_chunk(ln2, m, m % 2)


def kernel(**inputs):
    import numpy as np
    import concourse.bacc as bacc
    from concourse.bass_utils import run_bass_kernel_spmd as run

    def units(w):
        n = w.shape[1] // P
        return w.reshape(w.shape[0] // P, P, n, P).transpose(2, 1, 0, 3).reshape(n, P, -1)

    a = {n: np.asarray(v) for n, v in inputs.items()}
    w_in = a["w_in"][0]
    w_u, w_q, w_k, w_v = (w_in[:, i * 512:(i + 1) * 512] for i in range(4))
    w2 = a["w_mlp2"][0].reshape(2, 2, KC, P, KC, P).transpose(0, 4, 1, 3, 2, 5).reshape(2, 2 * KC, P, UNIT)
    w1 = units(a["w_mlp1"][0])
    stream = np.concatenate([
        units(w_k), w_v.reshape(4, 2, P, ATTN_W).transpose(0, 2, 1, 3).reshape(4, P, UNIT), units(w_q), units(w_u),
        units(w_in[:, 2048:]),
        np.concatenate([units(a["w_br_pool"][0]), units(a["w_br_attn"][0])], axis=2),
        units(a["w_out"][0]), w1[:FH], w2[0], w1[FH:], w2[1]])
    cols = [a["b_in"][0], a["pool_scale"][0], a["b_out"][0], a["ln_in_g"], a["ln_in_b"], a["ln1_g"][0],
            a["ln1_b"][0], a["ln2_g"][0], a["ln2_b"][0], a["b_mlp1"][0], a["b_mlp2"][0]]
    arrays = {
        "x_t": np.concatenate([a["meta"], a["x_prompt"][0], a["x_sample"][0]]).T.reshape(KC, P, T),
        "w_stream": stream,
        "vecs": np.concatenate([c.reshape(-1, P) for c in cols]).T,
        "b_v": np.broadcast_to(a["b_in"][0][1536:2048], (P, ATTN_W)),
        "k_cache": a["cache_k"].reshape(PAST, PAIRS, P).transpose(2, 1, 0),
        "v_cache": a["cache_v"].reshape(PAST // P, P, ATTN_W).transpose(1, 0, 2),
        "pool_state": a["state_pool"].reshape(STATE, 4, P).transpose(2, 1, 0),
        "w_pool": a["w_pool_grp"][0].transpose(1, 0, 2),
    }
    arrays = {n: np.ascontiguousarray(v) for n, v in arrays.items()}
    nc = bacc.Bacc("TRN2", target_bir_lowering=False, num_devices=1)
    args = [nc.dram_tensor(n, v.shape, F32, kind="ExternalInput").ap() for n, v in arrays.items()]
    outs = {"y": (P, KC, TA), "k_new": (P, PAIRS, T), "v_new": (T, ATTN_W), "state_new": (P, 4, 2 * STATE)}
    args += [nc.dram_tensor(n, s, F32, kind="ExternalOutput").ap() for n, s in outs.items()]
    encoder_step(nc, *args)
    got = run(nc, [arrays], core_ids=[0]).results[0]
    y = got["y"].transpose(2, 1, 0).reshape(TA, D_MODEL)
    k = got["k_new"].transpose(2, 1, 0).reshape(T, HEADS, HD)
    v = got["v_new"].reshape(T, HEADS, HD)
    s = got["state_new"].transpose(2, 1, 0).reshape(2, STATE, POOL_W)
    return (y[None, :SEQ], y[None, SEQ:], k[None, None, :UP], v[None, None, :UP], s[None, None, 0],
            k[None, None, UP:], v[None, None, UP:], s[None, None, 1])
```

```python
from contextlib import ExitStack

import concourse.bass as bass
from concourse import mybir

F32 = mybir.dt.float32
F32R = mybir.dt.float32r
BF16 = mybir.dt.bfloat16
ALU = mybir.AluOpType
ACT = mybir.ActivationFunctionType

P = 128
D_MODEL, META, SEQ, DEC, PAST = 1024, 16, 512, 64, 1024
HEADS, HD = 8, 64
ATTN_W, POOL_W, D_FF = HEADS * HD, 512, 4096
POOL_WINDOWS = (2, 4, 8, 16)
STATE = max(POOL_WINDOWS) - 1
T = META + SEQ + DEC
TA = SEQ + DEC
HT, HA = T // 2, TA // 2
KC = D_MODEL // P
PAIRS = HEADS // 2
ALPHA = 2.0 ** 0.25
SB_SCALE = HD ** -0.5
LN_EPS = 1e-5
NEG = -1.0e30
BANK = 512
EXP_AND_LN, SIGMOIDS = 6, 2

UNIT = KC * P
U_K, U_Q, U_V, U_U, U_GATE, U_BR, U_OUT = 0, 4, 8, 12, 16, 32, 40
U_MLP1, U_MLP2 = (48, 80), (64, 96)
UNITS = 112
RAW, SPLIT = 4, 2
N_K, N_Q, N_U, N_GATE, N_BR, N_OUT = 0, 4, 8, 12, 28, 36
N_MLP1, N_MLP2 = (44, 68), (60, 84)
FH = D_FF // P // 2

V_BIN, V_PSCALE, V_BOUT = 0, 32, 36
V_LNIN_G, V_LNIN_B, V_LN1_G, V_LN1_B, V_LN2_G, V_LN2_B = 44, 52, 60, 68, 76, 84
V_B1, V_B2, V_COUNT = 92, 124, 132
C_U, C_Q, C_K, C_GATE = 0, 4, 8, 16

QS = [max(0, P * b - META) for b in range(5)]
QW = [SEQ - q for q in QS]
OFF = [sum(QW[:b]) for b in range(5)]
ZP = sum(QW)
ZS = 3 * BANK
TAIL = T - P
SAMPLE_BLOCKS = [(8, 7, 6), (5, 4, 3), (2, 1, 0)]
ITEMS = 3 + HEADS
_halves = [(u, h) for u in range(U_U, U_BR) for h in range(2)]
BEFORE = [_halves[4 * i - 2:4 * i + 1] for i in range(1, ITEMS - 1)]
BEFORE = [[]] + BEFORE + [_halves[-2:]]
AFTER = [_halves[:2]] + [_halves[4 * i + 1:4 * i + 2] for i in range(1, ITEMS - 1)] + [[]]
UP = META + SEQ
UT = UP + STATE + DEC


def bank_pieces(dst, n):
    at = 0
    while at < n:
        w = min(n - at, BANK - (dst + at) % BANK)
        yield dst + at, at, w
        at += w


def encoder_step(nc, x, wstream, vecs_d, bv_d, kc_d, vc_d, state_d, wpool_d, y_out, k_out, v_out, s_out):
    with ExitStack() as ctx:
        base = 16512

        def sb(name, shape, dt, at):
            return nc.alloc_sbuf_tensor_at(name, [P] + shape, dt, offset=base + 4 * at)

        def sem(name):
            return ctx.enter_context(nc.semaphore(name))

        raw = sb("raw", [RAW, UNIT], F32, 0)
        whi = sb("whi", [SPLIT, UNIT], F32R, 4096)
        wlo = sb("wlo", [SPLIT, UNIT], F32R, 6144)
        h_hi = sb("h_hi", [KC, T], F32R, 8192)
        h_lo = sb("h_lo", [KC, T], F32R, 12928)
        bv = sb("bv", [ATTN_W], F32, 17664)
        tri = sb("tri", [P], F32, 18176)
        neg1 = sb("neg1", [P], F32, 18304)
        tri_r = sb("tri_r", [P], F32R, 18432)
        neg1_r = sb("neg1_r", [P], F32R, 18560)
        ident = sb("ident", [P], BF16, 18688)
        mask_diag = sb("mask_diag", [P], BF16, 18752)
        mask_tail = sb("mask_tail", [META], BF16, 18816)
        mask_new = sb("mask_new", [HEADS, DEC], BF16, 18824)
        vecs = sb("vecs", [V_COUNT], F32, 19080)
        bq8 = sb("bq8", [4], F32, 19216)
        b1_now = sb("b1_now", [4], F32, 19224)
        wpool = sb("wpool", [4, P], F32, 19232)
        A0 = 19744
        kcache = sb("kcache", [PAIRS, PAST], F32, A0)
        vcache = sb("vcache", [8, ATTN_W], F32, A0 + 4096)
        gates = sb("gates", [2, KC, TA], F32, A0)
        k_t = sb("k_t", [PAIRS, T], F32, A0 + 9216)
        q_t = sb("q_t", [HEADS, TA], F32, A0 + 11584)
        v_t = sb("v_t", [5, ATTN_W], F32, A0 + 16192)
        attn_hi = sb("attn_hi", [PAIRS, TA], F32R, A0 + 18752)
        attn_lo = sb("attn_lo", [PAIRS, TA], F32R, A0 + 21056)
        u_t = sb("u_t", [4, UT], F32, A0 + 23360)
        sa = sb("sa", [ZS], F32, A0 + 25848)
        sp_hi = sb("sp_hi", [ZS], F32R, A0 + 27384)
        sp_lo = sb("sp_lo", [ZS], F32R, A0 + 28920)
        later = sb("later", [2, BANK], F32, A0 + 30456)
        win = sb("win", [2, 608], F32, A0 + 31480)
        ust = sb("ust", [4, 2 * STATE], F32, A0 + 32704)
        pool_hi = sb("pool_hi", [4, TA], F32R, A0 + 9216)
        pool_lo = sb("pool_lo", [4, TA], F32R, A0 + 11520)
        mix_hi = sb("mix_hi", [KC, TA], F32R, A0 + 13824)
        mix_lo = sb("mix_lo", [KC, TA], F32R, A0 + 23360)
        br_a = sb("br_a", [2, HA], F32, A0 + 29000)
        br_b = sb("br_b", [2, HA], F32, A0 + 29576)
        f_hi = sb("f_hi", [FH, TA], F32R, A0 + 4608)
        f_lo = sb("f_lo", [FH, TA], F32R, A0 + 13824)
        relu_t = sb("relu_t", [2, HA], F32, A0 + 29000)
        relu_sq = sb("relu_sq", [2, HA], F32, A0 + 29576)

        z = ctx.enter_context(nc.psum_tensor("z", [P, 3, BANK], F32))
        xo = ctx.enter_context(nc.psum_tensor("xo", [P, 2, BANK], F32))
        lin = ctx.enter_context(nc.psum_tensor("lin", [P, 2, BANK], F32))
        small = ctx.enter_context(nc.psum_tensor("small", [P, BANK], F32))
        zf = z[:, :, :].rearrange("p b n -> p (b n)")

        vecs_in, bv_in, wpool_in = sem("vecs_in"), sem("bv_in"), sem("wpool_in")
        kc_in, vc_in, state_in = sem("kc_in"), sem("vc_in"), sem("state_in")
        x_in = [sem(f"x_in{k}") for k in range(KC)]
        unit_in = [sem(f"unit_in{s}") for s in range(RAW)]
        hi_split, lo_split = sem("hi_split"), sem("lo_split")
        half_done, unit_done = sem("half_done"), sem("unit_done")
        bank_free = [sem("bank_free0"), sem("bank_free1")]
        made, consts = sem("made"), sem("consts")
        q_zero, bq8_done = sem("q_zero"), sem("bq8_done")
        v_ready, k_stored, v_stored, s_stored, y_stored = (
            sem("v_ready"), sem("k_stored"), sem("v_stored"), sem("s_stored"), sem("y_stored"))
        qk_done, abs_done, expn_done, ln_done, sp_done = (
            sem("qk_done"), sem("abs_done"), sem("expn_done"), sem("ln_done"), sem("sp_done"))
        sphi_done, splo_done, later_done, tri_done, w_done, pv_done = (
            sem("sphi_done"), sem("splo_done"), sem("later_done"), sem("tri_done"), sem("w_done"), sem("pv_done"))
        attn_hi_done, attn_lo_done = sem("attn_hi_done"), sem("attn_lo_done")
        win_done, ust_done, pooled = sem("win_done"), sem("ust_done"), sem("pooled")
        pool_mm, pool_scaled, pool_hi_done, pool_lo_done = (
            sem("pool_mm"), sem("pool_scaled"), sem("pool_hi_done"), sem("pool_lo_done"))
        sig_done, br_gated, br_summed, mix_hi_done, mix_lo_done = (
            sem("sig_done"), sem("br_gated"), sem("br_summed"), sem("mix_hi_done"), sem("mix_lo_done"))
        b1_loaded = sem("b1_loaded")
        relu_done, f_hi_done, f_sq_done, f_lo_done = (
            sem("relu_done"), sem("f_hi_done"), sem("f_sq_done"), sem("f_lo_done"))

        class Norm:

            def __init__(self, name, width, r_at, tmp_at, g, b, col):
                self.w, self.hw, self.g, self.b, self.col = width, width // 2, g, b, col
                self.r = sb(name + "_r", [KC, width], F32, A0 + r_at)
                t = [sb(f"{name}_{s}", [n, width], F32, A0 + tmp_at + o * width)
                     for s, n, o in (("shift", 1, 0), ("sum", 1, 1), ("sumsq", 1, 2), ("mean", 1, 3),
                                     ("rstd", 1, 4), ("d", 2, 5), ("sq", 2, 7))]
                self.shift, self.sum, self.sumsq, self.mean, self.rstd, self.d, self.sq = t
                self.s = {s: sem(f"{name}_{s}") for s in (
                    "row", "part", "shift_mm", "shift", "d", "sq", "sum", "sumsq", "sums_mm", "step",
                    "var", "std", "rstd", "centred", "scaled", "hi", "affine", "lo", "mm")}

        ln_in = Norm("ln_in", T, 18752, 23488, V_LNIN_G, V_LNIN_B, 0)
        ln1 = Norm("ln1", TA, 0, 4608, V_LN1_G, V_LN1_B, META)
        ln2 = Norm("ln2", TA, 0, 23040, V_LN2_G, V_LN2_B, META)
        block = ctx.enter_context(nc.Block())

        def vec(col):
            return vecs[:, bass.ds(col, 1)]

        def v_bank(t):
            return xo[:, t, :] if t < 2 else lin[:, t - 2, :] if t < 4 else small[:, :]

        def both(t, w):
            return t.rearrange("p (b n) -> p b n", b=2)

        @block.sync
        def _(sp):
            def load_unit(q4, j, first=False):
                if not first:
                    sp.wait_ge(lo_split, (q4 - 1) * RAW + j + 1)
                sp.dma_start(raw[:, j, :], wstream[q4 * RAW + j]).then_inc(unit_in[j], 16)

            for k in range(KC):
                sp.dma_start(ln_in.r[:, k, :], x[k]).then_inc(x_in[k], 16)
            for j in range(RAW):
                load_unit(0, j, first=True)
            sp.dma_start(bv[:, :], bv_d).then_inc(bv_in, 16)
            sp.dma_start(kcache[:, :, :], kc_d).then_inc(kc_in, 16)
            load_unit(1, 0)
            load_unit(1, 1)
            sp.dma_start(vcache[:, :, :], vc_d).then_inc(vc_in, 16)
            load_unit(1, 2)
            load_unit(1, 3)
            with sp.Fori(2, UNITS // RAW) as q4:
                for j in range(RAW):
                    load_unit(q4, j)
            for k in range(KC):
                sp.wait_ge(ln2.s["hi"], k + 1)
                sp.dma_start(y_out[:, k, :], ln2.r[:, k, :]).then_inc(y_stored, 16)
            sp.wait_ge(y_stored, 16 * KC)
            sp.wait_ge(k_stored, 16)
            sp.wait_ge(v_stored, 32)
            sp.wait_ge(s_stored, 16)

        @block.tensor
        def _(pe):
            def split_ready(q4, j):
                pe.wait_ge(lo_split, 4 * q4 + j + 1)

            def product(out, j, k, hi, lo, first, last):
                w_h, w_l = whi[:, j % SPLIT, bass.ts(k, P)], wlo[:, j % SPLIT, bass.ts(k, P)]
                pe.matmul(out, w_h, hi, start=first, stop=False)
                pe.matmul(out, w_h, lo, start=False, stop=False)
                return pe.matmul(out, w_l, hi, start=False, stop=last)

            def linear(q4, j, n, hi, lo, col, hw, chunk0=0, chunk_ready=None, part=(True, True)):
                split_ready(q4, j)
                opens, closes = part

                def free(h):
                    if opens and not (isinstance(n, int) and n == 0):
                        pe.wait_ge(bank_free[h], n)

                def mm(h, k):
                    c = slice(col + h * hw, col + (h + 1) * hw)
                    return product(lin[:, h, 0:hw], j, k, hi[:, chunk0 + k, c], lo[:, chunk0 + k, c],
                                   opens and k == 0, closes and k == KC - 1)

                if chunk_ready is None:
                    for h in range(2):
                        free(h)
                        for k in range(KC):
                            last = mm(h, k)
                        if h == 0 and closes:
                            last.then_inc(half_done, 1)
                    last.then_inc(unit_done, 1)
                else:
                    free(0)
                    free(1)
                    for k in range(KC):
                        chunk_ready(k)
                        for h in range(2):
                            last = mm(h, k)
                            if h == 0 and k == KC - 1 and closes:
                                last.then_inc(half_done, 1)
                    last.then_inc(unit_done, 1)

            def sum_halves(dst, src, ln):
                for h in range(2):
                    last = pe.matmul(dst[:, h, 0:ln.hw], neg1[:, :], src[:, h * ln.hw:(h + 1) * ln.hw],
                                     start=True, stop=True)
                return last

            def norm_shift(ln):
                sum_halves(z, ln.r[:, 0, :], ln).then_inc(ln.s["shift_mm"], 1)

            def norm_sums(ln):
                pe.wait_ge(ln.s["sum"], KC)
                sum_halves(xo, ln.sum[:, 0, :], ln)
                pe.wait_ge(ln.s["sumsq"], KC)
                pe.wait_ge(ln.s["shift"], 1)
                sum_halves(z, ln.sumsq[:, 0, :], ln).then_inc(ln.s["sums_mm"], 1)

            pe.wait_ge(made, 4)
            pe.wait_ge(x_in[0], 16)
            norm_shift(ln_in)
            for k in range(KC):
                pe.wait_ge(ln_in.s["d"], k + 1)
                for h in range(2):
                    last = pe.matmul(xo[:, h, 0:HT], neg1[:, :], ln_in.d[:, k % 2, h * HT:(h + 1) * HT],
                                     start=(k == 0), stop=(k == KC - 1))
                last.then_inc(ln_in.s["mm"], 1)
            pe.wait_ge(ln_in.s["sumsq"], KC)
            sum_halves(z, ln_in.sumsq[:, 0, :], ln_in).then_inc(ln_in.s["sums_mm"], 1)

            for m in range(4):
                linear(0, m, N_K + m, h_hi, h_lo, 0, HT,
                       chunk_ready=(lambda k: pe.wait_ge(ln_in.s["lo"], k + 1)) if m == 0 else None)

            for m in range(4):
                linear(1, m, N_Q + m, h_hi, h_lo, META, HA)

            def values():
                for j in range(4):
                    split_ready(2, j)
                    for c in range(2):
                        k = 2 * j + c
                        m_h = whi[:, j % SPLIT, bass.ts(c, ATTN_W)]
                        m_l = wlo[:, j % SPLIT, bass.ts(c, ATTN_W)]
                        for t in range(5):
                            t0 = min(t * P, TAIL)
                            hi, lo = h_hi[:, k, t0:t0 + P], h_lo[:, k, t0:t0 + P]
                            pe.matmul(v_bank(t), hi, m_h, start=(k == 0), stop=False)
                            pe.matmul(v_bank(t), hi, m_l, start=False, stop=False)
                            last = pe.matmul(v_bank(t), lo, m_h, start=False, stop=(k == KC - 1))
                    last.then_inc(unit_done, 1)

            def linear_half(u, h):
                if u < U_GATE:
                    n, col, hw = N_U + u - U_U, 0, HT
                else:
                    n, col, hw = N_GATE + u - U_GATE, META, HA
                if h == 0:
                    split_ready(u // 4, u % 4)
                if u == U_U:
                    pe.wait_ge(v_ready, 5)
                pe.wait_ge(bank_free[h], n)
                c = slice(col + h * hw, col + (h + 1) * hw)
                for k in range(KC):
                    last = product(lin[:, h, 0:hw], u, k, h_hi[:, k, c], h_lo[:, k, c], k == 0, k == KC - 1)
                last.then_inc(half_done if h == 0 else unit_done, 1)

            def scores(i):
                if i == 0:
                    pe.wait_ge(bank_free[0], N_Q + 4)
                    pe.wait_ge(bank_free[1], N_Q + 4)
                    pe.wait_ge(kc_in, 16)
                    pe.wait_ge(made, 8)
                    pe.wait_ge(consts, 1)
                else:
                    pe.wait_ge(w_done, 2 * i)
                if i < 3:
                    for pos, b in enumerate(SAMPLE_BLOCKS[i]):
                        for p in range(PAIRS):
                            keys = k_t[:, p, TAIL:T] if b == 8 else kcache[:, p, bass.ts(b, P)]
                            last = pe.matmul(z[:, pos, bass.ts(p, P)], keys, q_t[:, 2 * p:2 * p + 2, SEQ:TA],
                                             start=(p == 0), stop=(b != 8), skip_group_check=True)
                        if b == 8:
                            last = pe.matmul(z[:, pos, :], ident[:, :],
                                             mask_new[:, :, :].rearrange("p h q -> p (h q)"),
                                             start=False, stop=True, skip_group_check=True)
                    last.then_inc(qk_done, 1)
                    return
                h = i - 3
                for b in range(5):
                    k0 = min(b * P, TAIL)
                    for dst, at, w in bank_pieces(OFF[b], QW[b]):
                        pe.matmul(zf[:, dst:dst + w], k_t[:, h // 2, k0:k0 + P],
                                  q_t[:, h, QS[b] + at:QS[b] + at + w],
                                  start=(dst % BANK == 0), stop=True, skip_group_check=True)
                for b in range(5):
                    mask = mask_diag[:, META:P] if b == 0 else mask_diag[:, :] if b < 4 else mask_tail[:, :]
                    for dst, at, w in bank_pieces(OFF[b], mask.shape[-1]):
                        last = pe.matmul(zf[:, dst:dst + w], ident[:, :], mask[:, at:at + w],
                                         start=False, stop=True, skip_group_check=True)
                last.then_inc(qk_done, 1)

            def subtract(dst, stationary, src, n):
                for d, at, w in bank_pieces(dst, n):
                    for part in (sp_hi, sp_lo):
                        last = pe.matmul(zf[:, d:d + w], stationary[:, :], part[:, src + at:src + at + w],
                                         start=False, stop=True, skip_group_check=True)
                return last

            def suffix_sums(i):
                pe.wait_ge(splo_done, 2 * i + 2)
                if i < 3:
                    if i:
                        pe.wait_ge(later_done, (2, 5)[i - 1])
                    for pos in range(3):
                        last = subtract(pos * BANK, tri_r, pos * BANK, BANK)
                        for before in range(pos):
                            last = subtract(pos * BANK, neg1_r, before * BANK, BANK)
                        if i:
                            last = pe.matmul(z[:, pos, :], neg1[:, :], later[:, i - 1, :],
                                             start=False, stop=True, skip_group_check=True)
                else:
                    for b in range(5):
                        last = subtract(OFF[b], tri_r, OFF[b], QW[b])
                        for c in range(b + 1, 5):
                            last = subtract(OFF[b] + QS[c] - QS[b], neg1_r, OFF[c], QW[c])
                last.then_inc(tri_done, 1)

            def weighted_values(i):
                pe.wait_ge(w_done, 2 * i + 1)
                if i < 3:
                    if i == 0:
                        pe.wait_ge(vc_in, 16)
                    for pos, b in enumerate(SAMPLE_BLOCKS[i]):
                        if pos == 1:
                            pe.wait_ge(w_done, 2 * i + 2)
                        for p in range(PAIRS):
                            vals = v_t[:, 4, bass.ts(p, P)] if b == 8 else vcache[:, b, bass.ts(p, P)]
                            last = pe.matmul(small[:, bass.ts(p, P)], vals,
                                             sa[:, pos * BANK + p * P:pos * BANK + (p + 1) * P],
                                             start=(b == 8 and p == 0), stop=(b == 0), skip_group_check=True)
                else:
                    h = i - 3
                    if h >= 2:
                        pe.wait_ge(attn_lo_done, 2 + h - 1)
                    for b in range(5):
                        if b == 1:
                            pe.wait_ge(w_done, 2 * i + 2)
                        last = pe.matmul(xo[:, h % 2, QS[b]:SEQ], v_t[:, b, bass.ts(h // 2, P)],
                                         sa[:, OFF[b]:OFF[b] + QW[b]],
                                         start=(b == 0), stop=(b == 4), skip_group_check=True)
                last.then_inc(pv_done, 1)

            def pool_group(s):
                pe.wait_ge(pooled, 1)
                pe.wait_ge(wpool_in, 16)
                pe.wait_ge(attn_lo_done, 2)
                if s:
                    pe.wait_ge(pool_scaled, s)
                if s < 4:
                    pe.matmul(small[:, :], wpool[:, s, :], u_t[:, s, META:UP], start=True, stop=True)\
                        .then_inc(pool_mm, 1)
                else:
                    for g in range(4):
                        last = pe.matmul(small[:, bass.ts(g, DEC)], wpool[:, g, :], u_t[:, g, UP + STATE:UT],
                                         start=(g == 0), stop=True, skip_group_check=True)
                    last.then_inc(pool_mm, 1)

            def branch_pool(m, h):
                if h == 0:
                    split_ready(U_BR // 4 + m // 4, m % 4)
                pe.wait_ge(bank_free[h], N_BR + m)
                for k in range(4):
                    product(lin[:, h, 0:HA], m, k, pool_hi[:, k, h * HA:(h + 1) * HA],
                            pool_lo[:, k, h * HA:(h + 1) * HA], k == 0, k == 3)

            def branch_attn(m, h):
                for k in range(4):
                    if m == 0 and h == 0 and k == 3:
                        pe.wait_ge(attn_lo_done, 2 + HEADS)
                    last = product(xo[:, h, 0:HA], m, 4 + k, attn_hi[:, k, h * HA:(h + 1) * HA],
                                   attn_lo[:, k, h * HA:(h + 1) * HA], k == 0, k == 3)
                last.then_inc(half_done if h == 0 else unit_done, 1)

            for i in range(ITEMS):
                scores(i)
                if i == 0:
                    values()
                for u, h in BEFORE[i]:
                    linear_half(u, h)
                if i == ITEMS - 2:
                    pool_group(3)
                suffix_sums(i)
                for u, h in AFTER[i]:
                    linear_half(u, h)
                if i == ITEMS - 1:
                    pe.wait_ge(pool_lo_done, 2)
                    branch_pool(0, 0)
                    branch_pool(0, 1)
                weighted_values(i)
                if ITEMS - 5 <= i <= ITEMS - 3:
                    pool_group(i - (ITEMS - 5))
                if i == ITEMS - 2:
                    pool_group(4)
            pe.wait_ge(attn_lo_done, 2 + HEADS - 1)
            branch_attn(0, 0)
            branch_attn(0, 1)
            for m in range(1, 8):
                for h in range(2):
                    branch_pool(m, h)
                    branch_attn(m, h)

            for m in range(8):
                linear(U_OUT // 4 + m // 4, m % 4, N_OUT + m, mix_hi, mix_lo, 0, HA,
                       chunk_ready=(lambda k: pe.wait_ge(mix_lo_done, 2 * k + 2)) if m == 0 else None)
                if m == 1:
                    pe.wait_ge(ln1.s["row"], 1)
                    norm_shift(ln1)
            norm_sums(ln1)

            for s in range(2):
                if s == 0:
                    linear(U_MLP1[0] // 4, 0, N_MLP1[0], h_hi, h_lo, META, HA,
                           chunk_ready=lambda k: pe.wait_ge(ln1.s["lo"], k + 1))
                    for j in range(1, 4):
                        linear(U_MLP1[0] // 4, j, N_MLP1[0] + j, h_hi, h_lo, META, HA)
                with pe.Fori(1 - s, FH // 4) as it:
                    for j in range(4):
                        linear(U_MLP1[s] // 4 + it, j, N_MLP1[s] + 4 * it + j, h_hi, h_lo, META, HA)

                def mlp2(it):
                    for j in range(4):
                        pe.wait_ge(f_lo_done, 2 * FH * s + FH * (j % 2 + 1))
                        linear(U_MLP2[s] // 4 + it, j, N_MLP2[s] + 2 * it + j // 2, f_hi, f_lo, 0, HA,
                               chunk0=KC * (j % 2), part=(j % 2 == 0, j % 2 == 1))
                if s == 0:
                    with pe.Fori(0, 4) as it:
                        mlp2(it)
                else:
                    mlp2(0)
                    pe.wait_ge(ln2.s["row"], 1)
                    norm_shift(ln2)
                    with pe.Fori(1, 4) as it:
                        mlp2(it)
            norm_sums(ln2)

        @block.scalar
        def _(act):
            def apart():
                act.wait_ge(consts, 1)

            def split(q4, j):
                act.wait_ge(unit_in[j], 16 * (q4 + 1))
                if not (isinstance(q4, int) and 4 * q4 + j < SPLIT):
                    act.wait_ge(unit_done, 4 * q4 + j - 1)
                nc.scalar.activation(whi[:, j % SPLIT, :], raw[:, j, :], ACT.Copy).then_inc(hi_split, 1)

            def split_next(q4, j):
                split(q4 + (j + 1) // 4, (j + 1) % 4)

            def use_tables(table_set):
                act.add_instruction(mybir.InstLoadActFuncSet(
                    name=nc.get_next_instruction_name(), act_func_set_id=table_set, engine=act.engine))

            def square_chunk(ln, k, par):
                act.wait_ge(ln.s["d"], k + 1)
                if not isinstance(k, int):
                    act.wait_ge(ln.s["sumsq"], k)
                elif k >= 2:
                    act.wait_ge(ln.s["sumsq"], k - 1)
                nc.scalar.activation(ln.sq[:, par, :], ln.d[:, par, :], ACT.Square).then_inc(ln.s["sq"], 1)

            def root(ln):
                act.wait_ge(ln.s["var"], 1)
                nc.scalar.activation(ln.rstd[:, 0, :], ln.sumsq[:, 0, :], ACT.Sqrt).then_inc(ln.s["std"], 1)

            def affine(ln, k):
                act.wait_ge(ln.s["scaled"], k + 1)
                out = ln.r[:, k, :] if ln is ln2 else h_hi[:, k, ln.col:T]
                nc.scalar.activation(out, ln.r[:, k, :], ACT.Identity, bias=vec(ln.b + k),
                                     scale=vec(ln.g + k)).then_inc(ln.s["hi"], 1)

            act.dma_start(vecs[:, :], vecs_d).then_inc(vecs_in, 16)
            act.dma_start(wpool[:, :, :], wpool_d).then_inc(wpool_in, 16)

            act.wait_ge(made, 4)
            nc.scalar.activation(tri_r[:, :], tri[:, :], ACT.Copy)
            nc.scalar.activation(neg1_r[:, :], neg1[:, :], ACT.Copy).then_inc(consts, 1)
            for k in range(KC):
                square_chunk(ln_in, k, k % 2)
            split(0, 0)
            root(ln_in)
            act.wait_ge(vecs_in, 16)
            for k in range(KC):
                affine(ln_in, k)

            for m in range(4):
                split_next(0, m)
                act.wait_ge(half_done, N_K + m + 1)
                nc.scalar.activation(k_t[:, m, 0:HT], lin[:, 0, 0:HT], ACT.Identity,
                                     bias=vec(V_BIN + C_K + m)).then_inc(bank_free[0], 1)
            act.wait_ge(bq8_done, 1)
            act.wait_ge(q_zero, 1)
            for m in range(4):
                split_next(1, m)
                act.wait_ge(half_done, N_Q + m + 1)
                for e in range(2):
                    rows = slice(64 * e, 64 * e + 64)
                    last = nc.scalar.activation(q_t[rows, 2 * m + e, 0:HA], lin[rows, 0, 0:HA], ACT.Identity,
                                                bias=bq8[rows, m:m + 1], scale=SB_SCALE)
                last.then_inc(bank_free[0], 1)

            use_tables(EXP_AND_LN)

            def softplus_tail(i):
                act.wait_ge(qk_done, i + 1)
                n = (ZS if i < 3 else ZP) // 2
                pieces = [slice(c * n, (c + 1) * n) for c in range(2)]
                for c in range(2):
                    nc.scalar.activation(sa[:, pieces[c]], zf[:, pieces[c]], ACT.Abs).then_inc(abs_done, 1)
                for c in range(2):
                    act.wait_ge(abs_done, 2 * i + c + 1)
                    nc.scalar.activation(sa[:, pieces[c]], sa[:, pieces[c]], ACT.Exp, scale=-1.0)\
                        .then_inc(expn_done, 1)
                for c in range(2):
                    act.wait_ge(expn_done, 2 * i + c + 1)
                    nc.scalar.activation(sa[:, pieces[c]], sa[:, pieces[c]], ACT.Ln, bias=1.0)\
                        .then_inc(ln_done, 1)

            def softplus_hi(i):
                n = (ZS if i < 3 else ZP) // 2
                for c in range(2):
                    act.wait_ge(sp_done, 2 * i + c + 1)
                    nc.scalar.activation(sp_hi[:, c * n:(c + 1) * n], sa[:, c * n:(c + 1) * n], ACT.Copy)\
                        .then_inc(sphi_done, 1)

            def weights(i):
                act.wait_ge(tri_done, i + 1)
                if i < 2:
                    act.wait_ge(later_done, (2, 5)[i])
                n = ZS if i < 3 else ZP
                for a, b in ((0, BANK), (BANK, n)):
                    nc.scalar.activation(sa[:, a:b], zf[:, a:b], ACT.Exp).then_inc(w_done, 1)

            def head_out_hi(i):
                if i < 2:
                    return
                act.wait_ge(pv_done, i + 1)
                if i == 2:
                    for e in range(2):
                        rows = slice(64 * e, 64 * e + 64)
                        src = small[rows, :].rearrange("p (c n) -> p c n", c=PAIRS)[:, :, 64 * e:64 * e + 64]
                        nc.scalar.activation(attn_hi[rows, :, SEQ:TA], src, ACT.Copy).then_inc(attn_hi_done, 1)
                else:
                    h = i - 3
                    rows = slice(64 * (h % 2), 64 * (h % 2) + 64)
                    nc.scalar.activation(attn_hi[rows, h // 2, 0:SEQ], xo[rows, h % 2, :], ACT.Copy)\
                        .then_inc(attn_hi_done, 1)

            def after_half(u, h):
                if h:
                    split((u + 2) // 4, (u + 2) % 4)
                elif u < U_GATE:
                    m = u - U_U
                    act.wait_ge(half_done, N_U + m + 1)
                    nc.scalar.activation(u_t[:, m, 0:HT], lin[:, 0, 0:HT], ACT.Identity,
                                         bias=vec(V_BIN + C_U + m)).then_inc(bank_free[0], 1)
                else:
                    m = u - U_GATE
                    act.wait_ge(half_done, N_GATE + m + 1)
                    nc.scalar.activation(gates[:, m // KC, m % KC, 0:HA], lin[:, 0, 0:HA], ACT.Identity,
                                         bias=vec(V_BIN + C_GATE + m)).then_inc(bank_free[0], 1)

            split(2, 1)
            for i in range(ITEMS):
                softplus_tail(i)
                if i == 0:
                    split(2, 2)
                for u, h in BEFORE[i][:1]:
                    after_half(u, h)
                softplus_hi(i)
                for u, h in BEFORE[i][1:]:
                    after_half(u, h)
                if i == 0:
                    split(2, 3)
                    split(3, 0)
                    split(3, 1)
                if i == ITEMS - 1:
                    act.wait_ge(pool_scaled, 5)
                    act.wait_ge(k_stored, 16)
                    nc.scalar.activation(pool_hi[:, :, 0:SEQ], u_t[:, :, META:UP], ACT.Copy)\
                        .then_inc(pool_hi_done, 1)
                    nc.scalar.activation(pool_hi[:, :, SEQ:TA], u_t[:, :, UP + STATE:UT], ACT.Copy)\
                        .then_inc(pool_hi_done, 1)
                weights(i)
                for u, h in AFTER[i]:
                    after_half(u, h)
                head_out_hi(i)
            act.wait_ge(v_stored, 32)

            use_tables(SIGMOIDS)
            for m in range(8):
                for g in range(2):
                    nc.scalar.activation(gates[:, g, m, :], gates[:, g, m, :], ACT.Sigmoid).then_inc(sig_done, 1)
                if m:
                    split_next(U_BR // 4 + m // 4, m % 4)
                for h in range(2):
                    act.wait_ge(br_summed, 2 * m + h + 1)
                    nc.scalar.activation(mix_hi[:, m, h * HA:(h + 1) * HA], br_a[:, h, :], ACT.Copy)\
                        .then_inc(mix_hi_done, 1)

            for m in range(8):
                split_next(U_OUT // 4 + m // 4, m % 4)
                act.wait_ge(half_done, N_OUT + m + 1)
                nc.scalar.activation(ln1.r[:, m, 0:HA], lin[:, 0, 0:HA], ACT.Identity,
                                     bias=vec(V_BOUT + m)).then_inc(bank_free[0], 1)
                act.wait_ge(unit_done, U_OUT + m + 1)
                nc.scalar.activation(ln1.r[:, m, HA:TA], lin[:, 1, 0:HA], ACT.Identity,
                                     bias=vec(V_BOUT + m)).then_inc(bank_free[1], 1)
                if m >= 2:
                    square_chunk(ln1, m - 2, m % 2)
            square_chunk(ln1, 6, 0)
            square_chunk(ln1, 7, 1)
            root(ln1)
            for k in range(KC):
                affine(ln1, k)

            def hidden(s, it):
                nc.scalar.activation(b1_now[:, :], vecs[:, bass.ds(V_B1 + FH * s + 4 * it, 4)], ACT.Copy)\
                    .then_inc(b1_loaded, 1)
                for j in range(4):
                    c = 4 * it + j
                    split_next(U_MLP1[s] // 4 + it, j)
                    if j == 0:
                        act.wait_ge(b1_loaded, FH // 4 * s + it + 1)
                    for h in range(2):
                        if h == 0:
                            if not (s == 0 and isinstance(c, int) and c == 0):
                                act.wait_ge(f_lo_done, 2 * (FH * s + c))
                            act.wait_ge(half_done, N_MLP1[s] + c + 1)
                        else:
                            act.wait_ge(unit_done, U_MLP1[s] + c + 1)
                        nc.scalar.activation(relu_t[:, h, :], lin[:, h, 0:HA], ACT.Relu,
                                             bias=b1_now[:, j:j + 1]).then_inc(bank_free[h], 1)
                        act.wait_ge(bank_free[h], N_MLP1[s] + c + 1)
                        apart()
                        nc.scalar.activation(f_hi[:, bass.ds(c, 1), h * HA:(h + 1) * HA], relu_t[:, h:h + 1, :],
                                             ACT.Square).then_inc(f_hi_done, 1)

            for s in range(2):
                if s == 0:
                    hidden(0, 0)
                with act.Fori(1 - s, FH // 4) as it:
                    hidden(s, it)
                if s == 0:
                    with act.Fori(0, 4) as it:
                        for j in range(4):
                            m = 2 * it + j // 2
                            split_next(U_MLP2[0] // 4 + it, j)
                            if j % 2:
                                act.wait_ge(half_done, N_MLP2[0] + m + 1)
                                apart()
                                nc.scalar.activation(ln2.r[:, bass.ds(m, 1), 0:HA], lin[:, 0:1, 0:HA],
                                                     ACT.Identity, bias=vec(V_B2 + m)).then_inc(bank_free[0], 1)
                                act.wait_ge(unit_done, U_MLP2[0] + 4 * it + j + 1)
                                apart()
                                nc.scalar.activation(ln2.r[:, bass.ds(m, 1), HA:TA], lin[:, 1:2, 0:HA],
                                                     ACT.Identity, bias=vec(V_B2 + m)).then_inc(bank_free[1], 1)
                else:
                    split_next(U_MLP2[1] // 4, 0)
                    split_next(U_MLP2[1] // 4, 1)
                    split_next(U_MLP2[1] // 4, 2)
                    split_next(U_MLP2[1] // 4, 3)
                    square_chunk(ln2, 0, 0)
                    with act.Fori(1, 3) as it:
                        for j in range(4):
                            split_next(U_MLP2[1] // 4 + it, j)
                            if j % 2 == 0:
                                square_chunk(ln2, 2 * it - 1 + j // 2, (1 + j // 2) % 2)
                    for j in range(3):
                        split_next(U_MLP2[1] // 4 + 3, j)
                        if j % 2 == 0:
                            square_chunk(ln2, 5 + j // 2, (1 + j // 2) % 2)
                    square_chunk(ln2, 7, 1)
            root(ln2)
            for k in range(KC):
                affine(ln2, k)

        @block.vector
        def _(dve):
            tt = nc.vector.tensor_tensor

            def split(q4, j):
                dve.wait_ge(hi_split, 4 * q4 + j + 1)
                tt(wlo[:, j % SPLIT, :], raw[:, j, :], whi[:, j % SPLIT, :].bitcast(F32), ALU.subtract)\
                    .then_inc(lo_split, 1)

            def split_next(q4, j):
                split(q4 + (j + 1) // 4, (j + 1) % 4)

            def norm_shift(ln):
                dve.wait_ge(ln.s["shift_mm"], 1)
                nc.vector.tensor_scalar(both(ln.shift[:, 0, :], ln.w), z[:, 0:2, 0:ln.hw], -1.0 / P, None,
                                        ALU.mult).then_inc(ln.s["shift"], 1)
                dve.wait_ge(ln.s["shift"], 1)

            def shifted(ln, k, par):
                if not isinstance(k, int):
                    dve.wait_ge(ln.s["sq"], k)
                    dve.wait_ge(ln.s["sum"], k)
                elif k >= 2:
                    dve.wait_ge(ln.s["sq"], k - 1)
                    dve.wait_ge(ln.s["mm"] if ln is ln_in else ln.s["sum"], k - 1)
                tt(ln.d[:, par:par + 1, :], ln.r[:, bass.ds(k, 1), :], ln.shift[:, 0:1, :], ALU.subtract)\
                    .then_inc(ln.s["d"], 1)

            def normalise(ln):
                s, n = ln.s, ln.w
                dve.wait_ge(s["sums_mm"], 1)
                ts = nc.vector.tensor_scalar
                ts(both(ln.sum[:, 0, :], n), xo[:, :, 0:ln.hw], -1.0 / D_MODEL, None, ALU.mult)\
                    .then_inc(s["step"], 1)
                dve.wait_ge(s["step"], 1)
                tt(ln.sq[:, 0, :], ln.sum[:, 0, :], ln.sum[:, 0, :], ALU.mult).then_inc(s["step"], 1)
                tt(ln.mean[:, 0, :], ln.sum[:, 0, :], ln.shift[:, 0, :], ALU.add).then_inc(s["step"], 1)
                dve.wait_ge(s["step"], 2)
                nc.vector.scalar_tensor_tensor(out=both(ln.sq[:, 1, :], n), in0=z[:, 0:2, 0:ln.hw],
                                               scalar=-1.0 / D_MODEL, in1=both(ln.sq[:, 0, :], n),
                                               op0=ALU.mult, op1=ALU.subtract).then_inc(s["step"], 1)
                dve.wait_ge(s["step"], 4)
                ts(ln.sumsq[:, 0, :], ln.sq[:, 1, :], 0.0, LN_EPS, ALU.max, ALU.add).then_inc(s["var"], 1)
                for k in range(KC):
                    tt(ln.r[:, k, :], ln.r[:, k, :], ln.mean[:, 0, :], ALU.subtract).then_inc(s["centred"], 1)
                dve.wait_ge(s["std"], 1)
                nc.vector.reciprocal(ln.rstd[:, 0, :], ln.rstd[:, 0, :]).then_inc(s["rstd"], 1)
                dve.wait_ge(s["rstd"], 1)
                dve.wait_ge(s["centred"], KC)
                for k in range(KC):
                    tt(ln.r[:, k, :], ln.r[:, k, :], ln.rstd[:, 0, :], ALU.mult).then_inc(s["scaled"], 1)
                    if ln is not ln2 and k:
                        norm_lo(ln, k - 1)
                if ln is not ln2:
                    norm_lo(ln, KC - 1)

            def norm_lo(ln, k):
                dve.wait_ge(ln.s["affine"], k + 1)
                dve.wait_ge(ln.s["hi"], k + 1)
                tt(h_lo[:, k, ln.col:T], ln.d[:, k % 2, :], h_hi[:, k, ln.col:T].bitcast(F32), ALU.subtract)\
                    .then_inc(ln.s["lo"], 1)

            dve.wait_ge(x_in[0], 16)
            norm_shift(ln_in)

            def add_squares(k):
                dve.wait_ge(ln_in.s["sq"], k + 1)
                if k == 0:
                    nc.vector.tensor_copy(ln_in.sumsq[:, 0, :], ln_in.sq[:, 0, :]).then_inc(ln_in.s["sumsq"], 1)
                else:
                    dve.wait_ge(ln_in.s["sumsq"], k)
                    tt(ln_in.sumsq[:, 0, :], ln_in.sumsq[:, 0, :], ln_in.sq[:, k % 2, :], ALU.add)\
                        .then_inc(ln_in.s["sumsq"], 1)

            for k in range(KC):
                dve.wait_ge(x_in[k], 16)
                shifted(ln_in, k, k % 2)
                if k:
                    add_squares(k - 1)
            add_squares(KC - 1)
            split(0, 0)
            normalise(ln_in)
            dve.wait_ge(vecs_in, 16)
            nc.vector.tensor_scalar(bq8[:, :], vecs[:, V_BIN + C_Q:V_BIN + C_Q + 4], SB_SCALE, None, ALU.mult)\
                .then_inc(bq8_done, 1)

            def add_bias(out, src, col, freed=None):
                op = nc.vector.tensor_scalar(out, src, vec(col), None, ALU.add)
                if freed is not None:
                    op.then_inc(freed, 1)

            for m in range(4):
                split_next(0, m)
                dve.wait_ge(unit_done, U_K + m + 1)
                add_bias(k_t[:, m, HT:T], lin[:, 1, 0:HT], V_BIN + C_K + m, bank_free[1])
            dve.wait_ge(q_zero, 1)
            for m in range(4):
                split_next(1, m)
                dve.wait_ge(unit_done, U_Q + m + 1)
                for e in range(2):
                    rows = slice(64 * e, 64 * e + 64)
                    last = nc.vector.tensor_scalar(q_t[rows, 2 * m + e, HA:TA], lin[rows, 1, 0:HA],
                                                   vecs[rows, V_BIN + C_Q + m:V_BIN + C_Q + m + 1], SB_SCALE,
                                                   ALU.add, ALU.mult)
                last.then_inc(bank_free[1], 1)

            def softplus(i):
                n = (ZS if i < 3 else ZP) // 2
                for c in range(2):
                    cols = slice(c * n, (c + 1) * n)
                    dve.wait_ge(ln_done, 2 * i + c + 1)
                    nc.vector.scalar_tensor_tensor(out=sa[:, cols], in0=zf[:, cols], scalar=0.0, in1=sa[:, cols],
                                                   op0=ALU.max, op1=ALU.add).then_inc(sp_done, 1)

            def add_later(i):
                if i > 1:
                    return
                dve.wait_ge(sp_done, 2 * i + 2)
                terms = [sa[:, pos * BANK:(pos + 1) * BANK] for pos in range(3)]
                if i == 1:
                    terms.insert(0, later[:, 0, :])
                acc, done = later[:, i, :], 2 * i
                tt(acc, terms[0], terms[1], ALU.add).then_inc(later_done, 1)
                for t in terms[2:]:
                    done += 1
                    dve.wait_ge(later_done, done)
                    tt(acc, acc, t, ALU.add).then_inc(later_done, 1)

            def softplus_lo(i):
                n = (ZS if i < 3 else ZP) // 2
                for c in range(2):
                    cols = slice(c * n, (c + 1) * n)
                    dve.wait_ge(sphi_done, 2 * i + c + 1)
                    tt(sp_lo[:, cols], sa[:, cols], sp_hi[:, cols].bitcast(F32), ALU.subtract)\
                        .then_inc(splo_done, 1)

            def head_out_lo(i):
                if i == 2:
                    for e in range(2):
                        rows = slice(64 * e, 64 * e + 64)
                        dve.wait_ge(attn_hi_done, e + 1)
                        src = small[rows, :].rearrange("p (c n) -> p c n", c=PAIRS)[:, :, 64 * e:64 * e + 64]
                        tt(attn_lo[rows, :, SEQ:TA], src, attn_hi[rows, :, SEQ:TA].bitcast(F32), ALU.subtract)\
                            .then_inc(attn_lo_done, 1)
                elif i > 2:
                    h = i - 3
                    rows = slice(64 * (h % 2), 64 * (h % 2) + 64)
                    dve.wait_ge(attn_hi_done, 2 + h + 1)
                    tt(attn_lo[rows, h // 2, 0:SEQ], xo[rows, h % 2, :], attn_hi[rows, h // 2, 0:SEQ].bitcast(F32),
                       ALU.subtract).then_inc(attn_lo_done, 1)

            def after_half(u, h):
                if h == 0:
                    return
                dve.wait_ge(unit_done, u + 1)
                if u < U_GATE:
                    m = u - U_U
                    add_bias(u_t[:, m, HT:UP], lin[:, 1, 0:UP - HT], V_BIN + C_U + m)
                    add_bias(u_t[:, m, UP + STATE:UT], lin[:, 1, UP - HT:HT], V_BIN + C_U + m, bank_free[1])
                else:
                    m = u - U_GATE
                    add_bias(gates[:, m // KC, m % KC, HA:TA], lin[:, 1, 0:HA], V_BIN + C_GATE + m, bank_free[1])
                split((u + 2) // 4, (u + 2) % 4)

            def pool_scale(s):
                dve.wait_ge(pool_mm, s + 1)
                if s < 4:
                    nc.vector.tensor_scalar(u_t[:, s, META:UP], small[:, :], vec(V_PSCALE + s), None, ALU.mult)\
                        .then_inc(pool_scaled, 1)
                else:
                    for g in range(4):
                        last = nc.vector.tensor_scalar(u_t[:, g, UP + STATE:UT], small[:, bass.ts(g, DEC)],
                                                       vec(V_PSCALE + g), None, ALU.mult)
                    last.then_inc(pool_scaled, 1)

            def values_out():
                dve.wait_ge(unit_done, U_V + 4)
                dve.wait_ge(bv_in, 16)
                for t in range(5):
                    tt(v_t[:, t, :], v_bank(t), bv[:, :], ALU.add).then_inc(v_ready, 1)

            def pool_lo_part(piece, cols, src):
                dve.wait_ge(pool_hi_done, piece + 1)
                tt(pool_lo[:, :, cols], src, pool_hi[:, :, cols].bitcast(F32), ALU.subtract)\
                    .then_inc(pool_lo_done, 1)

            split(2, 1)
            for i in range(ITEMS):
                softplus(i)
                if i == 0:
                    split(2, 2)
                softplus_lo(i)
                add_later(i)
                for u, h in BEFORE[i]:
                    after_half(u, h)
                if i == 0:
                    split(2, 3)
                    split(3, 0)
                    values_out()
                    split(3, 1)
                if i == ITEMS - 2:
                    pool_scale(3)
                if i == ITEMS - 1:
                    pool_lo_part(0, slice(0, SEQ), u_t[:, :, META:UP])
                    pool_lo_part(1, slice(SEQ, TA), u_t[:, :, UP + STATE:UT])
                for u, h in AFTER[i]:
                    after_half(u, h)
                head_out_lo(i)
                if ITEMS - 5 <= i <= ITEMS - 3:
                    pool_scale(i - (ITEMS - 5))
                if i == ITEMS - 2:
                    pool_scale(4)

            for m in range(8):
                if m:
                    split_next(U_BR // 4 + m // 4, m % 4)
                for h in range(2):
                    cols = slice(h * HA, (h + 1) * HA)
                    dve.wait_ge(half_done, N_BR + m + 1) if h == 0 else dve.wait_ge(unit_done, U_BR + m + 1)
                    dve.wait_ge(sig_done, 2 * m + 2)
                    tt(br_a[:, h, :], lin[:, h, 0:HA], gates[:, 0, m, cols], ALU.mult)
                    tt(br_b[:, h, :], xo[:, h, 0:HA], gates[:, 1, m, cols], ALU.mult).then_inc(bank_free[h], 1)
                    dve.wait_ge(bank_free[h], N_BR + m + 1)
                    tt(br_a[:, h, :], br_a[:, h, :], br_b[:, h, :], ALU.add).then_inc(br_summed, 1)
                for h in range(2):
                    cols = slice(h * HA, (h + 1) * HA)
                    dve.wait_ge(mix_hi_done, 2 * m + h + 1)
                    tt(mix_lo[:, m, cols], br_a[:, h, :], mix_hi[:, m, cols].bitcast(F32), ALU.subtract)\
                        .then_inc(mix_lo_done, 1)
                dve.wait_ge(mix_lo_done, 2 * m + 2)

            stt = nc.vector.scalar_tensor_tensor

            def add_residual(ln, m):
                for part, done in ((h_hi, ln.s["part"]), (h_lo, ln.s["row"])):
                    stt(out=ln.r[:, bass.ds(m, 1), :], in0=part[:, bass.ds(m, 1), META:T].bitcast(F32),
                        scalar=ALPHA, in1=ln.r[:, bass.ds(m, 1), :], op0=ALU.mult, op1=ALU.add).then_inc(done, 1)
                    dve.wait_ge(done, m + 1)

            for m in range(8):
                split_next(U_OUT // 4 + m // 4, m % 4)
                dve.wait_ge(bank_free[0], N_OUT + m + 1)
                dve.wait_ge(bank_free[1], N_OUT + m + 1)
                add_residual(ln1, m)
                if m == 2:
                    norm_shift(ln1)
                if m >= 2:
                    shifted(ln1, m - 2, m % 2)
            shifted(ln1, 6, 0)
            shifted(ln1, 7, 1)
            normalise(ln1)

            def hidden(s, it):
                for j in range(4):
                    c = 4 * it + j
                    split_next(U_MLP1[s] // 4 + it, j)
                    for h in range(2):
                        dve.wait_ge(bank_free[h], N_MLP1[s] + c + 1)
                        tt(relu_sq[:, h, :], relu_t[:, h, :], relu_t[:, h, :], ALU.mult).then_inc(f_sq_done, 1)
                        dve.wait_ge(f_sq_done, 2 * (FH * s + c) + h + 1)
                        dve.wait_ge(f_hi_done, 2 * (FH * s + c) + h + 1)
                        cols = slice(h * HA, (h + 1) * HA)
                        tt(f_lo[:, bass.ds(c, 1), cols], relu_sq[:, h:h + 1, :],
                           f_hi[:, bass.ds(c, 1), cols].bitcast(F32), ALU.subtract).then_inc(f_lo_done, 1)

            for s in range(2):
                if s == 0:
                    hidden(0, 0)
                with dve.Fori(1 - s, FH // 4) as it:
                    hidden(s, it)
                if s == 0:
                    with dve.Fori(0, 4) as it:
                        for j in range(4):
                            m = 2 * it + j // 2
                            split_next(U_MLP2[0] // 4 + it, j)
                            if j % 2:
                                dve.wait_ge(bank_free[0], N_MLP2[0] + m + 1)
                                dve.wait_ge(bank_free[1], N_MLP2[0] + m + 1)
                                stt(out=ln2.r[:, bass.ds(m, 1), :], in0=h_hi[:, bass.ds(m, 1), META:T].bitcast(F32),
                                    scalar=ALPHA, in1=ln2.r[:, bass.ds(m, 1), :], op0=ALU.mult, op1=ALU.add)\
                                    .then_inc(ln2.s["part"], 1)
                                dve.wait_ge(ln2.s["part"], 2 * m + 1)
                                stt(out=ln2.r[:, bass.ds(m, 1), :], in0=h_lo[:, bass.ds(m, 1), META:T].bitcast(F32),
                                    scalar=ALPHA, in1=ln2.r[:, bass.ds(m, 1), :], op0=ALU.mult, op1=ALU.add)\
                                    .then_inc(ln2.s["part"], 1)
                else:
                    dve.wait_ge(ln2.s["part"], 2 * KC)
                    U4 = U_MLP2[1] // 4

                    def pair(it, first=False, final=False):
                        for j in range(4):
                            m = 2 * it + j // 2
                            if not (final and j == 3):
                                split_next(U4 + it, j)
                            if j % 2:
                                for h in range(2):
                                    if h == 0:
                                        dve.wait_ge(half_done, N_MLP2[1] + m + 1)
                                    else:
                                        dve.wait_ge(unit_done, U_MLP2[1] + 4 * it + j + 1)
                                    cols = slice(h * HA, (h + 1) * HA)
                                    op = tt(ln2.r[:, bass.ds(m, 1), cols], lin[:, h:h + 1, 0:HA],
                                            ln2.r[:, bass.ds(m, 1), cols], ALU.add)
                                    op.then_inc(bank_free[h], 1)
                                if first and j == 1:
                                    dve.wait_ge(bank_free[1], N_MLP2[1] + 1)
                                    nc.vector.tensor_copy(ln2.d[:, 1, 0:1], ln2.r[:, 0, TA - 1:TA])\
                                        .then_inc(ln2.s["row"], 1)
                            elif first and j == 2:
                                pass
                            elif not first:
                                dve.wait_ge(bank_free[1], N_MLP2[1] + m)
                                shifted(ln2, m - 1, (j // 2 + 1) % 2)

                    pair(0, first=True)
                    norm_shift(ln2)
                    shifted(ln2, 0, 0)
                    with dve.Fori(1, 3) as it:
                        pair(it)
                    pair(3, final=True)
                    dve.wait_ge(bank_free[1], N_MLP2[1] + 8)
                    shifted(ln2, 7, 1)
            normalise(ln2)

        @block.gpsimd
        def _(pool):
            nc.gpsimd.memset(tri[:, :], -1.0).then_inc(made, 1)
            nc.gpsimd.memset(neg1[:, :], -1.0).then_inc(made, 1)
            nc.gpsimd.memset(ident[:, :], 0.0).then_inc(made, 1)
            pool.wait_ge(made, 3)
            nc.gpsimd.affine_select(out=tri[:, :], in_=tri[:, :], compare_op=ALU.is_ge, fill=0.0, base=0,
                                    pattern=[[-1, P]], channel_multiplier=1).then_inc(made, 1)
            nc.gpsimd.affine_select(out=ident[:, :], in_=ident[:, :], compare_op=ALU.not_equal, fill=1.0, base=0,
                                    pattern=[[-1, P]], channel_multiplier=1).then_inc(made, 1)
            nc.gpsimd.memset(mask_diag[:, :], 0.0)
            nc.gpsimd.memset(mask_tail[:, :], 0.0)
            nc.gpsimd.memset(mask_new[:, :, :], 0.0).then_inc(win_done, 1)
            pool.wait_ge(win_done, 1)
            nc.gpsimd.affine_select(out=mask_diag[:, :], in_=mask_diag[:, :], compare_op=ALU.is_ge, fill=NEG,
                                    base=-1, pattern=[[1, P]], channel_multiplier=-1).then_inc(made, 1)
            lead = UP - META - TAIL
            nc.gpsimd.affine_select(out=mask_tail[:, :], in_=mask_tail[:, :], compare_op=ALU.is_ge, fill=NEG,
                                    base=-lead, pattern=[[0, META]], channel_multiplier=1)
            nc.gpsimd.affine_select(out=mask_new[:, :, :], in_=mask_new[:, :, :], compare_op=ALU.is_ge, fill=NEG,
                                    base=-(P - DEC), pattern=[[0, HEADS], [0, DEC]], channel_multiplier=1)\
                .then_inc(win_done, 1)
            pool.wait_ge(win_done, 2)
            nc.gpsimd.affine_select(out=mask_tail[:, :], in_=mask_tail[:, :], compare_op=ALU.is_ge, fill=NEG,
                                    base=lead - 1, pattern=[[1, META]], channel_multiplier=-1).then_inc(made, 1)
            nc.gpsimd.affine_select(out=mask_new[:, :, :], in_=mask_new[:, :, :], compare_op=ALU.is_ge, fill=NEG,
                                    base=P - DEC - 1, pattern=[[0, HEADS], [1, DEC]], channel_multiplier=-1)\
                .then_inc(made, 1)
            nc.gpsimd.memset(q_t[:, :, :], 0.0).then_inc(q_zero, 1)

            def affine_chunks(ln):
                for k in range(KC):
                    pool.wait_ge(ln.s["scaled"], k + 1)
                    if k >= 2:
                        pool.wait_ge(ln.s["lo"], k - 1)
                    nc.gpsimd.tensor_scalar(ln.d[:, k % 2, :], ln.r[:, k, :], vec(ln.g + k), vec(ln.b + k),
                                            ALU.mult, ALU.add).then_inc(ln.s["affine"], 1)

            pool.wait_ge(vecs_in, 16)
            affine_chunks(ln_in)
            pool.dma_start(u_t[:, :, UP:UP + STATE], state_d).then_inc(state_in, 16)
            for h in range(2):
                pool.wait_ge(bank_free[h], N_K + 4)
            pool.dma_start(k_out, k_t[:, :, :]).then_inc(k_stored, 16)
            pool.wait_ge(v_ready, 5)
            pool.dma_start(v_out[0:4 * P, :].rearrange("(t p) d -> p t d", p=P), v_t[:, 0:4, :])\
                .then_inc(v_stored, 16)
            pool.dma_start(v_out[4 * P:T, :], v_t[4 * P - TAIL:P, 4, :]).then_inc(v_stored, 16)

            pool.wait_ge(state_in, 16)
            for h in range(2):
                pool.wait_ge(bank_free[h], N_U + 4)
            nc.gpsimd.tensor_copy(ust[:, :, 0:STATE], u_t[:, :, UP - STATE:UP])
            nc.gpsimd.tensor_copy(ust[:, :, STATE:2 * STATE], u_t[:, :, UT - STATE:UT]).then_inc(ust_done, 1)
            done = 2
            for g, w in enumerate(POOL_WINDOWS):
                src, reach = u_t[:, g, :], 1
                while reach < w:
                    dst = win[:, (reach.bit_length() - 1) % 2, 0:UT]
                    nc.gpsimd.tensor_tensor(dst[:, 2 * reach - 1:UT], src[:, 2 * reach - 1:UT],
                                            src[:, reach - 1:UT - reach], ALU.add).then_inc(win_done, 1)
                    done += 1
                    pool.wait_ge(win_done, done)
                    src, reach = dst, 2 * reach
                nc.gpsimd.tensor_scalar(src[:, META:UT], src[:, META:UT], 1.0 / w, 0.0, ALU.mult, ALU.add)\
                    .then_inc(win_done, 1)
                done += 1
                pool.wait_ge(win_done, done)
                if g == 0:
                    pool.wait_ge(ust_done, 1)
                last = nc.gpsimd.tensor_tensor(u_t[:, g, META:UT], src[:, META:UT], u_t[:, g, META:UT],
                                               ALU.subtract)
                if g < 3:
                    last.then_inc(win_done, 1)
                    done += 1
                    pool.wait_ge(win_done, done)
            last.then_inc(pooled, 1)
            pool.dma_start(s_out, ust[:, :, :]).then_inc(s_stored, 16)

            def add_chunk(ln, k, par):
                first = isinstance(k, int) and k == 0
                for t, acc, src in (("d", ln.sum, ln.d), ("sq", ln.sumsq, ln.sq)):
                    done = ln.s["sum"] if t == "d" else ln.s["sumsq"]
                    pool.wait_ge(ln.s[t], k + 1)
                    if first:
                        nc.gpsimd.tensor_copy(acc[:, 0, :], src[:, par, :]).then_inc(done, 1)
                    else:
                        pool.wait_ge(done, k)
                        nc.gpsimd.tensor_tensor(acc[:, 0, :], acc[:, 0, :], src[:, par, :], ALU.add)\
                            .then_inc(done, 1)

            for m in range(8):
                add_chunk(ln1, m, m % 2)
            affine_chunks(ln1)
            for m in range(8):
                add_chunk(ln2, m, m % 2)


def kernel(**inputs):
    import numpy as np
    import concourse.bacc as bacc
    from concourse.bass_utils import run_bass_kernel_spmd as run

    def units(w):
        n = w.shape[1] // P
        return w.reshape(w.shape[0] // P, P, n, P).transpose(2, 1, 0, 3).reshape(n, P, -1)

    a = {n: np.asarray(v) for n, v in inputs.items()}
    w_in = a["w_in"][0]
    w_u, w_q, w_k, w_v = (w_in[:, i * 512:(i + 1) * 512] for i in range(4))
    w2 = a["w_mlp2"][0].reshape(2, 2, KC, P, KC, P).transpose(0, 4, 1, 3, 2, 5).reshape(2, 2 * KC, P, UNIT)
    w1 = units(a["w_mlp1"][0])
    stream = np.concatenate([
        units(w_k), units(w_q), w_v.reshape(4, 2, P, ATTN_W).transpose(0, 2, 1, 3).reshape(4, P, UNIT), units(w_u),
        units(w_in[:, 2048:]),
        np.concatenate([units(a["w_br_pool"][0]), units(a["w_br_attn"][0])], axis=2),
        units(a["w_out"][0]), w1[:FH], w2[0], w1[FH:], w2[1]])
    cols = [a["b_in"][0], a["pool_scale"][0], a["b_out"][0], a["ln_in_g"], a["ln_in_b"], a["ln1_g"][0],
            a["ln1_b"][0], a["ln2_g"][0], a["ln2_b"][0], a["b_mlp1"][0], a["b_mlp2"][0]]
    arrays = {
        "x_t": np.concatenate([a["meta"], a["x_prompt"][0], a["x_sample"][0]]).T.reshape(KC, P, T),
        "w_stream": stream,
        "vecs": np.concatenate([c.reshape(-1, P) for c in cols]).T,
        "b_v": np.broadcast_to(a["b_in"][0][1536:2048], (P, ATTN_W)),
        "k_cache": a["cache_k"].reshape(PAST, PAIRS, P).transpose(2, 1, 0),
        "v_cache": a["cache_v"].reshape(PAST // P, P, ATTN_W).transpose(1, 0, 2),
        "pool_state": a["state_pool"].reshape(STATE, 4, P).transpose(2, 1, 0),
        "w_pool": a["w_pool_grp"][0].transpose(1, 0, 2),
    }
    arrays = {n: np.ascontiguousarray(v) for n, v in arrays.items()}
    nc = bacc.Bacc("TRN2", target_bir_lowering=False, num_devices=1)
    args = [nc.dram_tensor(n, v.shape, F32, kind="ExternalInput").ap() for n, v in arrays.items()]
    outs = {"y": (P, KC, TA), "k_new": (P, PAIRS, T), "v_new": (T, ATTN_W), "state_new": (P, 4, 2 * STATE)}
    args += [nc.dram_tensor(n, s, F32, kind="ExternalOutput").ap() for n, s in outs.items()]
    encoder_step(nc, *args)
    got = run(nc, [arrays], core_ids=[0]).results[0]
    y = got["y"].transpose(2, 1, 0).reshape(TA, D_MODEL)
    k = got["k_new"].transpose(2, 1, 0).reshape(T, HEADS, HD)
    v = got["v_new"].reshape(T, HEADS, HD)
    s = got["state_new"].transpose(2, 1, 0).reshape(2, STATE, POOL_W)
    return (y[None, :SEQ], y[None, SEQ:], k[None, None, :UP], v[None, None, :UP], s[None, None, 0],
            k[None, None, UP:], v[None, None, UP:], s[None, None, 1])
```

```python
from contextlib import ExitStack

import concourse.bass as bass
from concourse import mybir

F32 = mybir.dt.float32
F32R = mybir.dt.float32r
BF16 = mybir.dt.bfloat16
ALU = mybir.AluOpType
ACT = mybir.ActivationFunctionType

P = 128
D_MODEL, META, SEQ, DEC, PAST = 1024, 16, 512, 64, 1024
HEADS, HD = 8, 64
ATTN_W, POOL_W, D_FF = HEADS * HD, 512, 4096
POOL_WINDOWS = (2, 4, 8, 16)
STATE = max(POOL_WINDOWS) - 1
T = META + SEQ + DEC
TA = SEQ + DEC
HT, HA = T // 2, TA // 2
KC = D_MODEL // P
PAIRS = HEADS // 2
ALPHA = 2.0 ** 0.25
SB_SCALE = HD ** -0.5
LN_EPS = 1e-5
NEG = -1.0e30
BANK = 512
EXP_AND_LN, SIGMOIDS = 6, 2

UNIT = KC * P
U_K, U_Q, U_V, U_U, U_GATE, U_BR, U_OUT = 0, 4, 8, 12, 16, 32, 40
U_MLP1, U_MLP2 = (48, 80), (64, 96)
UNITS = 112
RAW, SPLIT = 4, 2
N_K, N_Q, N_U, N_GATE, N_BR, N_OUT = 0, 4, 8, 12, 28, 36
N_MLP1, N_MLP2 = (44, 68), (60, 84)
FH = D_FF // P // 2

V_BIN, V_PSCALE, V_BOUT = 0, 32, 36
V_LNIN_G, V_LNIN_B, V_LN1_G, V_LN1_B, V_LN2_G, V_LN2_B = 44, 52, 60, 68, 76, 84
V_B1, V_B2, V_COUNT = 92, 124, 132
C_U, C_Q, C_K, C_GATE = 0, 4, 8, 16

QS = [max(0, P * b - META) for b in range(5)]
QW = [SEQ - q for q in QS]
OFF = [sum(QW[:b]) for b in range(5)]
ZP = sum(QW)
ZS = 3 * BANK
SLOTS = 4
TAIL = T - P
SAMPLE_BLOCKS = [(8, 7, 6), (5, 4, 3), (2, 1, 0)]
ITEMS = 3 + HEADS


def pieces(i):
    return [(p * BANK, (p + 1) * BANK) for p in range(3)] if i < 3 else [(OFF[2], ZP), (0, OFF[2])]


def split_at(i, p):
    return (3 * i + p) % SLOTS * BANK if i < 3 else pieces(i)[p][0]


def pieces_before(i):
    return sum(len(pieces(j)) for j in range(i))


def adds(i, p):
    return 2 if i >= 3 or (i and p == 0) else 1 if p else 0


def adds_upto(i, p):
    return sum(adds(j, q) for j in range(i + 1) for q in range(len(pieces(j))) if (j, q) <= (i, p))


HALVES = [(u, h) for u in range(U_U, U_BR) for h in range(2)]
BEFORE = [[]] + [HALVES[4 * i - 2:4 * i + 1] for i in range(1, ITEMS - 1)] + [HALVES[-2:]]
AFTER = [HALVES[:2]] + [HALVES[4 * i + 1:4 * i + 2] for i in range(1, ITEMS - 1)] + [[]]
LAG = 4
SHIFT_AFTER = ((), (), (0,), (1, 2), (3, 4), (5,))
UP = META + SEQ
UT = UP + STATE + DEC


def bank_pieces(dst, n):
    at = 0
    while at < n:
        w = min(n - at, BANK - (dst + at) % BANK)
        yield dst + at, at, w
        at += w


def encoder_step(nc, x, wstream, vecs_d, bv_d, kc_d, vc_d, state_d, wpool_d, y_out, k_out, v_out, s_out):
    with ExitStack() as ctx:
        base = 16512

        def sb(name, shape, dt, at):
            return nc.alloc_sbuf_tensor_at(name, [P] + shape, dt, offset=base + 4 * at)

        def sem(name):
            return ctx.enter_context(nc.semaphore(name))

        raw = sb("raw", [RAW, UNIT], F32, 0)
        whi = sb("whi", [SPLIT, UNIT], F32R, 4096)
        wlo = sb("wlo", [SPLIT, UNIT], F32R, 6144)
        h_hi = sb("h_hi", [KC, T], F32R, 8192)
        h_lo = sb("h_lo", [KC, T], F32R, 12928)
        bv = sb("bv", [ATTN_W], F32, 17664)
        tri = sb("tri", [P], F32, 18176)
        below = sb("below", [P], F32, 18304)
        tri_r = sb("tri_r", [P], F32R, 18432)
        below_r = sb("below_r", [P], F32R, 18560)
        ident = sb("ident", [P], BF16, 18688)
        mask_diag = sb("mask_diag", [P], BF16, 18752)
        mask_tail = sb("mask_tail", [META], BF16, 18816)
        mask_new = sb("mask_new", [HEADS, DEC], BF16, 18824)
        vecs = sb("vecs", [V_COUNT], F32, 19080)
        bq8 = sb("bq8", [4], F32, 19216)
        b1_now = sb("b1_now", [4], F32, 19224)
        wpool = sb("wpool", [4, P], F32, 19232)
        A0 = 19744
        kcache = sb("kcache", [PAIRS, PAST], F32, A0)
        vcache = sb("vcache", [8, ATTN_W], F32, A0 + 4096)
        gates = sb("gates", [2, KC, TA], F32, A0)
        k_t = sb("k_t", [PAIRS, T], F32, A0 + 9216)
        q_t = sb("q_t", [HEADS, TA], F32, A0 + 11584)
        v_t = sb("v_t", [5, ATTN_W], F32, A0 + 16192)
        attn_hi = sb("attn_hi", [PAIRS, TA], F32R, A0 + 18752)
        attn_lo = sb("attn_lo", [PAIRS, TA], F32R, A0 + 21056)
        u_t = sb("u_t", [4, UT], F32, A0 + 23360)
        sa = sb("sa", [ZS], F32, A0 + 25848)
        sp_hi = sb("sp_hi", [SLOTS * BANK], F32R, A0 + 27384)
        sp_lo = sb("sp_lo", [SLOTS * BANK], F32R, A0 + 29432)
        win = sb("win", [2, 608], F32, A0 + 31480)
        ust = sb("ust", [4, 2 * STATE], F32, A0 + 32704)
        inv_d = sb("inv_d", [P], F32, A0 + 32832)
        pool_hi = sb("pool_hi", [4, TA], F32R, A0 + 9216)
        pool_lo = sb("pool_lo", [4, TA], F32R, A0 + 11520)
        mix_hi = sb("mix_hi", [KC, TA], F32R, A0 + 13824)
        mix_lo = sb("mix_lo", [KC, TA], F32R, A0 + 23360)
        br_a = sb("br_a", [2, HA], F32, A0 + 29000)
        br_b = sb("br_b", [2, HA], F32, A0 + 29576)
        f_hi = sb("f_hi", [FH, TA], F32R, A0 + 4608)
        f_lo = sb("f_lo", [FH, TA], F32R, A0 + 13824)
        relu_t = sb("relu_t", [2, HA], F32, A0 + 29000)
        relu_sq = sb("relu_sq", [2, HA], F32, A0 + 29576)

        z = ctx.enter_context(nc.psum_tensor("z", [P, 3, BANK], F32))
        xo = ctx.enter_context(nc.psum_tensor("xo", [P, 2, BANK], F32))
        lin = ctx.enter_context(nc.psum_tensor("lin", [P, 2, BANK], F32))
        small = ctx.enter_context(nc.psum_tensor("small", [P, BANK], F32))
        zf = z[:, :, :].rearrange("p b n -> p (b n)")

        vecs_in, bv_in, wpool_in = sem("vecs_in"), sem("bv_in"), sem("wpool_in")
        kc_in, vc_in, state_in = sem("kc_in"), sem("vc_in"), sem("state_in")
        x_in = [[sem(f"x_in{h}_{k}") for k in range(KC // 2)] for h in range(2)]
        unit_in = [sem(f"unit_in{s}") for s in range(RAW)]
        hi_split, lo_split = sem("hi_split"), sem("lo_split")
        half_done, unit_done = sem("half_done"), sem("unit_done")
        bank_free = [sem("bank_free0"), sem("bank_free1")]
        made, consts = sem("made"), sem("consts")
        q_zero, bq8_done = sem("q_zero"), sem("bq8_done")
        v_ready, k_stored, v_stored, s_stored, y_stored = (
            sem("v_ready"), sem("k_stored"), sem("v_stored"), sem("s_stored"), sem("y_stored"))
        qk_done, abs_done, expn_done, ln_done, sp_done = (
            sem("qk_done"), sem("abs_done"), sem("expn_done"), sem("ln_done"), sem("sp_done"))
        sphi_done, splo_done, run_done, tri_done, w_done, pv_done = (
            sem("sphi_done"), sem("splo_done"), sem("run_done"), sem("tri_done"), sem("w_done"), sem("pv_done"))
        attn_hi_done, attn_lo_done = sem("attn_hi_done"), sem("attn_lo_done")
        win_done, ust_done, pooled = sem("win_done"), sem("ust_done"), sem("pooled")
        pool_mm, pool_scaled, pool_hi_done, pool_lo_done = (
            sem("pool_mm"), sem("pool_scaled"), sem("pool_hi_done"), sem("pool_lo_done"))
        sig_done, br_summed, mix_hi_done, mix_lo_done = (
            sem("sig_done"), sem("br_summed"), sem("mix_hi_done"), sem("mix_lo_done"))
        shift1_done, pair_added, pair_sq_added = sem("shift1_done"), sem("pair_added"), sem("pair_sq_added")
        hi_added, prepared = sem("hi_added"), sem("prepared")
        b1_loaded, ln2_added = sem("b1_loaded"), sem("ln2_added")
        f_hi_done, f_sq_done, f_lo_done = sem("f_hi_done"), sem("f_sq_done"), sem("f_lo_done")

        class Norm:

            def __init__(self, name, width, r_at, tmp_at, g, b, col, direct, by_dve, sq_slots=2):
                self.w, self.hw, self.g, self.b, self.col = width, width // 2, g, b, col
                self.direct, self.by_dve = direct, by_dve
                self.r = sb(name + "_r", [KC, width], F32, A0 + r_at)
                t = [sb(f"{name}_{s}", [n, width], F32, A0 + tmp_at + o * width)
                     for s, n, o in (("shift", 1, 0), ("sum", 1, 1), ("sumsq", 1, 2), ("mean", 1, 3),
                                     ("var", 1, 4), ("rstd", 1, 5), ("sq", sq_slots, 6))]
                self.shift, self.sum, self.sumsq, self.mean, self.var, self.rstd, self.sq = t
                names = ["shift_mm", "shift", "half_sq", "terms", "msq", "mean", "var", "guess", "rstd", "centred_v",
                         "centred_g", "scaled", "hi"]
                if name != "ln_in":
                    names += ["res", "d", "sq", "sum", "sumsq"]
                if name != "ln2":
                    names += ["lo"]
                self.s = {s: sem(f"{name}_{s}") for s in names}
                self.half_d = [sem(f"{name}_half_d{h}") for h in range(2)] if name == "ln_in" else None
                last = KC - direct
                self.terms = last if direct else KC // 2
                self.per = {"half_sq": last, "terms": self.terms, "msq": 1, "mean": 1, "var": 2, "guess": 3, "rstd": 2,
                            "scaled": KC, "hi": KC, "lo": KC, "centred_v": by_dve[0], "centred_g": KC - by_dve[0]}

            def count(self, name, h, n):
                return self.s[name], h * self.per[name] + n

            def d_ready(self, h, i):
                if self is ln1:
                    return bank_free[i], N_OUT + 6 + h + 1
                if self is ln2:
                    return bank_free[h], N_MLP2[1] + 8
                return self.half_d[h], i + 1

            def cols(self, h):
                return slice(h * self.hw, (h + 1) * self.hw)

            def shift_bank(self, h):
                return z[:, 2, 0:self.hw] if h == 0 else small[:, 0:self.hw]

            def mean_bank(self, h):
                return z[:, h, 0:self.hw]

            def sq_bank(self, h):
                return xo[:, h, 0:self.hw]

        ln_in = Norm("ln_in", T, 18752, 23488, V_LNIN_G, V_LNIN_B, 0, 0, (3, 0), KC)
        pair_sum = (ln_in.sum, ln_in.sumsq, sb("pair_sum2", [1, T], F32, A0 + 23488 + 14 * T))
        ln1 = Norm("ln1", TA, 0, 4608, V_LN1_G, V_LN1_B, META, 6, (0, 0))
        ln2 = Norm("ln2", TA, 0, 23040, V_LN2_G, V_LN2_B, META, 7, (0, 0))
        block = ctx.enter_context(nc.Block())

        def vec(col):
            return vecs[:, bass.ds(col, 1)]

        def v_bank(t):
            return xo[:, t, :] if t < 2 else lin[:, t - 2, :] if t < 4 else small[:, :]

        @block.sync
        def _(sp):
            def load_unit(q4, j, first=False):
                if not first:
                    sp.wait_ge(lo_split, (q4 - 1) * RAW + j + 1)
                sp.dma_start(raw[:, j, :], wstream[q4 * RAW + j]).then_inc(unit_in[j], 16)

            for h in range(2):
                for k in range(KC // 2):
                    c = ln_in.cols(h)
                    sp.dma_start(ln_in.r[:, 2 * k:2 * k + 2, c], x[:, 2 * k:2 * k + 2, c]).then_inc(x_in[h][k], 16)
            for j in range(RAW):
                load_unit(0, j, first=True)
            sp.dma_start(bv[:, :], bv_d).then_inc(bv_in, 16)
            sp.dma_start(kcache[:, :, :], kc_d).then_inc(kc_in, 16)
            load_unit(1, 0)
            load_unit(1, 1)
            sp.dma_start(vcache[:, :, :], vc_d).then_inc(vc_in, 16)
            load_unit(1, 2)
            load_unit(1, 3)
            with sp.Fori(2, UNITS // RAW) as q4:
                for j in range(RAW):
                    load_unit(q4, j)
            for h in range(2):
                for k in range(KC):
                    c = ln2.cols(h)
                    sp.wait_ge(*ln2.count("hi", h, k + 1))
                    sp.dma_start(y_out[:, k, c], ln2.r[:, k, c]).then_inc(y_stored, 16)
            sp.wait_ge(y_stored, 2 * 16 * KC)
            sp.wait_ge(k_stored, 16)
            sp.wait_ge(v_stored, 32)
            sp.wait_ge(s_stored, 16)

        @block.tensor
        def _(pe):
            def split_ready(q4, j):
                pe.wait_ge(lo_split, 4 * q4 + j + 1)

            def product(out, j, k, hi, lo, first, last):
                w_h, w_l = whi[:, j % SPLIT, bass.ts(k, P)], wlo[:, j % SPLIT, bass.ts(k, P)]
                pe.matmul(out, w_h, hi, start=first, stop=False)
                pe.matmul(out, w_h, lo, start=False, stop=False)
                return pe.matmul(out, w_l, hi, start=False, stop=last)

            def linear(q4, j, n, hi, lo, col, hw, chunk0=0, chunk_ready=None, part=(True, True)):
                split_ready(q4, j)
                opens, closes = part

                def free(h):
                    if opens and not (isinstance(n, int) and n == 0):
                        pe.wait_ge(bank_free[h], n)

                def mm(h, k):
                    c = slice(col + h * hw, col + (h + 1) * hw)
                    return product(lin[:, h, 0:hw], j, k, hi[:, chunk0 + k, c], lo[:, chunk0 + k, c],
                                   opens and k == 0, closes and k == KC - 1)

                for h in range(2):
                    free(h)
                    for k in range(KC):
                        if chunk_ready is not None:
                            chunk_ready(k, h)
                        last = mm(h, k)
                    if h == 0 and closes:
                        last.then_inc(half_done, 1)
                last.then_inc(unit_done, 1)

            def linear_pair(u, n, hi, lo, col, hw, chunk_ready=None, between=None):
                def mm(e, h, k):
                    c = slice(col + h * hw, col + (h + 1) * hw)
                    return product(lin[:, e, 0:hw], u + e, k, hi[:, k, c], lo[:, k, c], k == 0, k == KC - 1)

                for h in range(2):
                    if chunk_ready is None:
                        steps = [(e, k) for e in range(2) for k in range(KC)]
                    else:
                        steps = [(0, k) for k in range(LAG)]
                        for k in range(LAG, KC):
                            steps += [(0, k), (1, k - LAG)]
                        steps += [(1, k) for k in range(KC - LAG, KC)]
                    for e, k in steps:
                        if k == 0:
                            if h == 0:
                                split_ready((u + e) // 4, (u + e) % 4)
                            if n + h:
                                pe.wait_ge(bank_free[e], n + h)
                        if chunk_ready is not None and e == 0:
                            chunk_ready(k, h)
                        last = mm(e, h, k)
                        if k == KC - 1:
                            last.then_inc(unit_done if h else half_done, 1)
                        if (h, e, k) == (1, 0, 2) and between is not None:
                            between()

            def norm_shift(ln, h):
                pe.matmul(ln.shift_bank(h), inv_d[:, :], ln.r[:, 0, ln.cols(h)], start=True, stop=True)\
                    .then_inc(ln.s["shift_mm"], 1)

            def norm_sums(ln, h):
                c = ln.cols(h)
                if ln.direct:
                    pe.wait_ge(ln.s["sum"], ln.direct - 1)
                    pe.matmul(ln.mean_bank(h), inv_d[:, :], ln.sum[:, 0, c], start=True, stop=False)
                    pe.wait_ge(ln.s["sumsq"], ln.direct - 1)
                    pe.matmul(ln.sq_bank(h), inv_d[:, :], ln.sumsq[:, 0, c], start=True, stop=False)
                for i, k in enumerate(range(ln.direct, KC)):
                    pe.wait_ge(*ln.d_ready(h, i))
                    pe.matmul(ln.mean_bank(h), inv_d[:, :], ln.r[:, k, c], start=(k == 0), stop=(k == KC - 1))
                    pe.wait_ge(*ln.count("half_sq", h, i + 1))
                    pe.matmul(ln.sq_bank(h), inv_d[:, :], ln.sq[:, k % 2, c], start=(k == 0), stop=(k == KC - 1))\
                        .then_inc(ln.s["terms"], 1)

            def pair_sums(h):
                c = ln_in.cols(h)
                for p in range(KC // 2):
                    if h == 0 and p == 1:
                        pe.wait_ge(x_in[1][0], 16)
                        norm_shift(ln_in, 1)
                    start, stop = p == 0, p == KC // 2 - 1
                    pe.wait_ge(pair_added, h * (KC // 2) + p + 1)
                    pe.matmul(ln_in.mean_bank(h), inv_d[:, :], pair_sum[p % 3][:, 0, c], start=start, stop=stop)
                    pe.wait_ge(pair_sq_added, h * (KC // 2) + p + 1)
                    pe.matmul(ln_in.sq_bank(h), inv_d[:, :], ln_in.sq[:, 2 * p, c], start=start, stop=stop)\
                        .then_inc(ln_in.s["terms"], 1)

            pe.wait_ge(made, 1)
            pe.wait_ge(x_in[0][0], 16)
            norm_shift(ln_in, 0)
            pair_sums(0)
            pair_sums(1)

            linear_pair(U_K, N_K, h_hi, h_lo, 0, HT,
                        chunk_ready=lambda k, h: pe.wait_ge(*ln_in.count("lo", h, k + 1)))
            for m in range(2, 4):
                linear(0, m, N_K + m, h_hi, h_lo, 0, HT)

            for m in range(4):
                linear(1, m, N_Q + m, h_hi, h_lo, META, HA)

            def values():
                for j in range(4):
                    split_ready(2, j)
                    for c in range(2):
                        k = 2 * j + c
                        m_h = whi[:, j % SPLIT, bass.ts(c, ATTN_W)]
                        m_l = wlo[:, j % SPLIT, bass.ts(c, ATTN_W)]
                        for t in range(5):
                            t0 = min(t * P, TAIL)
                            hi, lo = h_hi[:, k, t0:t0 + P], h_lo[:, k, t0:t0 + P]
                            pe.matmul(v_bank(t), hi, m_h, start=(k == 0), stop=False)
                            pe.matmul(v_bank(t), hi, m_l, start=False, stop=False)
                            last = pe.matmul(v_bank(t), lo, m_h, start=False, stop=(k == KC - 1))
                    last.then_inc(unit_done, 1)

            def linear_half(u, h):
                if u < U_GATE:
                    n, col, hw = N_U + u - U_U, 0, HT
                else:
                    n, col, hw = N_GATE + u - U_GATE, META, HA
                if h == 0:
                    split_ready(u // 4, u % 4)
                if u == U_U:
                    pe.wait_ge(v_ready, h + 1)
                pe.wait_ge(bank_free[h], n)
                c = slice(col + h * hw, col + (h + 1) * hw)
                for k in range(KC):
                    last = product(lin[:, h, 0:hw], u, k, h_hi[:, k, c], h_lo[:, k, c], k == 0, k == KC - 1)
                last.then_inc(half_done if h == 0 else unit_done, 1)

            def scores(i):
                if i == 0:
                    pe.wait_ge(kc_in, 16)
                    pe.wait_ge(made, 10)
                    pe.wait_ge(consts, 1)
                else:
                    pe.wait_ge(w_done, 2 * i)
                if i < 3:
                    for p in range(PAIRS):
                        if i == 0:
                            pe.wait_ge(bank_free[0], N_Q + p + 1)
                            pe.wait_ge(bank_free[1], N_Q + p + 1)
                        for pos, b in enumerate(SAMPLE_BLOCKS[i]):
                            keys = k_t[:, p, TAIL:T] if b == 8 else kcache[:, p, bass.ts(b, P)]
                            last = pe.matmul(z[:, pos, bass.ts(p, P)], keys, q_t[:, 2 * p:2 * p + 2, SEQ:TA],
                                             start=(p == 0), stop=(b != 8), skip_group_check=True)
                    if i == 0:
                        last = pe.matmul(z[:, 0, :], ident[:, :], mask_new[:, :, :].rearrange("p h q -> p (h q)"),
                                         start=False, stop=True, skip_group_check=True)
                    last.then_inc(qk_done, 1)
                    return
                h = i - 3
                for b in range(5):
                    k0 = min(b * P, TAIL)
                    for dst, at, w in bank_pieces(OFF[b], QW[b]):
                        pe.matmul(zf[:, dst:dst + w], k_t[:, h // 2, k0:k0 + P],
                                  q_t[:, h, QS[b] + at:QS[b] + at + w],
                                  start=(dst % BANK == 0), stop=True, skip_group_check=True)
                for b in range(5):
                    mask = mask_diag[:, META:P] if b == 0 else mask_diag[:, :] if b < 4 else mask_tail[:, :]
                    for dst, at, w in bank_pieces(OFF[b], mask.shape[-1]):
                        last = pe.matmul(zf[:, dst:dst + w], ident[:, :], mask[:, at:at + w],
                                         start=False, stop=True, skip_group_check=True)
                last.then_inc(qk_done, 1)

            def subtract(dst, stationary, src, n):
                for d, at, w in bank_pieces(dst, n):
                    for part in (sp_hi, sp_lo):
                        last = pe.matmul(zf[:, d:d + w], stationary[:, :], part[:, src + at:src + at + w],
                                         start=False, stop=True, skip_group_check=True)
                return last

            def suffix_sums(i):
                if i < 3:
                    for p in range(3):
                        pe.wait_ge(splo_done, pieces_before(i) + p + 1)
                        last = subtract(p * BANK, tri_r, split_at(i, p), BANK)
                        if i or p:
                            last = subtract(p * BANK, below_r, split_at(*((i, p - 1) if p else (i - 1, 2))), BANK)
                    last.then_inc(tri_done, 1)
                    return
                for b in range(4, -1, -1):
                    if b == 4:
                        pe.wait_ge(splo_done, pieces_before(i) + 1)
                    if b == 1:
                        pe.wait_ge(splo_done, pieces_before(i) + 2)
                    if b < 4:
                        last = subtract(OFF[b], tri_r, OFF[b], QW[b])
                    if b < 3:
                        last = subtract(OFF[b] + QS[b + 1] - QS[b], below_r, OFF[b + 1], QW[b + 1])
                    if b >= 3:
                        const = tri if b == 4 else below
                        dst = OFF[b] + QS[4] - QS[b]
                        pe.matmul(zf[:, dst:dst + QW[4]], const[:, :], sa[:, OFF[4]:ZP], start=False, stop=True,
                                  skip_group_check=True)
                last.then_inc(tri_done, 1)

            def weighted_values(i):
                pe.wait_ge(w_done, 2 * i + 1)
                if i < 3:
                    if i == 0:
                        pe.wait_ge(vc_in, 16)
                        pe.wait_ge(v_ready, 5)
                    for pos, b in enumerate(SAMPLE_BLOCKS[i]):
                        if pos == 1:
                            pe.wait_ge(w_done, 2 * i + 2)
                        for p in range(PAIRS):
                            vals = v_t[:, 4, bass.ts(p, P)] if b == 8 else vcache[:, b, bass.ts(p, P)]
                            last = pe.matmul(small[:, bass.ts(p, P)], vals,
                                             sa[:, pos * BANK + p * P:pos * BANK + (p + 1) * P],
                                             start=(b == 8 and p == 0), stop=(b == 0), skip_group_check=True)
                else:
                    h = i - 3
                    if h >= 2:
                        pe.wait_ge(attn_lo_done, 2 + h - 1)
                    for b in range(5):
                        if b == 1:
                            pe.wait_ge(w_done, 2 * i + 2)
                        last = pe.matmul(xo[:, h % 2, QS[b]:SEQ], v_t[:, b, bass.ts(h // 2, P)],
                                         sa[:, OFF[b]:OFF[b] + QW[b]],
                                         start=(b == 0), stop=(b == 4), skip_group_check=True)
                last.then_inc(pv_done, 1)

            def pool_group(s):
                pe.wait_ge(pooled, 1)
                pe.wait_ge(wpool_in, 16)
                pe.wait_ge(attn_lo_done, 2)
                if s:
                    pe.wait_ge(pool_scaled, s)
                if s < 4:
                    pe.matmul(small[:, :], wpool[:, s, :], u_t[:, s, META:UP], start=True, stop=True)\
                        .then_inc(pool_mm, 1)
                else:
                    for g in range(4):
                        last = pe.matmul(small[:, bass.ts(g, DEC)], wpool[:, g, :], u_t[:, g, UP + STATE:UT],
                                         start=(g == 0), stop=True, skip_group_check=True)
                    last.then_inc(pool_mm, 1)

            def branch_pool(m, h):
                if h == 0:
                    split_ready(U_BR // 4 + m // 4, m % 4)
                pe.wait_ge(bank_free[h], N_BR + m)
                for k in range(4):
                    product(lin[:, h, 0:HA], m, k, pool_hi[:, k, h * HA:(h + 1) * HA],
                            pool_lo[:, k, h * HA:(h + 1) * HA], k == 0, k == 3)

            def branch_attn(m, h):
                for k in range(4):
                    if m == 0 and h == 0 and k == 3:
                        pe.wait_ge(attn_lo_done, 2 + HEADS)
                    last = product(xo[:, h, 0:HA], m, 4 + k, attn_hi[:, k, h * HA:(h + 1) * HA],
                                   attn_lo[:, k, h * HA:(h + 1) * HA], k == 0, k == 3)
                last.then_inc(half_done if h == 0 else unit_done, 1)

            for i in range(ITEMS):
                scores(i)
                if i == 0:
                    values()
                for u, h in BEFORE[i]:
                    linear_half(u, h)
                if i == ITEMS - 2:
                    pool_group(3)
                suffix_sums(i)
                for u, h in AFTER[i]:
                    linear_half(u, h)
                weighted_values(i)
                if ITEMS - 5 <= i <= ITEMS - 3:
                    pool_group(i - (ITEMS - 5))
                if i == ITEMS - 2:
                    pool_group(4)
            pe.wait_ge(pool_lo_done, 2)
            branch_pool(0, 0)
            branch_pool(0, 1)
            pe.wait_ge(attn_lo_done, 2 + HEADS - 1)
            branch_attn(0, 0)
            branch_attn(0, 1)
            for m in range(1, 8):
                for h in range(2):
                    branch_pool(m, h)
                    branch_attn(m, h)

            for m in range(6):
                linear(U_OUT // 4 + m // 4, m % 4, N_OUT + m, mix_hi, mix_lo, 0, HA,
                       chunk_ready=(lambda k, h: pe.wait_ge(mix_lo_done, 2 * k + h + 1)) if m == 0 else None)
                if m == 1:
                    pe.wait_ge(ln1.s["res"], 1)
                    norm_shift(ln1, 0)
                    norm_shift(ln1, 1)
            linear_pair(U_OUT + 6, N_OUT + 6, mix_hi, mix_lo, 0, HA, between=lambda: norm_sums(ln1, 0))
            norm_sums(ln1, 1)

            for s in range(2):
                if s == 0:
                    linear_pair(U_MLP1[0], N_MLP1[0], h_hi, h_lo, META, HA,
                                chunk_ready=lambda k, h: pe.wait_ge(*ln1.count("lo", h, k + 1)))
                    for j in range(2, 4):
                        linear(U_MLP1[0] // 4, j, N_MLP1[0] + j, h_hi, h_lo, META, HA)
                with pe.Fori(1 - s, FH // 4) as it:
                    for j in range(4):
                        linear(U_MLP1[s] // 4 + it, j, N_MLP1[s] + 4 * it + j, h_hi, h_lo, META, HA)

                def mlp2(it, units=4):
                    for j in range(units):
                        pe.wait_ge(f_lo_done, 2 * FH * s + FH * (j % 2 + 1))
                        linear(U_MLP2[s] // 4 + it, j, N_MLP2[s] + 2 * it + j // 2, f_hi, f_lo, 0, HA,
                               chunk0=KC * (j % 2), part=(j % 2 == 0, j % 2 == 1))
                if s == 0:
                    with pe.Fori(0, 4) as it:
                        mlp2(it)
                else:
                    mlp2(0)
                    pe.wait_ge(ln2.s["res"], 1)
                    norm_shift(ln2, 0)
                    norm_shift(ln2, 1)
                    with pe.Fori(1, 3) as it:
                        mlp2(it)
                    mlp2(3, 2)
                    for h in range(2):
                        for j in (2, 3):
                            if h == 0:
                                split_ready(U_MLP2[1] // 4 + 3, j)
                            if j == 2:
                                pe.wait_ge(bank_free[h], N_MLP2[1] + 7)
                            for k in range(KC):
                                c = slice(h * HA, (h + 1) * HA)
                                last = product(lin[:, h, 0:HA], j, k, f_hi[:, KC * (j - 2) + k, c],
                                               f_lo[:, KC * (j - 2) + k, c], j == 2 and k == 0,
                                               j == 3 and k == KC - 1)
                                if (h, j, k) == (1, 2, 2):
                                    norm_sums(ln2, 0)
                            if h:
                                last.then_inc(unit_done, 1)
                            elif j == 3:
                                last.then_inc(half_done, 1)
            norm_sums(ln2, 1)

        @block.scalar
        def _(act):
            def apart():
                act.wait_ge(consts, 1)

            def split(q4, j):
                act.wait_ge(unit_in[j], 16 * (q4 + 1))
                if not (isinstance(q4, int) and 4 * q4 + j < SPLIT):
                    act.wait_ge(unit_done, 4 * q4 + j - 1)
                nc.scalar.activation(whi[:, j % SPLIT, :], raw[:, j, :], ACT.Copy).then_inc(hi_split, 1)

            def split_next(q4, j):
                split(q4 + (j + 1) // 4, (j + 1) % 4)

            def use_tables(table_set):
                act.add_instruction(mybir.InstLoadActFuncSet(
                    name=nc.get_next_instruction_name(), act_func_set_id=table_set, engine=act.engine))

            def square_chunk(ln, k, par):
                act.wait_ge(ln.s["d"], k + 1)
                if not isinstance(k, int):
                    act.wait_ge(ln.s["sumsq"], k - 1)
                elif k >= 2:
                    act.wait_ge(ln.s["sumsq"], max(k - 2, 1))
                nc.scalar.activation(ln.sq[:, par, :], ln.r[:, bass.ds(k, 1), :], ACT.Square)\
                    .then_inc(ln.s["sq"], 1)

            def square_half(ln, k, h):
                i = k - ln.direct
                act.wait_ge(*ln.d_ready(h, i))
                slot = k if ln is ln_in else k % 2
                if ln is not ln_in:
                    act.wait_ge(ln.s["sumsq"], k - 2)
                nc.scalar.activation(ln.sq[:, slot, ln.cols(h)], ln.r[:, k, ln.cols(h)], ACT.Square)\
                    .then_inc(ln.s["half_sq"], 1)

            def mean_out(ln, h):
                act.wait_ge(*ln.count("terms", h, ln.terms))
                nc.scalar.activation(ln.var[:, 0, ln.cols(h)], ln.mean_bank(h), ACT.Square)\
                    .then_inc(ln.s["msq"], 1)
                nc.scalar.activation(ln.mean[:, 0, ln.cols(h)], ln.mean_bank(h), ACT.Copy)\
                    .then_inc(ln.s["mean"], 1)

            def root(ln, h):
                c = ln.cols(h)
                rstd = ln.rstd[:, 0, c]
                act.wait_ge(*ln.count("var", h, 2))
                nc.scalar.activation(rstd, ln.var[:, 0, c], ACT.Ln).then_inc(ln.s["guess"], 1)
                act.wait_ge(*ln.count("guess", h, 1))
                nc.scalar.activation(rstd, rstd, ACT.Exp, scale=-0.5).then_inc(ln.s["guess"], 1)
                act.wait_ge(*ln.count("guess", h, 2))
                nc.scalar.activation(ln.sumsq[:, 0, c], rstd, ACT.Square).then_inc(ln.s["guess"], 1)

            def norm_hi(ln, k, h):
                act.wait_ge(*ln.count("scaled", h, k + 1))
                c = ln.cols(h)
                out = ln.r[:, k, c] if ln is ln2 else h_hi[:, k, ln.col + c.start:ln.col + c.stop]
                nc.scalar.activation(out, ln.r[:, k, c], ACT.Identity, bias=vec(ln.b + k))\
                    .then_inc(ln.s["hi"], 1)

            act.dma_start(vecs[:, :], vecs_d).then_inc(vecs_in, 16)
            act.dma_start(wpool[:, :, :], wpool_d).then_inc(wpool_in, 16)

            use_tables(EXP_AND_LN)
            for k in range(KC):
                square_half(ln_in, k, 0)
                if k == 5:
                    act.wait_ge(ln_in.s["shift_mm"], 2)
                    nc.scalar.activation(ln_in.shift[:, 0, ln_in.cols(1)], ln_in.shift_bank(1), ACT.Copy,
                                         scale=D_MODEL / P).then_inc(shift1_done, 1)
            for k in range(4):
                square_half(ln_in, k, 1)
            mean_out(ln_in, 0)
            root(ln_in, 0)
            for k in range(4, KC):
                square_half(ln_in, k, 1)
            split(0, 0)
            split(0, 1)
            act.wait_ge(vecs_in, 16)
            for k in range(KC):
                norm_hi(ln_in, k, 0)
                if k == 3:
                    mean_out(ln_in, 1)
                if k == 5:
                    root(ln_in, 1)

            def key_out(m, c, bank):
                nc.scalar.activation(k_t[:, m, c], lin[:, bank, 0:HT], ACT.Identity,
                                     bias=vec(V_BIN + C_K + m)).then_inc(bank_free[bank], 1)

            for k in range(KC):
                norm_hi(ln_in, k, 1)
                if k == 1:
                    act.wait_ge(half_done, N_K + 1)
                    key_out(0, slice(0, HT), 0)
                if k == 4:
                    act.wait_ge(half_done, N_K + 2)
                    key_out(1, slice(0, HT), 1)
            split(0, 2)
            key_out(0, slice(HT, T), 0)
            split(0, 3)
            for m in range(2, 4):
                if m == 3:
                    split_next(0, m)
                act.wait_ge(half_done, N_K + m + 1)
                key_out(m, slice(0, HT), 0)
            act.wait_ge(bq8_done, 1)
            act.wait_ge(q_zero, 1)
            for m in range(4):
                split_next(1, m)
                act.wait_ge(half_done, N_Q + m + 1)
                for e in range(2):
                    rows = slice(64 * e, 64 * e + 64)
                    last = nc.scalar.activation(q_t[rows, 2 * m + e, 0:HA], lin[rows, 0, 0:HA], ACT.Identity,
                                                bias=bq8[rows, m:m + 1], scale=SB_SCALE)
                last.then_inc(bank_free[0], 1)
            act.wait_ge(made, 6)
            nc.scalar.activation(tri_r[:, :], tri[:, :], ACT.Copy)
            nc.scalar.activation(below_r[:, :], below[:, :], ACT.Copy).then_inc(consts, 1)

            def softplus_tail(i):
                act.wait_ge(qk_done, i + 1)
                n = pieces_before(i)
                for a, b in pieces(i):
                    nc.scalar.activation(sa[:, a:b], zf[:, a:b], ACT.Abs).then_inc(abs_done, 1)
                for p, (a, b) in enumerate(pieces(i)):
                    act.wait_ge(abs_done, n + p + 1)
                    nc.scalar.activation(sa[:, a:b], sa[:, a:b], ACT.Exp, scale=-1.0).then_inc(expn_done, 1)
                for p, (a, b) in enumerate(pieces(i)):
                    act.wait_ge(expn_done, n + p + 1)
                    nc.scalar.activation(sa[:, a:b], sa[:, a:b], ACT.Ln, bias=1.0).then_inc(ln_done, 1)

            def pool_output_hi():
                act.wait_ge(pool_scaled, 5)
                act.wait_ge(k_stored, 16)
                nc.scalar.activation(pool_hi[:, :, 0:SEQ], u_t[:, :, META:UP], ACT.Copy).then_inc(pool_hi_done, 1)
                nc.scalar.activation(pool_hi[:, :, SEQ:TA], u_t[:, :, UP + STATE:UT], ACT.Copy)\
                    .then_inc(pool_hi_done, 1)

            def sums_hi(i):
                for p, (a, b) in enumerate(pieces(i)):
                    if i == ITEMS - 1 and p == 1:
                        pool_output_hi()
                    if adds(i, p):
                        act.wait_ge(run_done, adds_upto(i, p))
                    else:
                        act.wait_ge(sp_done, pieces_before(i) + p + 1)
                    at = split_at(i, p)
                    nc.scalar.activation(sp_hi[:, at:at + b - a], sa[:, a:b], ACT.Copy).then_inc(sphi_done, 1)

            def weights(i):
                act.wait_ge(tri_done, i + 1)
                n = ZS if i < 3 else ZP
                for a, b in ((0, BANK), (BANK, n)):
                    nc.scalar.activation(sa[:, a:b], zf[:, a:b], ACT.Exp).then_inc(w_done, 1)

            def head_out_hi(i):
                if i < 2:
                    return
                act.wait_ge(pv_done, i + 1)
                if i == 2:
                    for e in range(2):
                        rows = slice(64 * e, 64 * e + 64)
                        src = small[rows, :].rearrange("p (c n) -> p c n", c=PAIRS)[:, :, 64 * e:64 * e + 64]
                        nc.scalar.activation(attn_hi[rows, :, SEQ:TA], src, ACT.Copy).then_inc(attn_hi_done, 1)
                else:
                    h = i - 3
                    rows = slice(64 * (h % 2), 64 * (h % 2) + 64)
                    nc.scalar.activation(attn_hi[rows, h // 2, 0:SEQ], xo[rows, h % 2, :], ACT.Copy)\
                        .then_inc(attn_hi_done, 1)

            def after_half(u, h):
                if h:
                    split((u + 2) // 4, (u + 2) % 4)
                elif u < U_GATE:
                    m = u - U_U
                    act.wait_ge(half_done, N_U + m + 1)
                    nc.scalar.activation(u_t[:, m, 0:HT], lin[:, 0, 0:HT], ACT.Identity,
                                         bias=vec(V_BIN + C_U + m)).then_inc(bank_free[0], 1)
                else:
                    m = u - U_GATE
                    act.wait_ge(half_done, N_GATE + m + 1)
                    nc.scalar.activation(gates[:, m // KC, m % KC, 0:HA], lin[:, 0, 0:HA], ACT.Identity,
                                         bias=vec(V_BIN + C_GATE + m)).then_inc(bank_free[0], 1)

            split(2, 1)
            for i in range(ITEMS):
                softplus_tail(i)
                if i == 0:
                    split(2, 2)
                for u, h in BEFORE[i][:1]:
                    after_half(u, h)
                sums_hi(i)
                for u, h in BEFORE[i][1:]:
                    after_half(u, h)
                if i == 0:
                    split(2, 3)
                    split(3, 0)
                    split(3, 1)
                weights(i)
                for u, h in AFTER[i]:
                    after_half(u, h)
                head_out_hi(i)
            act.wait_ge(v_stored, 32)

            use_tables(SIGMOIDS)

            def gate(m):
                for g in range(2):
                    nc.scalar.activation(gates[:, g, m, :], gates[:, g, m, :], ACT.Sigmoid).then_inc(sig_done, 1)

            gate(0)
            for m in range(8):
                if m:
                    split_next(U_BR // 4 + m // 4, m % 4)
                for h in range(2):
                    act.wait_ge(br_summed, 2 * m + h + 1)
                    nc.scalar.activation(mix_hi[:, m, h * HA:(h + 1) * HA], br_a[:, h, :], ACT.Copy)\
                        .then_inc(mix_hi_done, 1)
                    if h == 0 and m < 7:
                        gate(m + 1)

            use_tables(EXP_AND_LN)

            def out_half(m, h, bank):
                nc.scalar.activation(ln1.r[:, m, ln1.cols(h)], lin[:, bank, 0:HA], ACT.Identity,
                                     bias=vec(V_BOUT + m)).then_inc(bank_free[bank], 1)

            for m in range(6):
                split_next(U_OUT // 4 + m // 4, m % 4)
                act.wait_ge(half_done, N_OUT + m + 1)
                out_half(m, 0, 0)
                for k in SHIFT_AFTER[m - 1] if m else ():
                    square_chunk(ln1, k, k % 2)
                act.wait_ge(unit_done, U_OUT + m + 1)
                out_half(m, 1, 1)
            split(U_OUT // 4 + 1, 3)
            square_chunk(ln1, 5, 1)
            square_half(ln1, 6, 0)
            square_half(ln1, 7, 0)
            mean_out(ln1, 0)
            root(ln1, 0)
            split(U_MLP1[0] // 4, 0)
            square_half(ln1, 6, 1)
            for k in range(KC):
                norm_hi(ln1, k, 0)
                if k == 1:
                    square_half(ln1, 7, 1)
                    split(U_MLP1[0] // 4, 1)
                if k == 4:
                    mean_out(ln1, 1)
                if k == 5:
                    root(ln1, 1)

            def load_b1(col):
                nc.scalar.activation(b1_now[:, :], vecs[:, bass.ds(col, 4)], ACT.Copy).then_inc(b1_loaded, 1)

            def hidden_tile(e, h):
                if h:
                    act.wait_ge(f_lo_done, e + 1)
                    act.wait_ge(unit_done, U_MLP1[0] + e + 1)
                else:
                    act.wait_ge(half_done, N_MLP1[0] + e + 1)
                nc.scalar.activation(relu_t[:, e, :], lin[:, e, 0:HA], ACT.Relu,
                                     bias=b1_now[:, e:e + 1]).then_inc(bank_free[e], 1)
                act.wait_ge(bank_free[e], N_MLP1[0] + h + 1)
                nc.scalar.activation(f_hi[:, e, h * HA:(h + 1) * HA], relu_t[:, e, :],
                                     ACT.Square).then_inc(f_hi_done, 1)

            load_b1(V_B1)
            act.wait_ge(b1_loaded, 1)
            for k in range(KC):
                norm_hi(ln1, k, 1)
                if k == 1:
                    hidden_tile(0, 0)
                if k == 4:
                    hidden_tile(1, 0)
            split(U_MLP1[0] // 4, 2)
            hidden_tile(0, 1)
            hidden_tile(1, 1)

            def hidden(s, it):
                first = isinstance(it, int)
                if not first:
                    load_b1(V_B1 + FH * s + 4 * it)
                    act.wait_ge(b1_loaded, FH // 4 * s + it + 1)
                for j in range(2 if first else 0, 4):
                    c = 4 * it + j
                    split_next(U_MLP1[s] // 4 + it, j)
                    for h in range(2):
                        if h == 0:
                            act.wait_ge(f_lo_done, 2 * (FH * s + c))
                            act.wait_ge(half_done, N_MLP1[s] + c + 1)
                        else:
                            act.wait_ge(unit_done, U_MLP1[s] + c + 1)
                        nc.scalar.activation(relu_t[:, h, :], lin[:, h, 0:HA], ACT.Relu,
                                             bias=b1_now[:, j:j + 1]).then_inc(bank_free[h], 1)
                        act.wait_ge(bank_free[h], N_MLP1[s] + c + 1)
                        apart()
                        nc.scalar.activation(f_hi[:, bass.ds(c, 1), h * HA:(h + 1) * HA], relu_t[:, h:h + 1, :],
                                             ACT.Square).then_inc(f_hi_done, 1)

            for s in range(2):
                if s == 0:
                    hidden(0, 0)
                with act.Fori(1 - s, FH // 4) as it:
                    hidden(s, it)
                if s == 0:
                    with act.Fori(0, 4) as it:
                        for j in range(4):
                            m = 2 * it + j // 2
                            split_next(U_MLP2[0] // 4 + it, j)
                            if j % 2:
                                act.wait_ge(half_done, N_MLP2[0] + m + 1)
                                apart()
                                nc.scalar.activation(ln2.r[:, bass.ds(m, 1), 0:HA], lin[:, 0:1, 0:HA],
                                                     ACT.Identity, bias=vec(V_B2 + m)).then_inc(bank_free[0], 1)
                                act.wait_ge(unit_done, U_MLP2[0] + 4 * it + j + 1)
                                apart()
                                nc.scalar.activation(ln2.r[:, bass.ds(m, 1), HA:TA], lin[:, 1:2, 0:HA],
                                                     ACT.Identity, bias=vec(V_B2 + m)).then_inc(bank_free[1], 1)
                else:
                    split_next(U_MLP2[1] // 4, 0)
                    split_next(U_MLP2[1] // 4, 1)
                    split_next(U_MLP2[1] // 4, 2)
                    split_next(U_MLP2[1] // 4, 3)
                    square_chunk(ln2, 0, 0)
                    with act.Fori(1, 3) as it:
                        for j in range(4):
                            split_next(U_MLP2[1] // 4 + it, j)
                            if j % 2 == 0:
                                square_chunk(ln2, 2 * it - 1 + j // 2, (1 + j // 2) % 2)
                    for j in range(3):
                        split_next(U_MLP2[1] // 4 + 3, j)
                        if j % 2 == 0:
                            square_chunk(ln2, 5 + j // 2, (1 + j // 2) % 2)
            square_half(ln2, 7, 0)
            mean_out(ln2, 0)
            root(ln2, 0)
            for k in range(KC):
                norm_hi(ln2, k, 0)
                if k == 3:
                    square_half(ln2, 7, 1)
                if k == 5:
                    mean_out(ln2, 1)
                if k == 6:
                    root(ln2, 1)
            for k in range(KC):
                norm_hi(ln2, k, 1)

        @block.vector
        def _(dve):
            tt = nc.vector.tensor_tensor
            stt = nc.vector.scalar_tensor_tensor

            def split(q4, j):
                dve.wait_ge(hi_split, 4 * q4 + j + 1)
                tt(wlo[:, j % SPLIT, :], raw[:, j, :], whi[:, j % SPLIT, :].bitcast(F32), ALU.subtract)\
                    .then_inc(lo_split, 1)

            def split_next(q4, j):
                split(q4 + (j + 1) // 4, (j + 1) % 4)

            def norm_shift(ln, h):
                dve.wait_ge(ln.s["shift_mm"], h + 1)
                nc.vector.tensor_scalar(ln.shift[:, 0, ln.cols(h)], ln.shift_bank(h), D_MODEL / P, None,
                                        ALU.mult).then_inc(ln.s["shift"], 1)

            def shifted(ln, k):
                tt(ln.r[:, bass.ds(k, 1), :], ln.r[:, bass.ds(k, 1), :], ln.shift[:, 0:1, :], ALU.subtract)\
                    .then_inc(ln.s["d"], 1)

            def shifted_half(ln, k, h):
                c = ln.cols(h)
                tt(ln.r[:, k, c], ln.r[:, k, c], ln.shift[:, 0, c], ALU.subtract).then_inc(ln.half_d[h], 1)

            def variance(ln, h):
                c = ln.cols(h)
                dve.wait_ge(*ln.count("msq", h, 1))
                nc.vector.scalar_tensor_tensor(out=ln.var[:, 0, c], in0=ln.sq_bank(h), scalar=LN_EPS,
                                               in1=ln.var[:, 0, c], op0=ALU.add, op1=ALU.subtract)\
                    .then_inc(ln.s["var"], 1)
                dve.wait_ge(*ln.count("var", h, 1))
                nc.vector.tensor_scalar(ln.var[:, 0, c], ln.var[:, 0, c], LN_EPS, None, ALU.max)\
                    .then_inc(ln.s["var"], 1)

            def centre(ln, h):
                c = ln.cols(h)
                if ln.by_dve[h]:
                    dve.wait_ge(*ln.count("mean", h, 1))
                for k in range(ln.by_dve[h]):
                    tt(ln.r[:, k, c], ln.r[:, k, c], ln.mean[:, 0, c], ALU.subtract)\
                        .then_inc(ln.s["centred_v"], 1)

            def inverse(ln, h):
                c = ln.cols(h)
                dve.wait_ge(*ln.count("guess", h, 3))
                stt(out=ln.sumsq[:, 0, c], in0=ln.var[:, 0, c], scalar=-0.5, in1=ln.sumsq[:, 0, c],
                    op0=ALU.mult, op1=ALU.mult).then_inc(ln.s["rstd"], 1)
                dve.wait_ge(*ln.count("rstd", h, 1))
                stt(out=ln.rstd[:, 0, c], in0=ln.sumsq[:, 0, c], scalar=1.5, in1=ln.rstd[:, 0, c],
                    op0=ALU.add, op1=ALU.mult).then_inc(ln.s["rstd"], 1)
                dve.wait_ge(*ln.count("rstd", h, 2))

            def norm_scale(ln, k, h):
                c, n = ln.cols(h), ln.by_dve[h]
                if k < n:
                    dve.wait_ge(*ln.count("centred_v", h, k + 1))
                else:
                    dve.wait_ge(*ln.count("centred_g", h, k - n + 1))
                stt(out=ln.r[:, k, c], in0=ln.r[:, k, c], scalar=vec(ln.g + k), in1=ln.rstd[:, 0, c],
                    op0=ALU.mult, op1=ALU.mult).then_inc(ln.s["scaled"], 1)

            def norm_lo(ln, k, h):
                c = ln.cols(h)
                cc = slice(ln.col + c.start, ln.col + c.stop)
                dve.wait_ge(*ln.count("hi", h, k + 1))
                stt(out=h_lo[:, k, cc], in0=ln.r[:, k, c], scalar=vec(ln.b + k), in1=h_hi[:, k, cc].bitcast(F32),
                    op0=ALU.add, op1=ALU.subtract).then_inc(ln.s["lo"], 1)

            def scale_half(ln, h, between=None):
                for k in range(KC):
                    norm_scale(ln, k, h)
                    if ln is not ln2 and k:
                        norm_lo(ln, k - 1, h)
                    if between is not None:
                        between(k)
                if ln is not ln2:
                    norm_lo(ln, KC - 1, h)

            def add_pair(p, h):
                c = ln_in.cols(h)
                dve.wait_ge(ln_in.half_d[h], 2 * p + 2)
                if p == 3:
                    dve.wait_ge(*ln_in.count("terms", h, 1))
                tt(pair_sum[p % 3][:, 0, c], ln_in.r[:, 2 * p, c], ln_in.r[:, 2 * p + 1, c], ALU.add)\
                    .then_inc(pair_added, 1)

            def add_pair_sq(p, h):
                c, slot = ln_in.cols(h), 2 * p
                dve.wait_ge(*ln_in.count("half_sq", h, 2 * p + 2))
                tt(ln_in.sq[:, slot, c], ln_in.sq[:, slot, c], ln_in.sq[:, slot + 1, c], ALU.add)\
                    .then_inc(pair_sq_added, 1)

            norm_shift(ln_in, 0)
            dve.wait_ge(ln_in.s["shift"], 1)
            for p in range(KC // 2):
                dve.wait_ge(x_in[0][p], 16)
                shifted_half(ln_in, 2 * p, 0)
                shifted_half(ln_in, 2 * p + 1, 0)
                if p:
                    add_pair_sq(p - 1, 0)
                add_pair(p, 0)
            add_pair_sq(3, 0)
            for p in range(2):
                add_pair(p, 1)
                add_pair_sq(p, 1)
            variance(ln_in, 0)
            centre(ln_in, 0)
            inverse(ln_in, 0)
            for p in range(2, 4):
                add_pair(p, 1)
                add_pair_sq(p, 1)
            split(0, 0)
            dve.wait_ge(vecs_in, 16)

            def between_in(k):
                if k == 5:
                    variance(ln_in, 1)
                if k == 6:
                    inverse(ln_in, 1)

            scale_half(ln_in, 0, between_in)
            scale_half(ln_in, 1)
            nc.vector.tensor_scalar(bq8[:, :], vecs[:, V_BIN + C_Q:V_BIN + C_Q + 4], SB_SCALE, None, ALU.mult)\
                .then_inc(bq8_done, 1)

            def add_bias(out, src, col, freed=None):
                op = nc.vector.tensor_scalar(out, src, vec(col), None, ALU.add)
                if freed is not None:
                    op.then_inc(freed, 1)

            split(0, 2)
            dve.wait_ge(unit_done, U_K + 2)
            add_bias(k_t[:, 1, HT:T], lin[:, 1, 0:HT], V_BIN + C_K + 1, bank_free[1])
            split(0, 3)
            for m in range(2, 4):
                if m == 3:
                    split_next(0, m)
                dve.wait_ge(unit_done, U_K + m + 1)
                add_bias(k_t[:, m, HT:T], lin[:, 1, 0:HT], V_BIN + C_K + m, bank_free[1])
            dve.wait_ge(q_zero, 1)
            for m in range(4):
                split_next(1, m)
                dve.wait_ge(unit_done, U_Q + m + 1)
                for e in range(2):
                    rows = slice(64 * e, 64 * e + 64)
                    last = nc.vector.tensor_scalar(q_t[rows, 2 * m + e, HA:TA], lin[rows, 1, 0:HA],
                                                   vecs[rows, V_BIN + C_Q + m:V_BIN + C_Q + m + 1], SB_SCALE,
                                                   ALU.add, ALU.mult)
                last.then_inc(bank_free[1], 1)

            def softplus(i):
                n = pieces_before(i)

                def add(cols, term, first):
                    nonlocal run
                    if run:
                        dve.wait_ge(run_done, run)
                    if first:
                        dve.wait_ge(sp_done, n + p + 1)
                    run += 1
                    tt(sa[:, cols], sa[:, cols], term, ALU.add).then_inc(run_done, 1)

                for p, (a, b) in enumerate(pieces(i)):
                    dve.wait_ge(ln_done, n + p + 1)
                    nc.vector.scalar_tensor_tensor(out=sa[:, a:b], in0=zf[:, a:b], scalar=0.0, in1=sa[:, a:b],
                                                   op0=ALU.max, op1=ALU.add).then_inc(sp_done, 1)
                    run = adds_upto(i, p) - adds(i, p)
                    if i >= 3:
                        for j, later in enumerate((4, 3) if p == 0 else (2, 1)):
                            end = OFF[later]
                            add(slice(end - QW[later], end), sa[:, end:end + QW[later]], j == 0)
                    elif p:
                        add(slice(a, b), sa[:, a - BANK:a], True)
                    elif i:
                        prev = split_at(i - 1, 2)
                        add(slice(a, b), sp_hi[:, prev:prev + BANK].bitcast(F32), True)
                        add(slice(a, b), sp_lo[:, prev:prev + BANK].bitcast(F32), False)

            def sums_lo(i):
                for p, (a, b) in enumerate(pieces(i)):
                    dve.wait_ge(sphi_done, pieces_before(i) + p + 1)
                    at = split_at(i, p)
                    tt(sp_lo[:, at:at + b - a], sa[:, a:b], sp_hi[:, at:at + b - a].bitcast(F32), ALU.subtract)\
                        .then_inc(splo_done, 1)

            def head_out_lo(i):
                if i == 2:
                    for e in range(2):
                        rows = slice(64 * e, 64 * e + 64)
                        dve.wait_ge(attn_hi_done, e + 1)
                        src = small[rows, :].rearrange("p (c n) -> p c n", c=PAIRS)[:, :, 64 * e:64 * e + 64]
                        tt(attn_lo[rows, :, SEQ:TA], src, attn_hi[rows, :, SEQ:TA].bitcast(F32), ALU.subtract)\
                            .then_inc(attn_lo_done, 1)
                elif i > 2:
                    h = i - 3
                    rows = slice(64 * (h % 2), 64 * (h % 2) + 64)
                    dve.wait_ge(attn_hi_done, 2 + h + 1)
                    tt(attn_lo[rows, h // 2, 0:SEQ], xo[rows, h % 2, :], attn_hi[rows, h // 2, 0:SEQ].bitcast(F32),
                       ALU.subtract).then_inc(attn_lo_done, 1)

            def after_half(u, h):
                if h == 0:
                    return
                dve.wait_ge(unit_done, u + 1)
                if u < U_GATE:
                    m = u - U_U
                    add_bias(u_t[:, m, HT:UP], lin[:, 1, 0:UP - HT], V_BIN + C_U + m)
                    add_bias(u_t[:, m, UP + STATE:UT], lin[:, 1, UP - HT:HT], V_BIN + C_U + m, bank_free[1])
                else:
                    m = u - U_GATE
                    add_bias(gates[:, m // KC, m % KC, HA:TA], lin[:, 1, 0:HA], V_BIN + C_GATE + m, bank_free[1])
                split((u + 2) // 4, (u + 2) % 4)

            def pool_scale(s):
                dve.wait_ge(pool_mm, s + 1)
                if s < 4:
                    nc.vector.tensor_scalar(u_t[:, s, META:UP], small[:, :], vec(V_PSCALE + s), None, ALU.mult)\
                        .then_inc(pool_scaled, 1)
                else:
                    for g in range(4):
                        last = nc.vector.tensor_scalar(u_t[:, g, UP + STATE:UT], small[:, bass.ts(g, DEC)],
                                                       vec(V_PSCALE + g), None, ALU.mult)
                    last.then_inc(pool_scaled, 1)

            def values_out():
                dve.wait_ge(unit_done, U_V + 4)
                dve.wait_ge(bv_in, 16)
                for t in (2, 3, 4, 0, 1):
                    tt(v_t[:, t, :], v_bank(t), bv[:, :], ALU.add).then_inc(v_ready, 1)

            def pool_lo_part(piece, cols, src):
                dve.wait_ge(pool_hi_done, piece + 1)
                tt(pool_lo[:, :, cols], src, pool_hi[:, :, cols].bitcast(F32), ALU.subtract)\
                    .then_inc(pool_lo_done, 1)

            split(2, 1)
            for i in range(ITEMS):
                softplus(i)
                if i == 0:
                    split(2, 2)
                sums_lo(i)
                for u, h in BEFORE[i]:
                    after_half(u, h)
                if i == 0:
                    split(2, 3)
                    split(3, 0)
                    values_out()
                    split(3, 1)
                if i == ITEMS - 2:
                    pool_scale(3)
                if i == ITEMS - 1:
                    pool_lo_part(0, slice(0, SEQ), u_t[:, :, META:UP])
                    pool_lo_part(1, slice(SEQ, TA), u_t[:, :, UP + STATE:UT])
                for u, h in AFTER[i]:
                    after_half(u, h)
                head_out_lo(i)
                if ITEMS - 5 <= i <= ITEMS - 3:
                    pool_scale(i - (ITEMS - 5))
                if i == ITEMS - 2:
                    pool_scale(4)

            for m in range(8):
                for h in range(2):
                    cols = slice(h * HA, (h + 1) * HA)
                    dve.wait_ge(half_done, N_BR + m + 1) if h == 0 else dve.wait_ge(unit_done, U_BR + m + 1)
                    dve.wait_ge(sig_done, 2 * m + 2)
                    if m:
                        dve.wait_ge(mix_lo_done, 2 * m + h - 1)
                    tt(br_a[:, h, :], lin[:, h, 0:HA], gates[:, 0, m, cols], ALU.mult)
                    tt(br_b[:, h, :], xo[:, h, 0:HA], gates[:, 1, m, cols], ALU.mult).then_inc(bank_free[h], 1)
                    dve.wait_ge(bank_free[h], N_BR + m + 1)
                    tt(br_a[:, h, :], br_a[:, h, :], br_b[:, h, :], ALU.add).then_inc(br_summed, 1)
                    if h == 0 and m:
                        split_next(U_BR // 4 + m // 4, m % 4)
                    dve.wait_ge(mix_hi_done, 2 * m + h + 1)
                    tt(mix_lo[:, m, cols], br_a[:, h, :], mix_hi[:, m, cols].bitcast(F32), ALU.subtract)\
                        .then_inc(mix_lo_done, 1)

            def add_residual(m):
                for part, done in ((h_hi, hi_added), (h_lo, ln1.s["res"])):
                    stt(out=ln1.r[:, m, :], in0=part[:, m, META:T].bitcast(F32), scalar=ALPHA,
                        in1=ln1.r[:, m, :], op0=ALU.mult, op1=ALU.add).then_inc(done, 1)
                    dve.wait_ge(done, m + 1)

            def prepare(m):
                n = 2 * (m - 6)
                h_cols = slice(META, T)
                nc.vector.tensor_scalar(ln1.r[:, m, :], h_hi[:, m, h_cols].bitcast(F32), ALPHA, None, ALU.mult)\
                    .then_inc(prepared, 1)
                dve.wait_ge(prepared, n + 1)
                stt(out=ln1.r[:, m, :], in0=h_lo[:, m, h_cols].bitcast(F32), scalar=ALPHA, in1=ln1.r[:, m, :],
                    op0=ALU.mult, op1=ALU.add).then_inc(prepared, 1)

            for m in range(6):
                split_next(U_OUT // 4 + m // 4, m % 4)
                dve.wait_ge(bank_free[0], N_OUT + m + 1)
                dve.wait_ge(bank_free[1], N_OUT + m + 1)
                if m == 5:
                    split(U_OUT // 4 + 1, 3)
                add_residual(m)
                if m == 2:
                    norm_shift(ln1, 0)
                    norm_shift(ln1, 1)
                    dve.wait_ge(ln1.s["shift"], 2)
                for k in SHIFT_AFTER[m]:
                    shifted(ln1, k)
                if m < 2:
                    prepare(6 + m)
                if m in (3, 4):
                    dve.wait_ge(prepared, 4)
                    tt(ln1.r[:, m + 3, :], ln1.r[:, m + 3, :], ln1.shift[:, 0, :], ALU.subtract)\
                        .then_inc(prepared, 1)

            def out_half(m, h):
                if h == 0:
                    dve.wait_ge(half_done, N_OUT + m + 1)
                else:
                    dve.wait_ge(unit_done, U_OUT + m + 1)
                c = ln1.cols(h)
                stt(out=ln1.r[:, m, c], in0=lin[:, m - 6, 0:HA], scalar=vec(V_BOUT + m), in1=ln1.r[:, m, c],
                    op0=ALU.add, op1=ALU.add).then_inc(bank_free[m - 6], 1)

            dve.wait_ge(prepared, 6)
            out_half(6, 0)
            out_half(7, 0)
            variance(ln1, 0)
            inverse(ln1, 0)
            out_half(6, 1)

            def between_1(k):
                if k == 1:
                    out_half(7, 1)
                if k == 5:
                    variance(ln1, 1)
                if k == 6:
                    inverse(ln1, 1)

            scale_half(ln1, 0, between_1)
            scale_half(ln1, 1)

            def hidden_tile(e, h):
                i = 2 * h + e
                dve.wait_ge(bank_free[e], N_MLP1[0] + h + 1)
                tt(relu_sq[:, e, :], relu_t[:, e, :], relu_t[:, e, :], ALU.mult).then_inc(f_sq_done, 1)
                dve.wait_ge(f_sq_done, i + 1)
                dve.wait_ge(f_hi_done, i + 1)
                tt(f_lo[:, e, h * HA:(h + 1) * HA], relu_sq[:, e, :],
                   f_hi[:, e, h * HA:(h + 1) * HA].bitcast(F32), ALU.subtract).then_inc(f_lo_done, 1)

            hidden_tile(0, 0)
            hidden_tile(1, 0)
            split(U_MLP1[0] // 4, 2)
            hidden_tile(0, 1)
            hidden_tile(1, 1)

            def hidden(s, it):
                first = isinstance(it, int)
                for j in range(2 if first else 0, 4):
                    c = 4 * it + j
                    split_next(U_MLP1[s] // 4 + it, j)
                    for h in range(2):
                        dve.wait_ge(bank_free[h], N_MLP1[s] + c + 1)
                        tt(relu_sq[:, h, :], relu_t[:, h, :], relu_t[:, h, :], ALU.mult).then_inc(f_sq_done, 1)
                        dve.wait_ge(f_sq_done, 2 * (FH * s + c) + h + 1)
                        dve.wait_ge(f_hi_done, 2 * (FH * s + c) + h + 1)
                        cols = slice(h * HA, (h + 1) * HA)
                        tt(f_lo[:, bass.ds(c, 1), cols], relu_sq[:, h:h + 1, :],
                           f_hi[:, bass.ds(c, 1), cols].bitcast(F32), ALU.subtract).then_inc(f_lo_done, 1)

            for s in range(2):
                if s == 0:
                    hidden(0, 0)
                with dve.Fori(1 - s, FH // 4) as it:
                    hidden(s, it)
                if s == 0:
                    with dve.Fori(0, 4) as it:
                        for j in range(4):
                            m = 2 * it + j // 2
                            split_next(U_MLP2[0] // 4 + it, j)
                            if j % 2:
                                dve.wait_ge(bank_free[0], N_MLP2[0] + m + 1)
                                dve.wait_ge(bank_free[1], N_MLP2[0] + m + 1)
                                stt(out=ln2.r[:, bass.ds(m, 1), :], in0=h_hi[:, bass.ds(m, 1), META:T].bitcast(F32),
                                    scalar=ALPHA, in1=ln2.r[:, bass.ds(m, 1), :], op0=ALU.mult, op1=ALU.add)\
                                    .then_inc(ln2_added, 1)
                                dve.wait_ge(ln2_added, 2 * m + 1)
                                stt(out=ln2.r[:, bass.ds(m, 1), :], in0=h_lo[:, bass.ds(m, 1), META:T].bitcast(F32),
                                    scalar=ALPHA, in1=ln2.r[:, bass.ds(m, 1), :], op0=ALU.mult, op1=ALU.add)\
                                    .then_inc(ln2_added, 1)
                else:
                    dve.wait_ge(ln2_added, 2 * KC)
                    U4 = U_MLP2[1] // 4

                    def add_half(it, m, h):
                        if h == 0:
                            dve.wait_ge(half_done, N_MLP2[1] + m + 1)
                        else:
                            dve.wait_ge(unit_done, U_MLP2[1] + 2 * m + 2)
                        cols = slice(h * HA, (h + 1) * HA)
                        tt(ln2.r[:, bass.ds(m, 1), cols], lin[:, h:h + 1, 0:HA], ln2.r[:, bass.ds(m, 1), cols],
                           ALU.add).then_inc(bank_free[h], 1)

                    def shift_last(m):
                        dve.wait_ge(bank_free[1], N_MLP2[1] + m)
                        shifted(ln2, m - 1)

                    split_next(U4, 0)
                    split_next(U4, 1)
                    add_half(0, 0, 0)
                    add_half(0, 0, 1)
                    dve.wait_ge(bank_free[1], N_MLP2[1] + 1)
                    nc.vector.tensor_copy(ln2.var[:, 0, 0:1], ln2.r[:, 0, TA - 1:TA]).then_inc(ln2.s["res"], 1)
                    split_next(U4, 2)
                    split_next(U4, 3)
                    add_half(0, 1, 0)
                    add_half(0, 1, 1)
                    norm_shift(ln2, 0)
                    norm_shift(ln2, 1)
                    dve.wait_ge(ln2.s["shift"], 2)
                    shifted(ln2, 0)
                    with dve.Fori(1, 3) as it:
                        for e in range(2):
                            m = 2 * it + e
                            split_next(U4 + it, 2 * e)
                            shift_last(m)
                            split_next(U4 + it, 2 * e + 1)
                            add_half(it, m, 0)
                            add_half(it, m, 1)
                    split_next(U4 + 3, 0)
                    shift_last(6)
                    split_next(U4 + 3, 1)
                    add_half(3, 6, 0)
                    add_half(3, 6, 1)
                    split_next(U4 + 3, 2)
                    shift_last(7)
                    shifted(ln2, 7)
                    dve.wait_ge(ln2.s["d"], 8)
                    add_half(3, 7, 0)
                    variance(ln2, 0)
                    inverse(ln2, 0)

                    def between_2(k):
                        if k == 3:
                            add_half(3, 7, 1)
                        if k == 6:
                            variance(ln2, 1)

                    scale_half(ln2, 0, between_2)
                    inverse(ln2, 1)
                    scale_half(ln2, 1)

        @block.gpsimd
        def _(pool):
            nc.gpsimd.memset(inv_d[:, :], 1.0 / D_MODEL).then_inc(made, 1)

            def centre(ln, h, first=0, stop=KC):
                pool.wait_ge(*ln.count("mean", h, 1))
                c = ln.cols(h)
                for k in range(max(first, ln.by_dve[h]), stop):
                    nc.gpsimd.tensor_tensor(ln.r[:, k, c], ln.r[:, k, c], ln.mean[:, 0, c], ALU.subtract)\
                        .then_inc(ln.s["centred_g"], 1)

            def lo_part(u):
                pool.wait_ge(hi_split, u + 1)
                nc.gpsimd.tensor_tensor(wlo[:, u % SPLIT, :], raw[:, u % RAW, :],
                                        whi[:, u % SPLIT, :].bitcast(F32), ALU.subtract).then_inc(lo_split, 1)

            pool.wait_ge(shift1_done, 1)
            for k in range(KC):
                pool.wait_ge(x_in[1][k // 2], 16)
                c = ln_in.cols(1)
                nc.gpsimd.tensor_tensor(ln_in.r[:, k, c], ln_in.r[:, k, c], ln_in.shift[:, 0, c], ALU.subtract)\
                    .then_inc(ln_in.half_d[1], 1)
            centre(ln_in, 0)
            pool.wait_ge(lo_split, 1)
            lo_part(1)
            centre(ln_in, 1)
            nc.gpsimd.memset(tri[:, :], -1.0).then_inc(made, 1)
            nc.gpsimd.memset(below[:, :], -1.0).then_inc(made, 1)
            nc.gpsimd.memset(ident[:, :], 0.0).then_inc(made, 1)
            pool.wait_ge(made, 4)
            nc.gpsimd.affine_select(out=tri[:, :], in_=tri[:, :], compare_op=ALU.is_ge, fill=0.0, base=0,
                                    pattern=[[-1, P]], channel_multiplier=1).then_inc(made, 1)
            nc.gpsimd.affine_select(out=below[:, :], in_=below[:, :], compare_op=ALU.is_ge, fill=0.0, base=-1,
                                    pattern=[[1, P]], channel_multiplier=-1).then_inc(made, 1)
            nc.gpsimd.affine_select(out=ident[:, :], in_=ident[:, :], compare_op=ALU.not_equal, fill=1.0, base=0,
                                    pattern=[[-1, P]], channel_multiplier=1).then_inc(made, 1)
            nc.gpsimd.memset(mask_diag[:, :], 0.0)
            nc.gpsimd.memset(mask_tail[:, :], 0.0)
            nc.gpsimd.memset(mask_new[:, :, :], 0.0).then_inc(win_done, 1)
            pool.wait_ge(win_done, 1)
            nc.gpsimd.affine_select(out=mask_diag[:, :], in_=mask_diag[:, :], compare_op=ALU.is_ge, fill=NEG,
                                    base=-1, pattern=[[1, P]], channel_multiplier=-1).then_inc(made, 1)
            lead = UP - META - TAIL
            nc.gpsimd.affine_select(out=mask_tail[:, :], in_=mask_tail[:, :], compare_op=ALU.is_ge, fill=NEG,
                                    base=-lead, pattern=[[0, META]], channel_multiplier=1)
            nc.gpsimd.affine_select(out=mask_new[:, :, :], in_=mask_new[:, :, :], compare_op=ALU.is_ge, fill=NEG,
                                    base=-(P - DEC), pattern=[[0, HEADS], [0, DEC]], channel_multiplier=1)\
                .then_inc(win_done, 1)
            pool.wait_ge(win_done, 2)
            nc.gpsimd.affine_select(out=mask_tail[:, :], in_=mask_tail[:, :], compare_op=ALU.is_ge, fill=NEG,
                                    base=lead - 1, pattern=[[1, META]], channel_multiplier=-1).then_inc(made, 1)
            nc.gpsimd.affine_select(out=mask_new[:, :, :], in_=mask_new[:, :, :], compare_op=ALU.is_ge, fill=NEG,
                                    base=P - DEC - 1, pattern=[[0, HEADS], [1, DEC]], channel_multiplier=-1)\
                .then_inc(made, 1)
            nc.gpsimd.memset(q_t[:, :, :], 0.0).then_inc(q_zero, 1)

            pool.wait_ge(*ln_in.count("scaled", 1, KC))
            pool.dma_start(u_t[:, :, UP:UP + STATE], state_d).then_inc(state_in, 16)
            for h in range(2):
                pool.wait_ge(bank_free[h], N_K + 4)
            pool.dma_start(k_out, k_t[:, :, :]).then_inc(k_stored, 16)
            pool.wait_ge(v_ready, 5)
            pool.dma_start(v_out[0:4 * P, :].rearrange("(t p) d -> p t d", p=P), v_t[:, 0:4, :])\
                .then_inc(v_stored, 16)
            pool.dma_start(v_out[4 * P:T, :], v_t[4 * P - TAIL:P, 4, :]).then_inc(v_stored, 16)

            pool.wait_ge(state_in, 16)
            for h in range(2):
                pool.wait_ge(bank_free[h], N_U + 4)
            nc.gpsimd.tensor_copy(ust[:, :, 0:STATE], u_t[:, :, UP - STATE:UP])
            nc.gpsimd.tensor_copy(ust[:, :, STATE:2 * STATE], u_t[:, :, UT - STATE:UT]).then_inc(ust_done, 1)
            done = 2
            for g, w in enumerate(POOL_WINDOWS):
                src, reach = u_t[:, g, :], 1
                while reach < w:
                    dst = win[:, (reach.bit_length() - 1) % 2, 0:UT]
                    nc.gpsimd.tensor_tensor(dst[:, 2 * reach - 1:UT], src[:, 2 * reach - 1:UT],
                                            src[:, reach - 1:UT - reach], ALU.add).then_inc(win_done, 1)
                    done += 1
                    pool.wait_ge(win_done, done)
                    src, reach = dst, 2 * reach
                nc.gpsimd.tensor_scalar(src[:, META:UT], src[:, META:UT], 1.0 / w, 0.0, ALU.mult, ALU.add)\
                    .then_inc(win_done, 1)
                done += 1
                pool.wait_ge(win_done, done)
                if g == 0:
                    pool.wait_ge(ust_done, 1)
                last = nc.gpsimd.tensor_tensor(u_t[:, g, META:UT], src[:, META:UT], u_t[:, g, META:UT],
                                               ALU.subtract)
                if g < 3:
                    last.then_inc(win_done, 1)
                    done += 1
                    pool.wait_ge(win_done, done)
            last.then_inc(pooled, 1)
            pool.dma_start(s_out, ust[:, :, :]).then_inc(s_stored, 16)

            def add_chunk(ln, k, par):
                pool.wait_ge(ln.s["d"], k + 1)
                first = isinstance(k, int) and k == 1
                if not first:
                    pool.wait_ge(ln.s["sum"], k - 1)
                nc.gpsimd.tensor_tensor(ln.sum[:, 0:1, :], ln.r[:, 0:1, :] if first else ln.sum[:, 0:1, :],
                                        ln.r[:, bass.ds(k, 1), :], ALU.add).then_inc(ln.s["sum"], 1)
                pool.wait_ge(ln.s["sq"], k + 1)
                if not first:
                    pool.wait_ge(ln.s["sumsq"], k - 1)
                nc.gpsimd.tensor_tensor(ln.sumsq[:, 0, :], ln.sq[:, 0, :] if first else ln.sumsq[:, 0, :],
                                        ln.sq[:, par, :], ALU.add).then_inc(ln.s["sumsq"], 1)

            for k in range(1, ln1.direct):
                add_chunk(ln1, k, k % 2)
            centre(ln1, 0, 0, 3)
            lo_part(U_MLP1[0])
            centre(ln1, 0, 3, 6)
            lo_part(U_MLP1[0] + 1)
            centre(ln1, 0, 6)
            centre(ln1, 1)
            for k in range(1, ln2.direct):
                add_chunk(ln2, k, k % 2)
            centre(ln2, 0)
            centre(ln2, 1)


def kernel(**inputs):
    import numpy as np
    import concourse.bacc as bacc
    from concourse.bass_utils import run_bass_kernel_spmd as run

    def units(w):
        n = w.shape[1] // P
        return w.reshape(w.shape[0] // P, P, n, P).transpose(2, 1, 0, 3).reshape(n, P, -1)

    a = {n: np.asarray(v) for n, v in inputs.items()}
    w_in = a["w_in"][0]
    w_u, w_q, w_k, w_v = (w_in[:, i * 512:(i + 1) * 512] for i in range(4))
    w2 = a["w_mlp2"][0].reshape(2, 2, KC, P, KC, P).transpose(0, 4, 1, 3, 2, 5).reshape(2, 2 * KC, P, UNIT)
    w1 = units(a["w_mlp1"][0])
    stream = np.concatenate([
        units(w_k), units(w_q), w_v.reshape(4, 2, P, ATTN_W).transpose(0, 2, 1, 3).reshape(4, P, UNIT), units(w_u),
        units(w_in[:, 2048:]),
        np.concatenate([units(a["w_br_pool"][0]), units(a["w_br_attn"][0])], axis=2),
        units(a["w_out"][0]), w1[:FH], w2[0], w1[FH:], w2[1]])
    cols = [a["b_in"][0], a["pool_scale"][0], a["b_out"][0], a["ln_in_g"], a["ln_in_b"], a["ln1_g"][0],
            a["ln1_b"][0], a["ln2_g"][0], a["ln2_b"][0], a["b_mlp1"][0], a["b_mlp2"][0]]
    arrays = {
        "x_t": np.concatenate([a["meta"], a["x_prompt"][0], a["x_sample"][0]]).T.reshape(KC, P, T).transpose(1, 0, 2),
        "w_stream": stream,
        "vecs": np.concatenate([c.reshape(-1, P) for c in cols]).T,
        "b_v": np.broadcast_to(a["b_in"][0][1536:2048], (P, ATTN_W)),
        "k_cache": a["cache_k"].reshape(PAST, PAIRS, P).transpose(2, 1, 0),
        "v_cache": a["cache_v"].reshape(PAST // P, P, ATTN_W).transpose(1, 0, 2),
        "pool_state": a["state_pool"].reshape(STATE, 4, P).transpose(2, 1, 0),
        "w_pool": a["w_pool_grp"][0].transpose(1, 0, 2),
    }
    arrays = {n: np.ascontiguousarray(v) for n, v in arrays.items()}
    nc = bacc.Bacc("TRN2", target_bir_lowering=False, num_devices=1)
    args = [nc.dram_tensor(n, v.shape, F32, kind="ExternalInput").ap() for n, v in arrays.items()]
    outs = {"y": (P, KC, TA), "k_new": (P, PAIRS, T), "v_new": (T, ATTN_W), "state_new": (P, 4, 2 * STATE)}
    args += [nc.dram_tensor(n, s, F32, kind="ExternalOutput").ap() for n, s in outs.items()]
    encoder_step(nc, *args)
    got = run(nc, [arrays], core_ids=[0]).results[0]
    y = got["y"].transpose(2, 1, 0).reshape(TA, D_MODEL)
    k = got["k_new"].transpose(2, 1, 0).reshape(T, HEADS, HD)
    v = got["v_new"].reshape(T, HEADS, HD)
    s = got["state_new"].transpose(2, 1, 0).reshape(2, STATE, POOL_W)
    return (y[None, :SEQ], y[None, SEQ:], k[None, None, :UP], v[None, None, :UP], s[None, None, 0],
            k[None, None, UP:], v[None, None, UP:], s[None, None, 1])
```
